# Optimizing a Trainium2 kernel written in Bass

```python
import jax, jax.numpy as jnp
from jax import lax
import numpy as np

D_MODEL = 1024
BATCH = 1
SEQ = 128
DEPTH = 2
DEC_BATCH = 1
DEC_SEQ = 1024
PAST_LEN = 128

GRID_W = 64
MIXER_ORDER = ('rglru', 'pool')
N_MIXERS = len(MIXER_ORDER)
D_RNN = D_MODEL
N_LRU_BLOCKS = 4
LRU_BLOCK = D_RNN // N_LRU_BLOCKS
CONV_W = 4
CONV_LEFT = 2
LRU_C = 8.0
POOL_WINDOWS = (2, 4, 8, 16)
N_POOL_GROUPS = len(POOL_WINDOWS)
POOL_GROUP = D_MODEL // N_POOL_GROUPS
D_FF = -(-8 * D_MODEL // (3 * 256)) * 256
N_MOD = 6
EPS = 1e-6
POS_THETA = 10000.0

kernel_name = 'hybrid_rglru_pool_diffusion_step'

def rms_norm(x, g):
    x32 = x.astype(jnp.float32)
    y = x32 * lax.rsqrt(jnp.mean(x32 * x32, axis=-1, keepdims=True) + EPS)
    return (y * g.astype(jnp.float32)).astype(x.dtype)

def modulation(cond, w, b):
    m = jax.nn.silu(cond) @ w + b
    return jnp.split(m[:, None, :], N_MOD, axis=-1)

def grid_pos_emb(t_len, dtype):
    rows = t_len // GRID_W
    r = jnp.repeat(jnp.arange(rows), GRID_W)
    col = jnp.tile(jnp.arange(GRID_W), rows)
    quarter = D_MODEL // 4
    omega = 1.0 / (POS_THETA ** (jnp.arange(quarter, dtype=jnp.float32) / quarter))

    def emb(p):
        ang = p.astype(jnp.float32)[:, None] * omega[None, :]
        return jnp.concatenate([jnp.sin(ang), jnp.cos(ang)], axis=-1)

    return jnp.concatenate([emb(r), emb(col)], axis=-1).astype(dtype)

def centred_depthwise_conv(u, w, b):
    t_len = u.shape[1]
    up = jnp.pad(u, ((0, 0), (CONV_LEFT, CONV_W - 1 - CONV_LEFT), (0, 0)))
    y = up[:, 0:t_len] * w[0]
    for k in range(1, CONV_W):
        y = y + up[:, k:k + t_len] * w[k]
    return y + b

def _lin_combine(left, right):
    a1, b1 = left
    a2, b2 = right
    return a1 * a2, a2 * b1 + b2

def rglru_direction(u, wa, ba, wx, bx, lam, h0, reverse):
    bsz, t_len, _ = u.shape
    u32 = u.astype(jnp.float32)
    ub = u32.reshape(bsz, t_len, N_LRU_BLOCKS, LRU_BLOCK)
    ra = jnp.einsum('btnd,nde->btne', ub, wa.astype(jnp.float32)).reshape(bsz, t_len, D_RNN)
    ix = jnp.einsum('btnd,nde->btne', ub, wx.astype(jnp.float32)).reshape(bsz, t_len, D_RNN)
    r = jax.nn.sigmoid(ra + ba.astype(jnp.float32))
    i = jax.nn.sigmoid(ix + bx.astype(jnp.float32))
    log_a = -LRU_C * r * jax.nn.softplus(-lam.astype(jnp.float32))
    a = jnp.exp(log_a)
    b = jnp.sqrt(-jnp.expm1(2.0 * log_a)) * (i * u32)
    a_cum, b_cum = lax.associative_scan(_lin_combine, (a, b), reverse=reverse, axis=1)
    h = a_cum * h0.astype(jnp.float32)[:, None, :] + b_cum
    h_last = h[:, 0] if reverse else h[:, -1]
    return h, h_last

def rglru_mixer(h, h0, w_in, conv_w, conv_b, wa, ba, wx, bx, lam, w_out):
    z = h @ w_in
    gate_br, rec = jnp.split(z, 2, axis=-1)
    u = centred_depthwise_conv(rec, conv_w, conv_b)
    hf, sf = rglru_direction(u, wa[0], ba[0], wx[0], bx[0], lam[0], h0[:, 0], False)
    hb, sb = rglru_direction(u, wa[1], ba[1], wx[1], bx[1], lam[1], h0[:, 1], True)
    mixed = (hf + hb) * jax.nn.gelu(gate_br.astype(jnp.float32))
    y = mixed.astype(h.dtype) @ w_out
    return y, jnp.stack([sf, sb], axis=1).astype(h.dtype)

def centred_window_mean(u32, win):
    t_len = u32.shape[1]
    cs = jnp.pad(jnp.cumsum(u32, axis=1), ((0, 0), (1, 0), (0, 0)))
    t = jnp.arange(t_len)
    lo = jnp.clip(t - win // 2, 0, t_len)
    hi = jnp.clip(t + win // 2, 0, t_len)
    cnt = (hi - lo).astype(jnp.float32)
    return (cs[:, hi] - cs[:, lo]) / cnt[None, :, None]

def pool_mixer(h, pool_w, pool_b, pool_scale):
    bsz, t_len, _ = h.shape
    groups = h.astype(jnp.float32).reshape(bsz, t_len, N_POOL_GROUPS, POOL_GROUP)
    pooled = jnp.stack(
        [centred_window_mean(groups[:, :, gi], win) - groups[:, :, gi]
         for gi, win in enumerate(POOL_WINDOWS)], axis=2)
    y = jnp.einsum('btgc,gcd->btgd', pooled, pool_w.astype(jnp.float32)).reshape(bsz, t_len, D_MODEL)
    y = (y + pool_b.astype(jnp.float32)) * pool_scale.astype(jnp.float32)
    return y.astype(h.dtype)

def swiglu(h, w_in, w_out):
    gate, up = jnp.split(h @ w_in, 2, axis=-1)
    return (jax.nn.silu(gate) * up) @ w_out

def layer_forward(x, cond, p, h0):
    sh1, sc1, g1, sh2, sc2, g2 = modulation(cond, p['mod_w'], p['mod_b'])
    h = rms_norm(x, p['mix_pre_g']) * (1.0 + sc1) + sh1
    state = None
    if p['kind'] == 'rglru':
        y, state = rglru_mixer(h, h0, p['w_in'], p['conv_w'], p['conv_b'], p['gate_a_w'], p['gate_a_b'],
                               p['gate_x_w'], p['gate_x_b'], p['lam'], p['w_out'])
    else:
        y = pool_mixer(h, p['pool_w'], p['pool_b'], p['pool_scale'])
    x = x + g1 * rms_norm(y, p['mix_post_g'])
    h = rms_norm(x, p['ffn_pre_g']) * (1.0 + sc2) + sh2
    x = x + g2 * rms_norm(swiglu(h, p['ffn_w_in'], p['ffn_w_out']), p['ffn_post_g'])
    return x, state

def setup_inputs(seed: int = 0) -> dict:
    key = jax.random.key(seed)
    ks = iter(jax.random.split(key, 48))
    d = D_MODEL

    def nrm(shape, scale):
        return jax.random.normal(next(ks), shape, jnp.float32) * scale

    def gain(shape):
        return 1.0 + nrm(shape, 0.05)

    def lru_lambda():
        u = jax.random.uniform(next(ks), (2, D_RNN), jnp.float32, 0.9, 0.999)
        a0 = u ** (1.0 / LRU_C)
        return jnp.log(a0) - jnp.log1p(-a0)

    inp = {}
    inp['x_prompt'] = nrm((BATCH, SEQ, d), 1.0)
    inp['x_sample'] = nrm((DEC_BATCH, DEC_SEQ, d), 1.0)
    inp['state_l0_rglru'] = nrm((DEC_BATCH, 2, D_RNN), 0.5)
    inp['c'] = nrm((DEC_BATCH, d), 1.0)
    inp['c_ctx'] = nrm((d,), 1.0)
    inp['l0_mod_w'] = nrm((d, N_MOD * d), 0.5 * d ** -0.5)
    inp['l0_mod_b'] = nrm((N_MOD * d,), 0.01)
    inp['l0_mix_pre_g'] = gain((d,))
    inp['l0_mix_post_g'] = gain((d,))
    inp['l0_w_in'] = nrm((d, 2 * D_RNN), d ** -0.5)
    inp['l0_conv_w'] = nrm((CONV_W, D_RNN), CONV_W ** -0.5)
    inp['l0_conv_b'] = nrm((D_RNN,), 0.01)
    inp['l0_gate_a_w'] = nrm((2, N_LRU_BLOCKS, LRU_BLOCK, LRU_BLOCK), LRU_BLOCK ** -0.5)
    inp['l0_gate_a_b'] = nrm((2, D_RNN), 0.01)
    inp['l0_gate_x_w'] = nrm((2, N_LRU_BLOCKS, LRU_BLOCK, LRU_BLOCK), LRU_BLOCK ** -0.5)
    inp['l0_gate_x_b'] = nrm((2, D_RNN), 0.01)
    inp['l0_lambda'] = lru_lambda()
    inp['l0_w_out'] = nrm((D_RNN, d), D_RNN ** -0.5)
    inp['l0_ffn_pre_g'] = gain((d,))
    inp['l0_ffn_post_g'] = gain((d,))
    inp['l0_ffn_w_in'] = nrm((d, 2 * D_FF), d ** -0.5)
    inp['l0_ffn_w_out'] = nrm((D_FF, d), D_FF ** -0.5)
    inp['l1_mod_w'] = nrm((d, N_MOD * d), 0.5 * d ** -0.5)
    inp['l1_mod_b'] = nrm((N_MOD * d,), 0.01)
    inp['l1_mix_pre_g'] = gain((d,))
    inp['l1_mix_post_g'] = gain((d,))
    inp['l1_pool_w'] = nrm((N_POOL_GROUPS, POOL_GROUP, POOL_GROUP), POOL_GROUP ** -0.5)
    inp['l1_pool_b'] = nrm((d,), 0.01)
    inp['l1_pool_scale'] = gain((d,))
    inp['l1_ffn_pre_g'] = gain((d,))
    inp['l1_ffn_post_g'] = gain((d,))
    inp['l1_ffn_w_in'] = nrm((d, 2 * D_FF), d ** -0.5)
    inp['l1_ffn_w_out'] = nrm((D_FF, d), D_FF ** -0.5)
    return inp

def reference(x_prompt, x_sample, state_l0_rglru, c, c_ctx,
              l0_mod_w, l0_mod_b, l0_mix_pre_g, l0_mix_post_g, l0_w_in, l0_conv_w, l0_conv_b,
              l0_gate_a_w, l0_gate_a_b, l0_gate_x_w, l0_gate_x_b, l0_lambda, l0_w_out,
              l0_ffn_pre_g, l0_ffn_post_g, l0_ffn_w_in, l0_ffn_w_out,
              l1_mod_w, l1_mod_b, l1_mix_pre_g, l1_mix_post_g, l1_pool_w, l1_pool_b, l1_pool_scale,
              l1_ffn_pre_g, l1_ffn_post_g, l1_ffn_w_in, l1_ffn_w_out):
    layers = [
        dict(kind=MIXER_ORDER[0 % N_MIXERS], mod_w=l0_mod_w, mod_b=l0_mod_b,
             mix_pre_g=l0_mix_pre_g, mix_post_g=l0_mix_post_g, w_in=l0_w_in,
             conv_w=l0_conv_w, conv_b=l0_conv_b, gate_a_w=l0_gate_a_w, gate_a_b=l0_gate_a_b,
             gate_x_w=l0_gate_x_w, gate_x_b=l0_gate_x_b, lam=l0_lambda, w_out=l0_w_out,
             ffn_pre_g=l0_ffn_pre_g, ffn_post_g=l0_ffn_post_g,
             ffn_w_in=l0_ffn_w_in, ffn_w_out=l0_ffn_w_out),
        dict(kind=MIXER_ORDER[1 % N_MIXERS], mod_w=l1_mod_w, mod_b=l1_mod_b,
             mix_pre_g=l1_mix_pre_g, mix_post_g=l1_mix_post_g, pool_w=l1_pool_w,
             pool_b=l1_pool_b, pool_scale=l1_pool_scale,
             ffn_pre_g=l1_ffn_pre_g, ffn_post_g=l1_ffn_post_g,
             ffn_w_in=l1_ffn_w_in, ffn_w_out=l1_ffn_w_out),
    ]
    cached_states = {0: state_l0_rglru}

    y_prompt = x_prompt
    ctx_cond = c_ctx[None, :]
    new_states = {}
    for i in range(DEPTH):
        p = layers[i]
        h0 = jnp.zeros((y_prompt.shape[0], 2, D_RNN), y_prompt.dtype) if p['kind'] == 'rglru' else None
        y_prompt, st = layer_forward(y_prompt, ctx_cond, p, h0)
        if st is not None:
            new_states[i] = st

    y_sample = x_sample + grid_pos_emb(x_sample.shape[1], x_sample.dtype)[None]
    for i in range(DEPTH):
        p = layers[i]
        h0 = cached_states[i] if p['kind'] == 'rglru' else None
        y_sample, _ = layer_forward(y_sample, c, p, h0)

    return (y_prompt, y_sample, new_states[0])


_drawn_inputs = setup_inputs


def setup_inputs(seed=0):
    import zlib

    import numpy as np

    out = dict(_drawn_inputs(seed))
    spreads = {}
    factors = {'state_l0_rglru': 8.0,
     'l0_mix_post_g': 4.17,
     'l0_gate_a_b': 36.849,
     'l0_gate_x_b': 8.0,
     'l0_ffn_pre_g': 3.031,
     'l0_ffn_post_g': 3.997,
     'l1_mod_b': 4.097,
     'l1_mix_pre_g': 4.377,
     'l1_mix_post_g': 4.257,
     'l1_pool_b': 35.158,
     'l1_pool_scale': 3.825,
     'l1_ffn_pre_g': 3.297,
     'l1_ffn_post_g': 4.248}
    for name, (base, spread) in spreads.items():
        noise = np.random.default_rng([zlib.crc32(name.encode()), seed]).standard_normal(out[name].shape)
        drawn = base * np.exp(spread * noise) if base else spread * noise
        out[name] = __import__('jax').numpy.asarray(drawn.astype(out[name].dtype))
    for name, factor in factors.items():
        out[name] = (out[name] * factor).astype(out[name].dtype)
    return out
```

```python
from contextlib import ExitStack

import numpy as np

import concourse.bass as bass
from concourse import mybir

F32 = mybir.dt.float32
F32R = mybir.dt.float32r
ALU = mybir.AluOpType
ACT = mybir.ActivationFunctionType

P = 128
D = 1024
KT = D // P
CTX = 128
LAT = 1024
T = CTX + LAT
NG = 3
GT = T // NG
DFF = 2816
HB = 2
NB = DFF // (HB * P)
NLB = 4
GRID_W = 64
GRID_H = LAT // GRID_W
WINDOWS = (2, 4, 8, 16)
EPS = 1e-6
GC = 2048
PAD = 8
PL = 3 * PAD + T
CP, LP = 2, CTX + 5
RL = T + 8
CTX_C, LAT_C = 1, 0

V_C, V_CCTX, V_CONVW, V_CONVB, V_BA, V_BX, V_LAM, V_STATE, V_POOLB = 0, 8, 16, 48, 56, 72, 88, 104, 120
V_GAIN, V_PSCALE = 128, 192
V_MODB = 200
NV = 296
G_MIXPRE, G_MIXPOST, G_FFNPRE, G_FFNPOST = 0, 8, 16, 24

C_ID, C_EDGE = 0, P
EDGES = [(w, w // 2, w // 2 - 1) for w in WINDOWS]
NC = C_EDGE + sum(a + b for _, a, b in EDGES)
NPOS = 4 * GRID_H + 4 * GRID_W


def stream_order():
    order = [("mod", 0, m) for m in range(8)]
    m = 8
    for kind, n in MIX_PHASES:
        order.append((kind, n))
        if kind != "gates":
            order += [("mod", 0, m), ("mod", 0, m + 1)]
            m += 2
    order += [("w_out", n) for n in range(4)]
    order += [("mod", 1, 0), ("mod", 1, 1)]
    m = 2
    for b in range(NB):
        order += [("gate", 0, b), ("up", 0, b), ("down", 0, b), ("mod", 1, m), ("mod", 1, m + 1)]
        m += 2
    order.append(("pool",))
    for b in range(NB):
        order += [("gate", 1, b), ("up", 1, b), ("down", 1, b)]
    return order


MIX_PHASES = [("rec", 0), ("rec", 1), ("gates", 0), ("rec", 2), ("gates", 1), ("rec", 3), ("gates", 2),
              ("branch", 0), ("gates", 3), ("branch", 1), ("branch", 2), ("branch", 3)]
STREAM = stream_order()
Q = {item: q for q, item in enumerate(STREAM)}
WEIGHT = {item: w for w, item in enumerate(i for i in STREAM if i[0] != "mod")}
MOD = {item: m for m, item in enumerate(i for i in STREAM if i[0] == "mod")}
LOOPS = (NB - 3) // 2


def landed_values():
    count, out = [0, 0], []
    for q, item in enumerate(STREAM):
        count[q % 2] += 64 if item[0] == "gates" else 16
        out.append(count[q % 2])
    return out


LANDED = landed_values()

P_START = {}
_n = 0
for _item in MIX_PHASES:
    P_START[_item] = _n
    _n += 24 if _item[0] == "gates" else 6
P_TOTAL = _n
O_XIN = 0
O_WOUT = O_XIN + 2 * T // P
O_FFN = [O_WOUT + 24, 0]
O_POOL = O_FFN[0] + 24 * NB
O_FFN[1] = O_POOL + 24
O_LAST = [start + 24 * (NB - 1) for start in O_FFN]
PAIRS = [0, 6 * NB]


def out_bank_of(n):
    if n >= O_LAST[1]:
        return n % 4
    beside = any(start <= n < last for start, last in zip(O_FFN, O_LAST))
    return 4 + n % 2 if beside else n % 6


def phase_start(n):
    return max(start for start in (O_XIN, O_WOUT, O_FFN[0], O_LAST[0], O_POOL, O_FFN[1], O_LAST[1]) if start <= n)


def bank_free(n):
    last = next((v for v in range(n - 1, phase_start(n) - 1, -1) if out_bank_of(v) == out_bank_of(n)), -1)
    return max(last + 1, phase_start(n))


def program(nc, a, scratch_x, scratch_h, consts, outs):
    ctx = ExitStack()
    at = [(nc.sbuf_base + 31) // 32 * 32]

    def place(name, shape, dt, offset):
        return nc.alloc_sbuf_tensor_at(name, shape, dt, offset=offset)

    def region(nbytes):
        here = at[0]
        at[0] += (nbytes + 31) // 32 * 32
        return here

    r_raw = region(2 * GC * 4)
    raw = place("raw", [P, 2, GC], F32, r_raw)
    w_hi = place("w_hi", [P, 3, GC], F32R, region(3 * GC * 4))
    w_lo = place("w_lo", [P, 3, GC], F32R, region(3 * GC * 4))
    r_hi = region(KT * T * 4)
    r_lo = region(KT * T * 4)
    mv_hi = place("mv_hi", [P, KT, T], F32R, r_hi)
    mv_lo = place("mv_lo", [P, KT, T], F32R, r_lo)
    x_old = place("x_old", [P, KT, T], F32, r_hi)
    wide = place("wide", [P, KT, T], F32, r_lo)
    stage = place("stage", [P, 3, P], F32, r_hi)
    r_y = region(6 * T * 4 + 2 * RL * 4)
    y = place("y", [P, KT, T], F32, r_y)
    mixed = place("mixed", [P, KT, T], F32, r_y)
    u_hi = place("u_hi", [P, 2, T], F32R, r_y)
    u_lo = place("u_lo", [P, 2, T], F32R, r_y + 2 * T * 4)
    u = place("u", [P, 2, T], F32, r_y + 4 * T * 4)
    rec = place("rec", [P, 2, RL], F32, r_y + 6 * T * 4)
    r_z = region(7 * T * 4)
    lru_a = place("lru_a", [P, 2, T], F32, r_z)
    lru_i = place("lru_i", [P, 2, T], F32, r_z + 2 * T * 4)
    lru_m = place("lru_m", [P, 2, T], F32, r_z + 4 * T * 4)
    lru_f = place("lru_f", [P, T], F32, r_z + 6 * T * 4)
    h_sum = place("h_sum", [P, 6, T], F32, r_z)
    hid_hi = place("hid_hi", [P, HB, T], F32R, r_z)
    hid_lo = place("hid_lo", [P, HB, T], F32R, r_z + HB * T * 4)
    hid = place("hid", [P, 2, GT], F32, r_z + 2 * HB * T * 4)
    x_stage = place("x_stage", [P, 4, D], F32, r_z)
    y_stage = place("y_stage", [P, 4, D], F32, r_raw)
    pool_d = place("pool_d", [P, 3, PL], F32, r_z)
    pool_g = place("pool_g", [P, 3, PL], F32, r_z + 3 * PL * 4)
    pos = place("pos", [P, NPOS], F32, r_z + 4 * D * 4)
    states_t = place("states_t", [16, P], F32, r_z + 6 * T * 4)
    acc = place("acc", [P, GT], F32, r_z + 7 * T * 4 - 2 * GT * 4)
    diag = place("diag", [P, GT], F32, r_z + 7 * T * 4 - GT * 4)
    const = place("const", [P, NC], F32, region(NC * 4))
    ones = place("ones", [P, P], F32, region(P * 4))
    vec = place("vec", [P, NV], F32, region(NV * 4))
    cond = place("cond", [P, KT, 2], F32, region(KT * 2 * 4))
    modv = place("modv", [P, 2, 48, 2], F32, region(2 * 96 * 4))
    coef = place("coef", [P, 2, 4, KT, 2], F32, region(2 * 4 * KT * 2 * 4))
    lam = place("lam", [P, 6, 16], F32, region(6 * 16 * 4))
    var = place("var", [P, GT // P], F32, region(GT // P * 4))
    states = place("states", [P, 16], F32, region(16 * 4))
    assert at[0] <= nc.sbuf_usable_end, at[0] - nc.sbuf_usable_end

    ident = const[:, C_ID:C_ID + P]
    neg_rate, half_rate = lam[:, 4, :], lam[:, 5, :]

    with ctx:
        bank = [ctx.enter_context(nc.psum_tensor(f"bank{i}", [P, 512], F32)) for i in range(8)]
        NORM_BANK, MOD_BANK, T_BANKS = 6, 7, (4, 5, 7)

        def sem(name):
            return ctx.enter_context(nc.semaphore(name))

        raw_landed = [sem("raw_landed0"), sem("raw_landed1")]
        stage_landed = sem("stage_landed")
        const_landed = sem("const_landed")
        pos_landed = sem("pos_landed")
        pads_ready = sem("pads_ready")
        x_landed = [sem(f"x_landed{t}") for t in range(T // P)]
        rows_turned = sem("rows_turned")
        vec_ready = sem("vec_ready")
        cond_ready = sem("cond_ready")
        ones_ready = sem("ones_ready")
        w_hi_ready = sem("w_hi_ready")
        w_ready = sem("w_ready")
        mod_used = sem("mod_used")
        lam_exp = sem("lam_exp")
        lam_abs = sem("lam_abs")
        rate_ready = sem("rate_ready")
        p_ready = sem("p_ready")
        p_freed = sem("p_freed")
        out_ready = sem("out_ready")
        out_taken = sem("out_taken")
        squares = sem("squares")
        acc_ready = sem("acc_ready")
        sum_ready = sem("sum_ready")
        var_ready = sem("var_ready")
        diag_ready = sem("diag_ready")
        spread_ready = sem("spread_ready")
        rstd_used = sem("rstd_used")
        t_ready, t_freed = sem("t_ready"), sem("t_freed")
        rstd_ready = sem("rstd_ready")
        x_new = sem("x_new")
        affine_ready = sem("affine_ready")
        mv_hi_done = sem("mv_hi_done")
        mv_ready = sem("mv_ready")
        x_stored = [sem(f"x_stored{g}") for g in range(NG)]
        x_loaded = [sem(f"x_loaded{g}") for g in range(NG)]
        conv_done = sem("conv_done")
        u_hi_done = sem("u_hi_done")
        u_ready = sem("u_ready")
        gates_ready = sem("gates_ready")
        scanned = sem("scanned")
        h_ready = sem("h_ready")
        h_stored = sem("h_stored")
        h_loaded = [sem(f"h_loaded{n}") for n in range(4)]
        mixed_ready = sem("mixed_ready")
        gate_ready = sem("gate_ready")
        pair_ready = sem("pair_ready")
        silu_done = sem("silu_done")
        hid_ready = sem("hid_ready")
        hid_hi_done = sem("hid_hi_done")
        hid_split = sem("hid_split")
        pooled_d, pooled_g = sem("pooled_d"), sem("pooled_g")
        pool_hi = sem("pool_hi")
        pool_ready_d, pool_ready_g = sem("pool_ready_d"), sem("pool_ready_g")
        y_stored = [sem(f"y_stored{i}") for i in range(4)]
        states_ready, states_turned, states_out = sem("states_ready"), sem("states_turned"), sem("states_out")
        states_stored = sem("states_stored")
        dve_step, act_step, pool_step = sem("dve_step"), sem("act_step"), sem("pool_step")

        def group(t, g):
            return t[:, :, g * GT:(g + 1) * GT]

        def segments(g):
            return [(0, CTX, CTX_C), (CTX, GT, LAT_C)] if g == 0 else [(g * GT, (g + 1) * GT, LAT_C)]

        def released(w):
            item = next(i for i, n in WEIGHT.items() if n == w)
            if item[0] in ("rec", "branch"):
                return p_ready, P_START[item] + 6
            if item[0] == "gates":
                return p_ready, P_START[item] + 24
            if item[0] == "w_out":
                return out_ready, O_WOUT + 12 * (item[1] // 2 + 1) - 2 * (1 - item[1] % 2)
            if item[0] == "pool":
                return out_ready, O_POOL + 24
            if item[0] in ("gate", "up"):
                return pair_ready, PAIRS[item[1]] + 6 * (item[2] + 1)
            return out_ready, O_FFN[item[1]] + 24 * (item[2] + 1)

        def slot(w):
            return w % 3

        def grow(base, step, i, odd):
            return base + step * odd if i is None else base + step * odd + i * (2 * step)

        block = ctx.enter_context(nc.Block())

        @block.sync
        def _(sp):
            def source(item, b=None):
                kind = item[0]
                if kind == "mod":
                    c0 = 2 * P * item[2] if b is None else b * (4 * 2 * P) + 2 * P * item[2]
                    return a[f"l{item[1]}_mod_w"][:, bass.ds(c0, 2 * P)].rearrange("(k p) n -> p k n", p=P)
                if kind in ("rec", "branch"):
                    c0 = (D if kind == "rec" else 0) + 2 * P * item[1]
                    return a["l0_w_in"][:, c0:c0 + 2 * P].rearrange("(k p) n -> p k n", p=P)
                if kind == "w_out":
                    c0 = 2 * P * item[1]
                    return a["l0_w_out"][:, c0:c0 + 2 * P].rearrange("(k p) n -> p k n", p=P)
                if kind in ("gate", "up"):
                    c0 = (0 if kind == "gate" else DFF) + 2 * P * item[2]
                    c0 = c0 if b is None else b * (4 * P) + c0
                    return a[f"l{item[1]}_ffn_w_in"][:, bass.ds(c0, 2 * P)].rearrange("(k p) n -> p k n", p=P)
                if kind == "down":
                    r0 = 2 * P * item[2]
                    r0 = r0 if b is None else b * (4 * P) + r0
                    return a[f"l{item[1]}_ffn_w_out"][bass.ds(r0, 2 * P), :].rearrange("(k p) n -> p k n", p=P)
                return a["l1_pool_w"].rearrange("g (k p) e -> p g k e", p=P)

            def load(q, i=None, per_w=0, per_m=0):
                s = q % 2
                if q >= 2:
                    before = STREAM[q - 2]
                    if before[0] == "mod":
                        sp.wait_ge(mod_used, MOD[before] + 1 if i is None else i * per_m + (MOD[before] + 1))
                    else:
                        sp.wait_ge(w_ready, WEIGHT[before] + 1 if i is None else i * per_w + (WEIGHT[before] + 1))
                item = STREAM[q]
                if item[0] == "gates":
                    n = item[1]
                    dst = raw[:, s, :].rearrange("p (x d k e) -> p x d k e", x=2, d=2, k=2)
                    for x, name in enumerate(("l0_gate_a_w", "l0_gate_x_w")):
                        for d in range(2):
                            sp.dma_start(dst[:, x, d], a[name][d, n].rearrange("(k p) e -> p k e", p=P)
                                         ).then_inc(raw_landed[s], 16)
                    return
                src = source(item, i)
                if item[0] == "pool":
                    dst = raw[:, s, :].rearrange("p (g k e) -> p g k e", g=4, k=2)
                elif item[0] == "down":
                    dst = raw[:, s, :].rearrange("p (k n) -> p k n", k=2)
                else:
                    dst = raw[:, s, :].rearrange("p (k n) -> p k n", k=KT)
                sp.dma_start(dst, src).then_inc(raw_landed[s], 16)

            q = 0
            while q < len(STREAM):
                item = STREAM[q]
                if item[0] == "gate" and item[2] == 1:
                    per_block = 5 if item[1] == 0 else 3
                    with sp.Fori(0, LOOPS) as i:
                        for c in range(2 * per_block):
                            load(q + c, i, 6, 4)
                    q += 2 * per_block * LOOPS
                    continue
                load(q)
                q += 1
                if item == ("mod", 1, 1):
                    sp.wait_ge(states_out, 1)
                    sp.dma_start(outs[2].rearrange("b s (k p) -> (b s k) p", p=P), states_t[:, :]
                                 ).then_inc(states_stored, 16)
            for t in range(T // P):
                sp.wait_ge(t_freed, 2 * (t + 1))
                dst = outs[0][0] if t == 0 else outs[1][0, (t - 1) * P:t * P, :]
                sp.dma_start(dst, y_stage[:, t % 4, :]).then_inc(y_stored[t % 4], 16)
            for i in range(4):
                sp.wait_ge(y_stored[i], 16 * len(range(i, T // P, 4)))
            sp.wait_ge(states_stored, 16)

        @block.tensor
        def _(pe):
            def parts(w, x):
                return (w[0], x[0]), (w[0], x[1]), (w[1], x[0])

            def product(out, weights, moving, ks, between={}):
                last = None
                steps = [(k, part) for k in ks for part in range(3)]
                for n, (k, part) in enumerate(steps):
                    if part == 0 and k in between:
                        between[k]()
                    w, x = parts(weights(k), moving(k))[part]
                    last = pe.matmul(out, w, x, start=n == 0, stop=n == len(steps) - 1)
                return last

            def columns(w_slot, c, tile=None, kt=KT):
                def get(k):
                    v = [t[:, w_slot, :].rearrange("p (k n) -> p k n", k=kt) for t in (w_hi, w_lo)]
                    return [t[:, k, c * P:(c + 1) * P] for t in v]
                return get

            def moving_of(hi, lo, g):
                return lambda k: [t[:, k, g * GT:(g + 1) * GT] for t in (hi, lo)]

            def modulation(m, i=None, per_m=4):
                item = next(x for x, n in MOD.items() if n == m)
                q = Q[item]
                step = 80 if per_m else 0
                pe.wait_ge(raw_landed[q % 2], LANDED[q] if i is None else i * step + LANDED[q])
                for c in range(2):
                    col = 4 * item[2] + 2 * c
                    col = (0 if item[1] == 0 else P) + col
                    if i is not None:
                        col = i * 16 + col
                    for k in range(KT):
                        last = pe.matmul(bank[MOD_BANK][:, bass.ds(col, 2)],
                                         raw[:, q % 2, k * 2 * P + c * P:k * 2 * P + (c + 1) * P],
                                         cond[:, k, :], start=k == 0, stop=k == KT - 1)
                last.then_inc(mod_used, 1)

            sums = [0]

            def norm_sum():
                n = sums[0]
                pe.wait_ge(acc_ready, n + 1)
                if n:
                    pe.wait_ge(rstd_used, n)
                for c in range(GT // P):
                    last = pe.matmul(bank[NORM_BANK][:, c:c + 1], acc[:, c * P:(c + 1) * P], ones[:, 0:1],
                                     start=True, stop=True)
                last.then_inc(sum_ready, 1)
                sums[0] += 1

            spreads = [0]

            def norm_spread():
                n = spreads[0]
                pe.wait_ge(diag_ready, n + 1)
                pe.matmul(bank[NORM_BANK][:, P:P + GT], ones[:, :], diag[:, :], start=True, stop=True
                          ).then_inc(spread_ready, 1)
                spreads[0] += 1

            def norm_both():
                norm_sum()
                norm_spread()

            def out_bank(n, i=None, per=0):
                free = bank_free(n)
                if free > 0:
                    pe.wait_ge(out_taken, free if i is None else i * per + free)
                return bank[out_bank_of(n)]

            pe.wait_ge(const_landed, 16)
            pe.wait_ge(stage_landed, 16 * STAGE_DMAS)
            for s, rows in enumerate((P, 72, 96)):
                if s:
                    pe.wait_ge(vec_ready, s)
                pe.transpose(bank[NORM_BANK][:, 0:rows], stage[0:rows, s, :], const[0:rows, 0:rows]
                             ).then_inc(rows_turned, 1)

            def turn_x(t):
                pe.wait_ge(x_landed[t], 16)
                for half in range(2):
                    b = out_bank(2 * t + half)
                    for c in range(4):
                        k = 4 * half + c
                        last = pe.transpose(b[:, c * P:(c + 1) * P], x_stage[:, t % 4, k * P:(k + 1) * P], ident)
                    last.then_inc(out_ready, 1)

            pe.wait_ge(cond_ready, 1)
            pe.wait_ge(ones_ready, 1)
            for t in range(T // P):
                turn_x(t)
                if 1 <= t <= 8:
                    modulation(t - 1)
            for g in range(NG):
                norm_both()
            pe.wait_ge(out_taken, O_WOUT)

            mods = [8]
            for item in MIX_PHASES:
                kind, n = item
                w = WEIGHT[item]
                pe.wait_ge(w_ready, w + 1)
                p = P_START[item]
                if kind == "gates":
                    pe.wait_ge(u_ready, 2 * (n + 1))
                    for j in range(2):
                        for d in range(2):
                            for x in range(2):
                                for g in range(NG):
                                    pe.wait_ge(p_freed, p - 3)
                                    product(bank[p % 4][:, 0:GT],
                                            lambda k, c=(x * 2 + d) * 2: [
                                                t[:, slot(w), (c + k) * 2 * P + j * P:(c + k) * 2 * P + (j + 1) * P]
                                                for t in (w_hi, w_lo)],
                                            moving_of(u_hi, u_lo, g), range(2)).then_inc(p_ready, 1)
                                    p += 1
                    continue
                for g in range(NG):
                    if item == ("rec", 0):
                        pe.wait_ge(mv_ready, g + 1)
                    if g == 2:
                        modulation(mods[0])
                        modulation(mods[0] + 1)
                        mods[0] += 2
                    for j in range(2):
                        if p >= 4:
                            pe.wait_ge(p_freed, p - 3)
                        product(bank[p % 4][:, 0:GT], columns(slot(w), j), moving_of(mv_hi, mv_lo, g), range(KT)
                                ).then_inc(p_ready, 1)
                        p += 1
                if item == ("branch", 3):
                    pe.wait_ge(states_ready, 1)
                    pe.transpose(bank[MOD_BANK][0:16, 2 * P:3 * P], states[:, :], ident).then_inc(states_turned, 1)

            n = O_WOUT
            pe.wait_ge(p_freed, P_TOTAL)
            norms_at = {(1, 1, 5): {3: norm_sum}, (1, 1, 6): {0: norm_spread},
                        (1, 2, 4): {1: norm_sum, 6: norm_spread},
                        (1, 2, 7): {1: norm_sum, 6: norm_spread}}
            for c in range(2):
                for g in range(NG):
                    if c == 0:
                        pe.wait_ge(mv_ready, NG + g + 1)
                    for m in range(4 * c, 4 * c + 4):
                        w = WEIGHT["w_out", m // 2]
                        pe.wait_ge(w_ready, w + 1)
                        product(out_bank(n)[:, 0:GT], columns(slot(w), m % 2), moving_of(mv_hi, mv_lo, g), range(KT),
                                norms_at.get((c, g, m), {})).then_inc(out_ready, 1)
                        n += 1
                    if (c, g) == (1, 0):
                        modulation(24)
                        modulation(25)

            def ffn_in(layer, b, g, j, i=None, gate_norms={}, up_norms={}):
                k = PAIRS[layer] + 6 * b + 2 * g + j
                wg, wu = WEIGHT["gate", layer, b], WEIGHT["up", layer, b]

                def at_round(v, per):
                    return v if i is None else i * per + v

                if g == 0 and j == 0:
                    pe.wait_ge(w_ready, at_round(wg + 1, 6))
                if k >= 2:
                    pe.wait_ge(silu_done, at_round(k - 1, 12))
                product(bank[2 * (k % 2)][:, 0:GT], columns(slot(wg), j), moving_of(mv_hi, mv_lo, g), range(KT),
                        gate_norms).then_inc(gate_ready, 1)
                if g == 0 and j == 0:
                    pe.wait_ge(w_ready, at_round(wu + 1, 6))
                if k >= 2:
                    pe.wait_ge(hid_ready, at_round(k - 1, 12))
                product(bank[2 * (k % 2) + 1][:, 0:GT], columns(slot(wu), j), moving_of(mv_hi, mv_lo, g), range(KT),
                        up_norms).then_inc(pair_ready, 1)

            def ffn_out(layer, b, g, m, i=None):
                n = O_FFN[layer] + 24 * b + KT * g + m
                wd = WEIGHT["down", layer, b]

                def at_round(v, per):
                    return v if i is None else i * per + v

                if m == 0:
                    if g == 0:
                        pe.wait_ge(w_ready, at_round(wd + 1, 6))
                    pe.wait_ge(hid_split, at_round(PAIRS[layer] + 6 * b + 2 * g + 2, 12))
                product(out_bank(n, i, 48)[:, 0:GT], columns(slot(wd), m, kt=HB), moving_of(hid_hi, hid_lo, g),
                        range(HB)).then_inc(out_ready, 1)

            def ffn_block(layer, b, i=None):
                for g in range(NG):
                    for j in range(HB):
                        ffn_in(layer, b, g, j, i)
                if layer == 0:
                    m = 24 + 2 * (b + 1)
                    modulation(m, i)
                    modulation(m + 1, i)
                for g in range(NG):
                    for m in range(KT):
                        ffn_out(layer, b, g, m, i)

            def ffn_first(layer, ready):
                pe.wait_ge(mv_ready, ready)
                pe.wait_ge(out_taken, O_FFN[layer] - 4)
                ffn_in(layer, 0, 0, 0, up_norms={0: norm_sum, 5: norm_spread})
                pe.wait_ge(out_taken, O_FFN[layer])
                ffn_in(layer, 0, 0, 1, up_norms={0: norm_sum, 5: norm_spread})
                pe.wait_ge(mv_ready, ready + 1)
                ffn_in(layer, 0, 1, 0)
                ffn_in(layer, 0, 1, 1, gate_norms={0: norm_sum, 5: norm_spread})
                pe.wait_ge(mv_ready, ready + 2)
                ffn_in(layer, 0, 2, 0)
                ffn_in(layer, 0, 2, 1)
                if layer == 0:
                    modulation(26)
                    modulation(27)
                for g in range(NG):
                    for m in range(KT):
                        ffn_out(layer, 0, g, m)

            def ffn_rest(layer):
                with pe.Fori(0, LOOPS) as i:
                    ffn_block(layer, 1, i)
                    ffn_block(layer, 2, i)
                ffn_block(layer, NB - 2)

            ffn_first(0, 2 * NG + 1)
            ffn_rest(0)

            for g in range(NG):
                for j in range(HB):
                    ffn_in(0, NB - 1, g, j)
            modulation(46)
            modulation(47)

            def two_groups(out):
                for m in range(KT):
                    out(0, m)
                for m in range(3):
                    out(1, m)
                norm_sum()
                for m in range(3, 5):
                    out(1, m)
                norm_spread()
                for m in range(5, KT):
                    out(1, m)

            pe.wait_ge(hid_split, PAIRS[0] + 6 * NB)
            two_groups(lambda g, m: ffn_out(0, NB - 1, g, m))
            norm_both()
            for m in range(KT):
                ffn_out(0, NB - 1, 2, m)
            for g in range(1, NG):
                norm_both()
                norm_both()

            w = WEIGHT["pool",]
            pe.wait_ge(w_ready, w + 1)
            pe.wait_ge(pool_ready_d, 4)
            pe.wait_ge(pool_ready_g, 4)

            def pool_out(g, m):
                gi, j = m // 2, m % 2
                product(out_bank(O_POOL + KT * g + m)[:, 0:GT],
                        lambda k: [t[:, slot(w), (gi * 2 + k) * 2 * P + j * P:(gi * 2 + k) * 2 * P + (j + 1) * P]
                                   for t in (w_hi, w_lo)],
                        lambda k: [t[:, 2 * gi + k, g * GT:(g + 1) * GT] for t in (mv_hi, mv_lo)],
                        range(2)).then_inc(out_ready, 1)

            two_groups(pool_out)
            norm_both()
            for m in range(KT):
                pool_out(2, m)
            norm_both()
            ffn_first(1, 3 * NG + 1)
            ffn_rest(1)
            for g in range(NG):
                for j in range(HB):
                    ffn_in(1, NB - 1, g, j)
            pe.wait_ge(hid_split, PAIRS[1] + 6 * NB)

            def turn_y(g):
                pe.wait_ge(x_new, KT * (3 * NG + g + 1))
                for t in range(3 * g, 3 * g + 3):
                    for half in range(2):
                        n = 2 * t + half
                        if n >= 3:
                            pe.wait_ge(t_freed, n - 2)
                        b = bank[T_BANKS[n % 3]]
                        for c in range(4):
                            last = pe.transpose(b[:, c * P:(c + 1) * P], y[:, 4 * half + c, t * P:(t + 1) * P], ident)
                        last.then_inc(t_ready, 1)

            for m in range(KT):
                ffn_out(1, NB - 1, 0, m)
            for g in range(1, NG):
                for m in range(4):
                    ffn_out(1, NB - 1, g, m)
                norm_both()
                for m in range(4, KT):
                    ffn_out(1, NB - 1, g, m)
                turn_y(g - 1)
            norm_both()
            turn_y(NG - 1)

        @block.scalar
        def _(act):
            steps = [0]

            def link(ins):
                steps[0] += 1
                ins.then_inc(act_step, 1)
                act.wait_ge(act_step, steps[0])

            act.dma_start(const[:, :], consts[:, 0:NC]).then_inc(const_landed, 16)
            act.dma_start(pos[:, :], consts[:, NC:NC + NPOS]).then_inc(pos_landed, 16)
            for s, row, src in STAGE_ROWS(a):
                act.dma_start(stage[row:row + src.shape[0], s, :], src).then_inc(stage_landed, 16)
            for t in range(4):
                src = a["x_prompt"][0] if t == 0 else a["x_sample"][0, (t - 1) * P:t * P, :]
                act.dma_start(x_stage[:, t, :], src).then_inc(x_landed[t], 16)

            for s, (c0, rows) in enumerate(((0, P), (P, 72), (V_MODB, 96))):
                act.wait_ge(rows_turned, s + 1)
                act.activation(vec[:, c0:c0 + rows], bank[NORM_BANK][:, 0:rows], ACT.Copy).then_inc(vec_ready, 1)
            act.wait_ge(vec_ready, 3)
            link(act.activation(cond[:, :, LAT_C], vec[:, V_C:V_C + KT], ACT.Silu))
            act.activation(cond[:, :, CTX_C], vec[:, V_CCTX:V_CCTX + KT], ACT.Silu).then_inc(cond_ready, 1)
            act.wait_ge(lam_abs, 1)
            act.activation(lam[:, 1, :], lam[:, 0, :], ACT.Exp, scale=-1.0).then_inc(lam_exp, 1)

            def split_hi(w, i=None):
                item = next(x for x, n in WEIGHT.items() if n == w)
                q = Q[item]
                per_q = 80 if item[0] in ("gate", "up", "down") and item[1] == 0 else 48
                act.wait_ge(raw_landed[q % 2], LANDED[q] if i is None else i * per_q + LANDED[q])
                if w >= 3:
                    s, v = released(w - 3)
                    act.wait_ge(s, v if i is None else i * (12 if s is pair_ready else 48) + v)
                act.activation(w_hi[:, slot(w), :], raw[:, q % 2, :], ACT.Copy).then_inc(w_hi_ready, 1)

            stats = [0]

            def norm_squares(g, sem_of, count):
                for m in range(KT):
                    act.wait_ge(sem_of, count(m))
                    act.activation(group(wide, g)[:, m], group(y, g)[:, m], ACT.Square).then_inc(squares, 1)

            def norm_root():
                n = stats[0]
                act.wait_ge(var_ready, n + 1)
                act.activation(var[:, :], var[:, :], ACT.Sqrt).then_inc(rstd_ready, 1)
                stats[0] += 1

            affines = [0]

            def norm_hi(g):
                for part in range(4):
                    affines[0] += 1
                    act.wait_ge(affine_ready, affines[0])
                    v = slice(2 * part, 2 * part + 2)
                    act.activation(group(mv_hi, g)[:, v], group(wide, g)[:, v], ACT.Copy).then_inc(mv_hi_done, 1)

            news = [0]

            def post_norm(g, taken):
                norm_squares(g, out_taken, lambda m: taken(g, m))
                norm_root()

            def pre_norm(g, split=True, first=False):
                if first:
                    norm_squares(g, out_taken, lambda m: 6 * (g + 1))
                else:
                    norm_squares(g, x_new, lambda m, n=news[0]: KT * n + m + 1)
                    news[0] += 1
                norm_root()
                if split:
                    norm_hi(g)

            for g in range(NG):
                pre_norm(g, first=True)
                if g == 0:
                    split_hi(0)

            def evacuate(item):
                kind, n = item
                p = P_START[item]
                if item == ("rec", 0):
                    act.wait_ge(pads_ready, 1)
                if kind == "rec" and n:
                    act.wait_ge(conv_done, 2 * n)
                if item == ("branch", 0):
                    act.wait_ge(conv_done, 8)
                if item == ("branch", 3):
                    act.wait_ge(scanned, 16)
                for g in range(NG):
                    if g == 2:
                        for w in NEXT_GRANULES[item]:
                            split_hi(w)
                    for j in range(2):
                        act.wait_ge(p_ready, p + 1)
                        src = bank[p % 4]
                        if kind == "branch":
                            act.activation(mixed[:, MIXED_AT[2 * n + j], g * GT:(g + 1) * GT], src[:, 0:GT],
                                           ACT.Gelu_apprx_tanh).then_inc(p_freed, 1)
                        elif g == 0:
                            act.activation(rec[:, j, CP:CP + CTX], src[:, 0:CTX], ACT.Copy)
                            act.activation(rec[:, j, LP:LP + GT - CTX], src[:, CTX:GT], ACT.Copy
                                           ).then_inc(p_freed, 1)
                        else:
                            c0 = LP + g * GT - CTX
                            act.activation(rec[:, j, c0:c0 + GT], src[:, 0:GT], ACT.Copy).then_inc(p_freed, 1)
                        p += 1

            def u_split_hi(n):
                for j in range(2):
                    act.wait_ge(conv_done, 2 * n + j + 1)
                    act.activation(u_hi[:, j, :], u[:, j, :], ACT.Copy).then_inc(u_hi_done, 1)

            def gates(n):
                p = P_START["gates", n]
                for j in range(2):
                    for d in range(2):
                        s = 4 * n + 2 * j + d
                        col = 8 * d + 2 * n + j
                        if s >= 2:
                            act.wait_ge(scanned, s - 1)
                        if d == 1 and s >= 2:
                            act.wait_ge(h_stored, 16 * (s // 2))
                        for dst, bias in ((lru_a, V_BA), (lru_i, V_BX)):
                            for g in range(NG):
                                act.wait_ge(p_ready, p + 1)
                                act.activation(dst[:, d, g * GT:(g + 1) * GT], bank[p % 4][:, 0:GT], ACT.Sigmoid,
                                               bias=vec[:, bias + col:bias + col + 1]).then_inc(p_freed, 1)
                                p += 1
                        if s == 0:
                            act.wait_ge(rate_ready, 1)
                        act.wait_ge(p_freed, p)
                        link(act.activation(lru_m[:, d, :], lru_a[:, d, :], ACT.Tanh,
                                            scale=half_rate[:, col:col + 1]))
                        act.activation(lru_a[:, d, :], lru_a[:, d, :], ACT.Exp,
                                       scale=neg_rate[:, col:col + 1]).then_inc(gates_ready, 1)
                        act.activation(lru_m[:, d, :], lru_m[:, d, :], ACT.Sqrt).then_inc(gates_ready, 1)

            evacuate(("rec", 0))
            u_split_hi(0)
            evacuate(("rec", 1))
            for n in range(NLB):
                gates(n)
                if n < 3:
                    u_split_hi(n + 1)
                    evacuate(("rec", n + 2) if n < 2 else ("branch", 0))
            for n in range(1, 4):
                evacuate(("branch", n))
            split_hi(WEIGHT["w_out", 2])
            act.wait_ge(states_turned, 1)
            act.activation(states_t[:, :], bank[MOD_BANK][0:16, 2 * P:3 * P], ACT.Copy).then_inc(states_out, 1)

            for g in range(NG):
                for t0, t1 in ((0, 2), (2, 8)):
                    act.wait_ge(mixed_ready, t1)
                    s0 = MIXED_AT[t0]
                    act.activation(group(mv_hi, g)[:, t0:t1], group(mixed, g)[:, s0:s0 + t1 - t0], ACT.Copy
                                   ).then_inc(mv_hi_done, 1)
            split_hi(WEIGHT["w_out", 3])
            split_hi(WEIGHT["gate", 0, 0])

            def ffn_evacuate(layer, b, g, i=None, js=range(HB)):
                def at_round(v, per):
                    return v if i is None else i * per + v

                for j in js:
                    k = PAIRS[layer] + 6 * b + 2 * g + j
                    act.wait_ge(gate_ready, at_round(k + 1, 12))
                    if k >= 2:
                        act.wait_ge(hid_split, at_round(k - 1, 12))
                    act.activation(hid[:, k % 2, :], bank[2 * (k % 2)][:, 0:GT], ACT.Silu).then_inc(silu_done, 1)
                    act.wait_ge(hid_ready, at_round(k + 1, 12))
                    if b:
                        act.wait_ge(out_ready, at_round(O_FFN[layer] + 24 * (b - 1) + KT * (g + 1), 48))
                    act.activation(hid_hi[:, j, g * GT:(g + 1) * GT], hid[:, k % 2, :], ACT.Copy
                                   ).then_inc(hid_hi_done, 1)

            def ffn_block(layer, b, i=None, last=False):
                w = WEIGHT["gate", layer, b]
                split_hi(w + 2, i)
                for g in range(NG):
                    ffn_evacuate(layer, b, g, i)
                if w + 3 in WEIGHTS:
                    split_hi(w + 3, i)
                    split_hi(w + 4, i)

            def ffn_first(layer, taken):
                w = WEIGHT["gate", layer, 0]
                post_norm(0, taken)
                pre_norm(0)
                post_norm(1, taken)
                split_hi(w + 1)
                pre_norm(1)
                split_hi(w + 2)
                ffn_evacuate(layer, 0, 0, js=[0])
                post_norm(2, taken)
                ffn_evacuate(layer, 0, 0, js=[1])
                pre_norm(2)
                ffn_evacuate(layer, 0, 1)
                ffn_evacuate(layer, 0, 2)
                split_hi(w + 3)
                split_hi(w + 4)

            def ffn_rest(layer):
                with act.Fori(0, LOOPS) as i:
                    ffn_block(layer, 1, i)
                    ffn_block(layer, 2, i)
                ffn_block(layer, NB - 2)
                ffn_block(layer, NB - 1)

            ffn_first(0, lambda g, m: O_WOUT + 12 + 4 * (g + 1))
            ffn_rest(0)
            for g in range(NG):
                post_norm(g, lambda g, m: O_LAST[0] + KT * g + m + 1)
                pre_norm(g, split=False)
            affines[0] += 4 * NG
            for gi in range(4):
                for j, done in ((0, pooled_d), (1, pooled_g)):
                    act.wait_ge(done, gi + 1)
                    act.activation(mv_hi[:, 2 * gi + j, :], y[:, 2 * gi + j, :], ACT.Copy).then_inc(pool_hi, 1)
            ffn_first(1, lambda g, m: O_POOL + KT * g + (m | 1) + 1)
            ffn_rest(1)
            act.wait_ge(w_ready, len(WEIGHTS))

            def take_turned(g):
                for t in range(3 * g, 3 * g + 3):
                    if t >= 4:
                        act.wait_ge(y_stored[t % 4], 16 * (t // 4))
                    for half in range(2):
                        n = 2 * t + half
                        act.wait_ge(t_ready, n + 1)
                        act.activation(y_stage[:, t % 4, 4 * half * P:4 * (half + 1) * P], bank[T_BANKS[n % 3]][:, :],
                                       ACT.Copy).then_inc(t_freed, 1)

            for g in range(NG):
                norm_squares(g, out_taken, lambda m: O_LAST[1] + KT * g + m + 1)
                if g:
                    take_turned(g - 1)
                norm_root()
            take_turned(NG - 1)

        @block.vector
        def _(dve):
            steps = [0]

            def link(ins):
                steps[0] += 1
                ins.then_inc(dve_step, 1)
                dve.wait_ge(dve_step, steps[0])

            dve.memset(ones[:, :], 1.0).then_inc(ones_ready, 1)

            dve.wait_ge(vec_ready, 3)
            lv = vec[:, V_LAM:V_LAM + 16]
            link(dve.tensor_scalar(lam[:, 2, :], lv, -1.0, None, ALU.mult))
            dve.tensor_tensor(lam[:, 0, :], lam[:, 2, :], lv, ALU.max).then_inc(lam_abs, 1)
            dve.wait_ge(lam_exp, 1)
            z, s, s2, t = lam[:, 1, :], lam[:, 3, :], lam[:, 4, :], lam[:, 5, :]
            link(dve.tensor_scalar(s, z, 2.0, None, ALU.add))
            link(dve.reciprocal(s, s))
            link(dve.tensor_tensor(s, s, z, ALU.mult))
            link(dve.tensor_tensor(s2, s, s, ALU.mult))
            link(dve.tensor_scalar(t, s2, 1.0 / 17, 1.0 / 15, ALU.mult, ALU.add))
            for odd in (13, 11, 9, 7, 5, 3, 1):
                link(dve.tensor_tensor(t, t, s2, ALU.mult))
                link(dve.tensor_scalar(t, t, 1.0 / odd, None, ALU.add))
            link(dve.tensor_tensor(t, t, s, ALU.mult))
            link(dve.tensor_scalar(lam[:, 2, :], lam[:, 2, :], 0.0, 0.5, ALU.max, ALU.mult))
            link(dve.tensor_tensor(s, t, lam[:, 2, :], ALU.add))
            link(dve.tensor_scalar(neg_rate, s, -16.0, None, ALU.mult))
            dve.tensor_scalar(half_rate, s, 8.0, None, ALU.mult).then_inc(rate_ready, 1)

            def mod_take(layer, t0, t1, used):
                dve.wait_ge(mod_used, used)
                c0 = P * layer
                b0 = V_MODB + 48 * layer
                link(dve.tensor_tensor(
                    modv[:, layer, t0:t1, :],
                    bank[MOD_BANK][:, c0 + 2 * t0:c0 + 2 * t1].rearrange("p (t c) -> p t c", c=2),
                    vec[:, b0 + t0:b0 + t1].unsqueeze(2).to_broadcast([P, t1 - t0, 2]), ALU.add))

            def gain(layer, which):
                c0 = V_GAIN + 32 * layer + which
                return vec[:, c0:c0 + KT].unsqueeze(2).to_broadcast([P, KT, 2])

            def scale_coef(layer, n, tile, which):
                link(dve.scalar_tensor_tensor(out=coef[:, layer, n], in0=modv[:, layer, tile:tile + KT, :], scalar=1.0,
                                              in1=gain(layer, which), op0=ALU.add, op1=ALU.mult))

            def gate_coef(layer, n, tile, which):
                link(dve.tensor_tensor(coef[:, layer, n], modv[:, layer, tile:tile + KT, :], gain(layer, which),
                                       ALU.mult))

            stats = [0]

            def norm_stats(g):
                n = stats[0]
                dve.wait_ge(sum_ready, n + 1)
                link(dve.tensor_scalar(var[:, :], bank[NORM_BANK][:, 0:GT // P], 1.0 / D, EPS, ALU.mult, ALU.add))
                dve.reciprocal(var[:, :], var[:, :]).then_inc(var_ready, 1)
                dve.wait_ge(rstd_ready, n + 1)
                if n:
                    dve.wait_ge(spread_ready, n)
                dve.tensor_tensor(diag[:, :].rearrange("p (c t) -> p c t", t=P),
                                  ident.unsqueeze(1).to_broadcast([P, GT // P, P]),
                                  var[:, :].unsqueeze(2).to_broadcast([P, GT // P, P]), ALU.mult).then_inc(diag_ready, 1)
                dve.wait_ge(spread_ready, n + 1)
                stats[0] += 1

            rstd = bank[NORM_BANK][:, P:P + GT]

            def mark(ins):
                steps[0] += 1
                ins.then_inc(dve_step, 1)
                return steps[0]

            def times_rstd(out, g, then):
                done = None
                for m in range(KT + 1):
                    if m < KT:
                        ins = dve.tensor_tensor(group(out, g)[:, m], group(y, g)[:, m], rstd, ALU.mult)
                        if m == KT - 1:
                            ins.then_inc(rstd_used, 1)
                            after = None
                        else:
                            after = mark(ins)
                    if m:
                        if done is None:
                            dve.wait_ge(rstd_used, stats[0])
                        else:
                            dve.wait_ge(dve_step, done)
                        then(m - 1)
                    done = after

            loads = [0] * NG

            def post_norm(g, layer, n):
                norm_stats(g)
                loads[g] += 1
                dve.wait_ge(x_loaded[g], 16 * loads[g])

                def residual(k):
                    for t0, t1, c in segments(g):
                        ins = dve.scalar_tensor_tensor(out=y[:, k, t0:t1], in0=y[:, k, t0:t1],
                                                       scalar=coef[:, layer, n, k, c:c + 1], in1=x_old[:, k, t0:t1],
                                                       op0=ALU.mult, op1=ALU.add)
                    ins.then_inc(x_new, 1)

                times_rstd(y, g, residual)

            def pre_norm(g, layer, n, shift):
                norm_stats(g)

                def affine(k):
                    for t0, t1, c in segments(g):
                        ins = dve.tensor_scalar(wide[:, k, t0:t1], wide[:, k, t0:t1], coef[:, layer, n, k, c:c + 1],
                                                modv[:, layer, shift + k, c:c + 1], ALU.mult, ALU.add)
                    if k % 2:
                        ins.then_inc(affine_ready, 1)

                times_rstd(wide, g, affine)

            def take_x(t):
                for half in range(2):
                    n = 2 * t + half
                    dve.wait_ge(out_ready, n + 1)
                    src = bank[out_bank_of(n)][:, :].rearrange("p (k t) -> p k t", k=4)
                    dst = y[:, 4 * half:4 * half + 4, t * P:(t + 1) * P]
                    if t == 0:
                        ins = dve.tensor_copy(dst, src)
                    elif half == 0:
                        if t == 1:
                            dve.wait_ge(pos_landed, 16)
                        rows = pos[:, 0:4 * GRID_H].rearrange("p (k r) -> p k r", k=4)
                        r0 = (t - 1) * P // GRID_W
                        for r in range(P // GRID_W):
                            v = slice(r * GRID_W, (r + 1) * GRID_W)
                            ins = dve.tensor_tensor(dst[:, :, v], src[:, :, v],
                                                    rows[:, :, r0 + r:r0 + r + 1].to_broadcast([P, 4, GRID_W]),
                                                    ALU.add)
                    else:
                        cols = pos[:, 4 * GRID_H:NPOS].rearrange("p (k c) -> p k c", k=4)
                        for r in range(P // GRID_W):
                            v = slice(r * GRID_W, (r + 1) * GRID_W)
                            ins = dve.tensor_tensor(dst[:, :, v], src[:, :, v], cols, ALU.add)
                    ins.then_inc(out_taken, 1)

            for t in range(T // P):
                take_x(t)
            mod_take(0, 0, 16, 8)
            scale_coef(0, 0, 8, G_MIXPRE)
            dve.wait_ge(out_taken, O_WOUT)
            for g in range(NG):
                pre_norm(g, 0, 0, 0)

            for g in range(NG):
                dve.wait_ge(x_stored[g], 16)
            dve.memset(rec[:, :, :], 0.0).then_inc(pads_ready, 1)

            def conv(n, j):
                k = 2 * n + j
                dve.wait_ge(p_freed, P_START["rec", n] + 5 + j)
                if k >= 2:
                    dve.wait_ge(scanned, 4 * (n - 1) + 2 * j + 2)
                for seq, (t0, p0, size) in enumerate(((0, CP, CTX), (CTX, LP, LAT))):
                    dst = u[:, j, t0:t0 + size]

                    def tap(i):
                        return rec[:, j, p0 - 2 + i:p0 - 2 + i + size], vec[:, V_CONVW + 8 * i + k:V_CONVW + 8 * i + k + 1]

                    link(dve.tensor_scalar(dst, tap(0)[0], tap(0)[1], vec[:, V_CONVB + k:V_CONVB + k + 1],
                                           ALU.mult, ALU.add))
                    for i in range(1, 4):
                        ins = dve.scalar_tensor_tensor(out=dst, in0=tap(i)[0], scalar=tap(i)[1], in1=dst,
                                                       op0=ALU.mult, op1=ALU.add)
                        if (seq, i) == (1, 3):
                            ins.then_inc(conv_done, 1)
                        else:
                            link(ins)

            def lru_step(s):
                n, j, d = s // 4, s // 2 % 2, s % 2
                k = 2 * n + j
                dve.wait_ge(gates_ready, 2 * s + 2)
                av, iv, mv = lru_a[:, d, :], lru_i[:, d, :], lru_m[:, d, :]
                dve.scalar_tensor_tensor(out=mv, in0=av, scalar=1.0, in1=mv, op0=ALU.add, op1=ALU.mult)
                link(dve.tensor_tensor(iv, iv, u[:, j, :], ALU.mult))
                link(dve.tensor_tensor(mv, mv, iv, ALU.mult))
                dst = lru_f[:, :] if d == 0 else iv
                h0 = vec[:, V_STATE + 8 * d + k:V_STATE + 8 * d + k + 1]
                for (t0, t1), start in (((0, CTX), 0.0), ((CTX, T), h0)):
                    v = slice(t0, t1) if d == 0 else slice(t1 - 1, t0 - 1 if t0 else None, -1)
                    ins = dve.tensor_tensor_scan(dst[:, v], av[:, v], mv[:, v], start, ALU.mult, ALU.add)
                ins.then_inc(scanned, 1)
                dve.wait_ge(scanned, s + 1)
                col = 8 * d + k
                end = CTX - 1 if d == 0 else 0
                ins = dve.tensor_copy(states[:, col:col + 1], dst[:, end:end + 1])
                if s == 15:
                    ins.then_inc(states_ready, 1)
                    dve.wait_ge(states_ready, 1)
                else:
                    link(ins)
                if d == 1:
                    dve.tensor_tensor(iv, lru_f[:, :], iv, ALU.add).then_inc(h_ready, 1)
                    dve.wait_ge(h_ready, k + 1)

            conv(0, 0)
            conv(0, 1)
            for n in range(NLB):
                for j in range(2):
                    lru_step(4 * n + 2 * j)
                    lru_step(4 * n + 2 * j + 1)
                    if n < NLB - 1:
                        conv(n + 1, j)

            for n in range(4):
                dve.wait_ge(h_loaded[n], 16)
                dve.wait_ge(p_freed, P_START["branch", n] + 6)
                for j in range(2):
                    k = MIXED_AT[2 * n + j]
                    dve.tensor_tensor(mixed[:, k, :], mixed[:, k, :], h_sum[:, 2 * (n % 3) + j, :], ALU.mult
                                      ).then_inc(mixed_ready, 1)

            dve.wait_ge(states_out, 1)
            mod_take(0, 16, 48, 24)
            gate_coef(0, 1, 16, G_MIXPOST)
            scale_coef(0, 2, 32, G_FFNPRE)
            gate_coef(0, 3, 40, G_FFNPOST)

            def take_y(n, m, g):
                dve.wait_ge(out_ready, n + 1)
                dve.tensor_copy(y[:, m, g * GT:(g + 1) * GT], bank[out_bank_of(n)][:, 0:GT]).then_inc(out_taken, 1)

            def wout(c, g, ms=range(4)):
                for m in ms:
                    take_y(O_WOUT + 12 * c + 4 * g + m, 4 * c + m, g)

            def ffn_hidden(layer, b, g, i=None, js=range(HB)):
                def at_round(v, per):
                    return v if i is None else i * per + v

                for j in js:
                    k = PAIRS[layer] + 6 * b + 2 * g + j
                    dve.wait_ge(silu_done, at_round(k + 1, 12))
                    dve.wait_ge(pair_ready, at_round(k + 1, 12))
                    h = hid[:, k % 2, :]
                    dve.tensor_tensor(h, h, bank[2 * (k % 2) + 1][:, 0:GT], ALU.mult).then_inc(hid_ready, 1)
                    dve.wait_ge(hid_hi_done, at_round(k + 1, 12))
                    v = slice(g * GT, (g + 1) * GT)
                    dve.tensor_tensor(hid_lo[:, j, v], h, hid_hi[:, j, v].bitcast(F32), ALU.subtract
                                      ).then_inc(hid_split, 1)

            def ffn_add(layer, b, g, i=None):
                def at_round(v, per):
                    return v if i is None else i * per + v

                for m in range(KT):
                    n = O_FFN[layer] + 24 * b + KT * g + m
                    dve.wait_ge(out_ready, at_round(n + 1, 48))
                    dst, src = y[:, m, g * GT:(g + 1) * GT], bank[out_bank_of(n)][:, 0:GT]
                    if b == 0:
                        if m == 0:
                            dve.wait_ge(x_stored[g], 16 * (2 if layer == 0 else 4))
                        dve.tensor_copy(dst, src).then_inc(out_taken, 1)
                    else:
                        dve.wait_ge(out_taken, at_round(n - 23, 48))
                        dve.tensor_tensor(dst, dst, src, ALU.add).then_inc(out_taken, 1)

            def ffn_block(layer, b, i=None):
                for g in range(NG):
                    ffn_hidden(layer, b, g, i)
                for g in range(NG):
                    ffn_add(layer, b, g, i)

            def ffn(layer, taking):
                taking("post 0")
                post_norm(0, layer, 1)
                taking("pre 0")
                pre_norm(0, layer, 2, 24)
                taking("post 1")
                post_norm(1, layer, 1)
                taking("pre 1")
                pre_norm(1, layer, 2, 24)
                ffn_hidden(layer, 0, 0, js=[0])
                post_norm(2, layer, 1)
                ffn_hidden(layer, 0, 0, js=[1])
                pre_norm(2, layer, 2, 24)
                ffn_hidden(layer, 0, 1)
                ffn_hidden(layer, 0, 2)
                for g in range(NG):
                    ffn_add(layer, 0, g)
                with dve.Fori(0, LOOPS) as i:
                    ffn_block(layer, 1, i)
                    ffn_block(layer, 2, i)
                ffn_block(layer, NB - 2)
                for g in range(NG):
                    ffn_hidden(layer, NB - 1, g)

            for g in range(NG):
                wout(0, g)

            def taking_wout(norm):
                if norm == "post 0":
                    wout(1, 0)
                elif norm == "pre 0":
                    wout(1, 1, [0, 1])
                elif norm == "post 1":
                    wout(1, 1, [2, 3])
                elif norm == "pre 1":
                    wout(1, 2)

            ffn(0, taking_wout)
            mod_take(1, 0, 48, 48)
            scale_coef(1, 0, 8, G_MIXPRE)
            gate_coef(1, 1, 16, G_MIXPOST)
            scale_coef(1, 2, 32, G_FFNPRE)
            gate_coef(1, 3, 40, G_FFNPOST)
            ffn_add(0, NB - 1, 0)
            post_norm(0, 0, 3)
            ffn_add(0, NB - 1, 1)
            pre_norm(0, 1, 0, 0)
            ffn_add(0, NB - 1, 2)
            for g in range(1, NG):
                post_norm(g, 0, 3)
                pre_norm(g, 1, 0, 0)
            dve.wait_ge(affine_ready, AFFINE_POOL)
            for g in range(NG):
                dve.wait_ge(x_stored[g], 16 * 3)

            link(dve.memset(pool_d[:, 0, :], 0.0))
            for gi in range(4):
                pool_tile(dve, pool_d, wide, y, const, gi, 2 * gi, link, pooled_d, fused=True)
                dve.wait_ge(pool_hi, 2 * gi + 1)
                dve.tensor_tensor(mv_lo[:, 2 * gi, :], y[:, 2 * gi, :], mv_hi[:, 2 * gi, :].bitcast(F32),
                                  ALU.subtract).then_inc(pool_ready_d, 1)

            def take_pooled(g):
                for m in range(KT):
                    n = O_POOL + KT * g + m
                    dve.wait_ge(out_ready, n + 1)
                    dve.tensor_scalar(y[:, m, g * GT:(g + 1) * GT], bank[out_bank_of(n)][:, 0:GT],
                                      vec[:, V_POOLB + m:V_POOLB + m + 1], vec[:, V_PSCALE + m:V_PSCALE + m + 1],
                                      ALU.add, ALU.mult).then_inc(out_taken, 1)

            def taking_pooled(norm):
                if norm == "post 0":
                    take_pooled(0)
                elif norm == "pre 0":
                    take_pooled(1)
                elif norm == "post 1":
                    take_pooled(2)

            ffn(1, taking_pooled)
            ffn_add(1, NB - 1, 0)
            post_norm(0, 1, 3)
            ffn_add(1, NB - 1, 1)
            post_norm(1, 1, 3)
            ffn_add(1, NB - 1, 2)
            post_norm(2, 1, 3)

        @block.gpsimd
        def _(pool):
            steps = [0]

            def link(ins):
                steps[0] += 1
                ins.then_inc(pool_step, 1)
                pool.wait_ge(pool_step, steps[0])

            def split_lo(w, i=None):
                item = next(x for x, n in WEIGHT.items() if n == w)
                q = Q[item]
                pool.wait_ge(w_hi_ready, w + 1 if i is None else i * 6 + (w + 1))
                pool.tensor_tensor(w_lo[:, slot(w), :], raw[:, q % 2, :], w_hi[:, slot(w), :].bitcast(F32),
                                   ALU.subtract).then_inc(w_ready, 1)

            his = [0]

            sums = [0]

            def norm_acc(g):
                n = sums[0]
                for m in range(1, KT):
                    pool.wait_ge(squares, KT * n + m + 1)
                    if m == 1 and n:
                        pool.wait_ge(sum_ready, n)
                    ins = pool.tensor_tensor(acc[:, :], group(wide, g)[:, 0] if m == 1 else acc[:, :],
                                             group(wide, g)[:, m], ALU.add)
                    if m == KT - 1:
                        ins.then_inc(acc_ready, 1)
                    else:
                        link(ins)
                sums[0] += 1

            def norm_lo(g):
                for part in range(4):
                    his[0] += 1
                    pool.wait_ge(mv_hi_done, his[0])
                    v = slice(2 * part, 2 * part + 2)
                    ins = pool.tensor_tensor(group(mv_lo, g)[:, v], group(wide, g)[:, v],
                                             group(mv_hi, g)[:, v].bitcast(F32), ALU.subtract)
                ins.then_inc(mv_ready, 1)

            stores = [0] * NG
            news = [0]

            def store_x(g, first=False):
                if first:
                    pool.wait_ge(out_taken, 6 * (g + 1))
                else:
                    news[0] += KT
                    pool.wait_ge(x_new, news[0])
                pool.dma_start(group(scratch_x, g), group(y, g)).then_inc(x_stored[g], 16)
                stores[g] += 1

            def load_x(g, free):
                pool.wait_ge(x_stored[g], 16 * stores[g])
                pool.wait_ge(out_ready, free)
                pool.dma_start(group(x_old, g), group(scratch_x, g)).then_inc(x_loaded[g], 16)

            for t in range(4, T // P):
                pool.wait_ge(out_ready, 2 * (t - 4) + 2)
                pool.dma_start(x_stage[:, t % 4, :], a["x_sample"][0, (t - 1) * P:t * P, :]
                               ).then_inc(x_landed[t], 16)
            for g in range(NG):
                norm_acc(g)
                store_x(g, first=True)
                norm_lo(g)
                if g == 0:
                    split_lo(0)

            def u_split_lo(n, j):
                pool.wait_ge(u_hi_done, 2 * n + j + 1)
                pool.tensor_tensor(u_lo[:, j, :], u[:, j, :], u_hi[:, j, :].bitcast(F32), ALU.subtract
                                   ).then_inc(u_ready, 1)

            def store_h(k):
                pool.wait_ge(h_ready, k + 1)
                pool.dma_start(scratch_h[:, k, :], lru_i[:, 1, :]).then_inc(h_stored, 16)

            def split_next(item):
                for w in NEXT_GRANULES[item]:
                    split_lo(w)

            split_next(("rec", 0))
            u_split_lo(0, 0)
            u_split_lo(0, 1)
            split_next(("rec", 1))
            for n in range(NLB):
                for j in range(2):
                    store_h(2 * n + j)
                    if n < NLB - 1:
                        u_split_lo(n + 1, j)
                if n < NLB - 1:
                    split_next(("rec", n + 2) if n < 2 else ("branch", 0))
            pool.wait_ge(h_stored, 16 * KT)
            pool.wait_ge(scanned, 16)
            for n in range(3):
                pool.dma_start(h_sum[:, 2 * n:2 * n + 2, :], scratch_h[:, 2 * n:2 * n + 2, :]).then_inc(h_loaded[n], 16)
            split_next(("branch", 1))
            split_next(("branch", 2))
            pool.wait_ge(mixed_ready, 2)
            pool.dma_start(h_sum[:, 0:2, :], scratch_h[:, 6:8, :]).then_inc(h_loaded[3], 16)
            split_next(("branch", 3))
            split_lo(WEIGHT["w_out", 2])
            for g in range(NG):
                for t0, t1 in ((0, 2), (2, 8)):
                    his[0] += 1
                    pool.wait_ge(mv_hi_done, his[0])
                    s0 = MIXED_AT[t0]
                    ins = pool.tensor_tensor(group(mv_lo, g)[:, t0:t1], group(mixed, g)[:, s0:s0 + t1 - t0],
                                             group(mv_hi, g)[:, t0:t1].bitcast(F32), ALU.subtract)
                ins.then_inc(mv_ready, 1)
            split_lo(WEIGHT["w_out", 3])
            split_lo(WEIGHT["gate", 0, 0])

            def ffn_first(layer, free):
                w = WEIGHT["gate", layer, 0]
                for g in range(NG):
                    load_x(g, free(g))
                    norm_acc(g)
                    if g == 1:
                        split_lo(w + 1)
                    norm_acc(g)
                    store_x(g)
                    norm_lo(g)
                    if g == 1:
                        split_lo(w + 2)
                split_lo(w + 3)
                split_lo(w + 4)

            def ffn_block(layer, b, i=None):
                w = WEIGHT["gate", layer, b]
                split_lo(w + 2, i)
                if w + 3 in WEIGHTS:
                    split_lo(w + 3, i)
                    split_lo(w + 4, i)

            def ffn_rest(layer):
                with pool.Fori(0, LOOPS) as i:
                    ffn_block(layer, 1, i)
                    ffn_block(layer, 2, i)
                ffn_block(layer, NB - 2)
                ffn_block(layer, NB - 1)

            ffn_first(0, lambda g: O_WOUT + 12 + 4 * (g + 1))
            ffn_rest(0)
            for g in range(NG):
                load_x(g, O_LAST[0] + KT * (g + 1))
                norm_acc(g)
                norm_acc(g)
                store_x(g)

            pool.wait_ge(affine_ready, AFFINE_POOL)
            for g in range(NG):
                pool.wait_ge(x_stored[g], 16 * 3)
            pool.wait_ge(states_stored, 16)
            link(pool.memset(pool_g[:, 0, :], 0.0))
            for gi in range(4):
                pool_tile(pool, pool_g, wide, y, const, gi, 2 * gi + 1, link, pooled_g, fused=False)
                pool.wait_ge(pool_hi, 2 * gi + 2)
                pool.tensor_tensor(mv_lo[:, 2 * gi + 1, :], y[:, 2 * gi + 1, :],
                                   mv_hi[:, 2 * gi + 1, :].bitcast(F32), ALU.subtract).then_inc(pool_ready_g, 1)
            ffn_first(1, lambda g: O_POOL + KT * (g + 1))
            ffn_rest(1)
            for g in range(NG):
                load_x(g, O_LAST[1] + KT * (g + 1))
                norm_acc(g)


NEXT_GRANULES = {("rec", 0): [1], ("rec", 1): [2, 3], ("rec", 2): [4, 5], ("rec", 3): [6, 7],
                 ("branch", 0): [8, 9], ("branch", 1): [10], ("branch", 2): [11], ("branch", 3): [12, 13]}
WEIGHTS = set(WEIGHT.values())
MIXED_AT = [6, 7, 0, 1, 2, 3, 4, 5]
AFFINE_POOL = 3 * 4 * NG


def pool_tile(eng, buf, h, out, const, gi, k, link, done, fused):
    w = WINDOWS[gi]
    c0, l0 = PAD, 2 * PAD + CTX
    eng.tensor_copy(buf[:, 0, c0:c0 + CTX], h[:, k, 0:CTX])
    link(eng.tensor_copy(buf[:, 0, l0:l0 + LAT], h[:, k, CTX:T]))
    src, dst, span, size = 0, 1, 1, PL
    while span < w:
        size -= span
        link(eng.tensor_tensor(buf[:, dst, 0:size], buf[:, src, 0:size], buf[:, src, span:span + size], ALU.add))
        src, dst, span = dst, 3 - dst if src else 2, span * 2
    e0 = C_EDGE + sum(a + b for v, a, b in EDGES if v < w)
    left, right = w // 2, w // 2 - 1
    for start, size in ((c0, CTX), (l0, LAT)):
        first = start - w // 2
        ins = eng.tensor_tensor(buf[:, src, first:first + left], buf[:, src, first:first + left],
                                const[:, e0:e0 + left], ALU.mult)
        if right:
            ins = eng.tensor_tensor(buf[:, src, first + size - right:first + size],
                                    buf[:, src, first + size - right:first + size],
                                    const[:, e0 + left:e0 + left + right], ALU.mult)
        link(ins)
    for n, (start, t0, size) in enumerate(((c0, 0, CTX), (l0, CTX, LAT))):
        first = start - w // 2
        s = buf[:, src, first:first + size]
        if fused:
            ins = eng.scalar_tensor_tensor(out=out[:, k, t0:t0 + size], in0=s, scalar=1.0 / w,
                                           in1=h[:, k, t0:t0 + size], op0=ALU.mult, op1=ALU.subtract)
        else:
            link(eng.tensor_scalar(s, s, 1.0 / w, None, ALU.mult))
            ins = eng.tensor_tensor(out[:, k, t0:t0 + size], s, h[:, k, t0:t0 + size], ALU.subtract)
    ins.then_inc(done, 1)


def STAGE_ROWS(a):
    rows = []
    for base, name in ((V_C, "c"), (V_CCTX, "c_ctx"), (V_CONVW, "l0_conv_w"), (V_CONVB, "l0_conv_b"),
                       (V_BA, "l0_gate_a_b"), (V_BX, "l0_gate_x_b"), (V_LAM, "l0_lambda"),
                       (V_STATE, "state_l0_rglru"), (V_POOLB, "l1_pool_b")):
        rows.append((0, base, name))
    for layer in range(2):
        for which, name in ((G_MIXPRE, "mix_pre_g"), (G_MIXPOST, "mix_post_g"), (G_FFNPRE, "ffn_pre_g"),
                            (G_FFNPOST, "ffn_post_g")):
            rows.append((1, V_GAIN - P + 32 * layer + which, f"l{layer}_{name}"))
    rows.append((1, V_PSCALE - P, "l1_pool_scale"))
    for layer in range(2):
        rows.append((2, 48 * layer, f"l{layer}_mod_b"))

    def flat(v):
        while len(v.shape) > 2:
            v = v.rearrange("a b c -> (a b) c")
        if len(v.shape) == 2:
            v = v.rearrange("a b -> (a b)")
        return v.rearrange("(r p) -> r p", p=P)

    return [(s, row, flat(a[name])) for s, row, name in rows]


STAGE_DMAS = 20


def constants():
    quarter = D // 4
    omega = (1.0 / (10000.0 ** (np.arange(quarter, dtype=np.float32) / np.float32(quarter)))).astype(np.float32)

    def emb(n):
        ang = np.arange(n, dtype=np.float32)[:, None] * omega[None, :]
        e = np.concatenate([np.sin(ang), np.cos(ang)], axis=-1).astype(np.float32)
        return e.T.reshape(4, P, n).transpose(1, 0, 2).reshape(P, 4 * n)

    edge = []
    for w, left, right in EDGES:
        edge += [w / (w // 2 + t) for t in range(left)]
        edge += [w / (w - t) for t in range(1, right + 1)]
    out = np.concatenate([np.eye(P), np.tile(np.array(edge)[None], (P, 1)), emb(GRID_H), emb(GRID_W)], axis=1)
    return np.ascontiguousarray(out.astype(np.float32))


_INS = ['x_prompt', 'x_sample', 'state_l0_rglru', 'c', 'c_ctx', 'l0_mod_w', 'l0_mod_b', 'l0_mix_pre_g',
        'l0_mix_post_g', 'l0_w_in', 'l0_conv_w', 'l0_conv_b', 'l0_gate_a_w', 'l0_gate_a_b', 'l0_gate_x_w',
        'l0_gate_x_b', 'l0_lambda', 'l0_w_out', 'l0_ffn_pre_g', 'l0_ffn_post_g', 'l0_ffn_w_in', 'l0_ffn_w_out',
        'l1_mod_w', 'l1_mod_b', 'l1_mix_pre_g', 'l1_mix_post_g', 'l1_pool_w', 'l1_pool_b', 'l1_pool_scale',
        'l1_ffn_pre_g', 'l1_ffn_post_g', 'l1_ffn_w_in', 'l1_ffn_w_out']
_OUTS = [(1, CTX, D), (1, LAT, D), (1, 2, D)]


def kernel(**inputs):
    import concourse.bacc as _bacc
    from concourse.bass_utils import run_bass_kernel_spmd as _run

    nc = _bacc.Bacc("TRN2", target_bir_lowering=False, num_devices=1)
    arrays, aps = {}, {}
    for name in _INS:
        arrays[f"in_{name}"] = np.ascontiguousarray(inputs[name])
        aps[name] = nc.dram_tensor(f"in_{name}", arrays[f"in_{name}"].shape, F32, kind="ExternalInput").ap()
    arrays["in_constants"] = constants()
    consts = nc.dram_tensor("in_constants", arrays["in_constants"].shape, F32, kind="ExternalInput").ap()
    scratch_x = nc.dram_tensor("residual", [P, KT, T], F32).ap()
    scratch_h = nc.dram_tensor("recurrence", [P, KT, T], F32).ap()
    outs = [nc.dram_tensor(f"out_{i}", shape, F32, kind="ExternalOutput").ap() for i, shape in enumerate(_OUTS)]
    program(nc, aps, scratch_x, scratch_h, consts, outs)
    r = _run(nc, [arrays], core_ids=[0])
    return tuple(r.results[0][f"out_{i}"] for i in range(len(_OUTS)))
```

```python
from contextlib import ExitStack

import numpy as np

import concourse.bass as bass
from concourse import mybir

F32 = mybir.dt.float32
F32R = mybir.dt.float32r
ALU = mybir.AluOpType
ACT = mybir.ActivationFunctionType

P = 128
D = 1024
KT = D // P
CTX = 128
LAT = 1024
T = CTX + LAT
NG = 3
GT = T // NG
DFF = 2816
HB = 2
NB = DFF // (HB * P)
NLB = 4
GRID_W = 64
GRID_H = LAT // GRID_W
WINDOWS = (2, 4, 8, 16)
EPS = 1e-6
GC = 2048
PAD = 8
PL = 3 * PAD + T
CP, LP = 2, CTX + 5
RL = T + 8
CTX_C, LAT_C = 1, 0

V_C, V_CCTX, V_CONVW, V_CONVB, V_BA, V_BX, V_LAM, V_STATE, V_POOLB = 0, 8, 16, 48, 56, 72, 88, 104, 120
V_GAIN, V_PSCALE = 128, 192
V_MODB = 200
NV = 296
G_MIXPRE, G_MIXPOST, G_FFNPRE, G_FFNPOST = 0, 8, 16, 24

C_ID, C_EDGE = 0, P
EDGES = [(w, w // 2, w // 2 - 1) for w in WINDOWS]
NC = C_EDGE + sum(a + b for _, a, b in EDGES)
NPOS = 4 * GRID_H + 4 * GRID_W


LOOPS = (NB - 3) // 2
FIRST_MODS = 8
DIRECT = 4
STAGED = 6
MOD_TURNS = [0, 1, 2, 4, 3, 5, 6, 7]


def stream_order():
    def mods(layer, m0, m1):
        return [("mod", layer, m) for m in range(m0, m1)]

    order = mods(0, STAGED, FIRST_MODS)
    order += MIX_PHASES[:-1] + mods(0, 8, 10) + MIX_PHASES[-1:]
    order += [("w_out", 0)] + mods(0, 10, 12) + [("w_out", 1)] + mods(0, 12, 14) + [("w_out", 2)]
    order += mods(0, 14, 20) + [("w_out", 3)]
    for b in range(NB):
        order += [("gate", 0, b), ("up", 0, b), ("down", 0, b)]
        if b == 0:
            order += mods(0, 20, 22)
        elif b <= 2 * LOOPS:
            order += mods(1, 3 * (b - 1), 3 * b)
        elif b == NB - 2:
            order += mods(0, 22, 24)
    order.append(("pool",))
    for b in range(NB):
        order += [("gate", 1, b), ("up", 1, b), ("down", 1, b)]
    return order


MIX_PHASES = [("rec", 0), ("rec", 1), ("gates", 0), ("rec", 2), ("gates", 1), ("rec", 3), ("gates", 2),
              ("branch", 0), ("gates", 3), ("branch", 1), ("branch", 2), ("branch", 3)]
STREAM = stream_order()
Q = {item: q for q, item in enumerate(STREAM)}
WEIGHT = {item: w for w, item in enumerate(i for i in STREAM if i[0] != "mod")}
MOD = {item: STAGED + m for m, item in enumerate(i for i in STREAM if i[0] == "mod")}
MOD.update({("mod", 0, m): m for m in range(STAGED)})


def landed_values():
    count, out = [0, 0], []
    for q, item in enumerate(STREAM):
        count[q % 2] += 64 if item[0] == "gates" else 16
        out.append(count[q % 2])
    return out


LANDED = landed_values()

P_START = {}
_n = 0
for _item in MIX_PHASES:
    P_START[_item] = _n
    _n += 24 if _item[0] == "gates" else 6
P_TOTAL = _n
O_XIN = 0
O_WOUT = O_XIN + 2 * T // P
O_FFN = [O_WOUT + 24, 0]
O_POOL = O_FFN[0] + 24 * NB
O_FFN[1] = O_POOL + 24
O_LAST = [start + 24 * (NB - 1) for start in O_FFN]
PAIRS = [0, 6 * NB]


def out_bank_of(n):
    if n >= O_LAST[1]:
        return n % 4
    beside = any(start <= n < last for start, last in zip(O_FFN, O_LAST))
    return 4 + n % 2 if beside else n % 6


def phase_start(n):
    return max(start for start in (O_XIN, O_WOUT, O_FFN[0], O_LAST[0], O_POOL, O_FFN[1], O_LAST[1]) if start <= n)


def bank_free(n):
    last = next((v for v in range(n - 1, phase_start(n) - 1, -1) if out_bank_of(v) == out_bank_of(n)), -1)
    return max(last + 1, phase_start(n))


def program(nc, a, scratch_x, scratch_h, consts, outs):
    ctx = ExitStack()
    at = [(nc.sbuf_base + 31) // 32 * 32]

    def place(name, shape, dt, offset):
        return nc.alloc_sbuf_tensor_at(name, shape, dt, offset=offset)

    def region(nbytes):
        here = at[0]
        at[0] += (nbytes + 31) // 32 * 32
        return here

    r_raw = region(2 * GC * 4)
    raw = place("raw", [P, 2, GC], F32, r_raw)
    w_hi = place("w_hi", [P, 3, GC], F32R, at[0])
    mod_stage = place("mod_stage", [P, STAGED, GC], F32, region(3 * GC * 4))
    w_lo = place("w_lo", [P, 3, GC], F32R, region(3 * GC * 4))
    r_hi = region(KT * T * 4)
    r_lo = region(KT * T * 4)
    mv_hi = place("mv_hi", [P, KT, T], F32R, r_hi)
    mv_lo = place("mv_lo", [P, KT, T], F32R, r_lo)
    x_old = place("x_old", [P, KT, T], F32, r_hi)
    wide = place("wide", [P, KT, T], F32, r_lo)
    x_stage = place("x_stage", [P, T // P, D], F32, r_hi)
    r_y = region(6 * T * 4 + 2 * RL * 4)
    y = place("y", [P, KT, T], F32, r_y)
    mixed = place("mixed", [P, KT, T], F32, r_y)
    u_hi = place("u_hi", [P, 2, T], F32R, r_y)
    u_lo = place("u_lo", [P, 2, T], F32R, r_y + 2 * T * 4)
    u = place("u", [P, 2, T], F32, r_y + 4 * T * 4)
    rec = place("rec", [P, 2, RL], F32, r_y + 6 * T * 4)
    r_z = region(7 * T * 4)
    lru_a = place("lru_a", [P, 2, T], F32, r_z)
    lru_i = place("lru_i", [P, 2, T], F32, r_z + 2 * T * 4)
    lru_m = place("lru_m", [P, 2, T], F32, r_z + 4 * T * 4)
    lru_f = place("lru_f", [P, T], F32, r_z + 6 * T * 4)
    h_sum = place("h_sum", [P, 6, T], F32, r_z)
    hid_hi = place("hid_hi", [P, HB, T], F32R, r_z)
    hid_lo = place("hid_lo", [P, HB, T], F32R, r_z + HB * T * 4)
    hid = place("hid", [P, 2, GT], F32, r_z + 2 * HB * T * 4)
    stage = place("stage", [P, 3, P], F32, r_z)
    mod_sum_norms = place("mod_sum_norms", [P, 2, 2, 2 * P], F32, r_z + 2 * HB * T * 4 + 2 * GT * 4)
    mod_sum_branch = place("mod_sum_branch", [P, 2, 2, 2 * P], F32, r_z + 6 * T * 4 + P * 4)
    y_stage = place("y_stage", [P, 4, D], F32, r_raw)
    pool_d = place("pool_d", [P, 3, PL], F32, r_z)
    pool_g = place("pool_g", [P, 3, PL], F32, r_z + 3 * PL * 4)
    pos = place("pos", [P, NPOS], F32, r_z + 4 * D * 4)
    states_t = place("states_t", [16, P], F32, r_z + 6 * T * 4)
    acc = place("acc", [P, GT], F32, r_z + 7 * T * 4 - 2 * GT * 4)
    diag = place("diag", [P, GT], F32, r_z + 7 * T * 4 - GT * 4)
    const = place("const", [P, NC], F32, region(NC * 4))
    ones = place("ones", [P, P], F32, region(P * 4))
    vec = place("vec", [P, NV], F32, region(NV * 4))
    cond = place("cond", [P, KT, 2], F32, region(KT * 2 * 4))
    modv = place("modv", [P, 2, 48, 2], F32, region(2 * 96 * 4))
    coef = place("coef", [P, 2, 4, KT, 2], F32, region(2 * 4 * KT * 2 * 4))
    lam = place("lam", [P, 6, 16], F32, region(6 * 16 * 4))
    var = place("var", [P, GT // P], F32, region(GT // P * 4))
    states = place("states", [P, 16], F32, region(16 * 4))
    assert at[0] <= nc.sbuf_usable_end, at[0] - nc.sbuf_usable_end

    ident = const[:, C_ID:C_ID + P]
    neg_rate, half_rate = lam[:, 4, :], lam[:, 5, :]

    with ctx:
        bank = [ctx.enter_context(nc.psum_tensor(f"bank{i}", [P, 512], F32)) for i in range(8)]
        NORM_BANK, MOD_BANK, T_BANKS = 6, 7, (4, 5, 7)

        def sem(name):
            return ctx.enter_context(nc.semaphore(name))

        raw_landed = [sem("raw_landed0"), sem("raw_landed1")]
        stage_landed = [sem(f"stage_landed{s}") for s in range(3)]
        const_landed = sem("const_landed")
        pos_landed = sem("pos_landed")
        pads_ready = sem("pads_ready")
        x_landed = [sem(f"x_landed{t}") for t in range(T // P)]
        rows_turned = sem("rows_turned")
        vec_ready = sem("vec_ready")
        cond_ready = sem("cond_ready")
        ones_ready = sem("ones_ready")
        w_hi_ready = sem("w_hi_ready")
        w_ready = sem("w_ready")
        mod_landed = [sem(f"mod_landed{m}") for m in range(STAGED)]
        mod_step, mod_summed, mod_done = sem("mod_step"), sem("mod_summed"), sem("mod_done")
        lam_exp = sem("lam_exp")
        lam_abs = sem("lam_abs")
        rate_ready = sem("rate_ready")
        p_ready = sem("p_ready")
        p_freed = sem("p_freed")
        out_ready = sem("out_ready")
        out_taken = sem("out_taken")
        squares = sem("squares")
        acc_ready = sem("acc_ready")
        sum_ready = sem("sum_ready")
        var_ready = sem("var_ready")
        diag_ready = sem("diag_ready")
        spread_ready = sem("spread_ready")
        rstd_used = sem("rstd_used")
        t_ready, t_freed = sem("t_ready"), sem("t_freed")
        rstd_ready = sem("rstd_ready")
        x_new = sem("x_new")
        affine_ready = sem("affine_ready")
        mv_hi_done = sem("mv_hi_done")
        mv_ready = sem("mv_ready")
        x_stored = [sem(f"x_stored{g}") for g in range(NG)]
        x_loaded = [sem(f"x_loaded{g}") for g in range(NG)]
        conv_done = sem("conv_done")
        u_hi_done = sem("u_hi_done")
        u_ready = sem("u_ready")
        gates_ready = sem("gates_ready")
        scanned = sem("scanned")
        h_ready = sem("h_ready")
        h_stored = sem("h_stored")
        h_loaded = [sem(f"h_loaded{n}") for n in range(4)]
        mixed_ready = sem("mixed_ready")
        gate_ready = sem("gate_ready")
        pair_ready = sem("pair_ready")
        silu_done = sem("silu_done")
        hid_ready = sem("hid_ready")
        hid_hi_done = sem("hid_hi_done")
        hid_split = sem("hid_split")
        pooled_d, pooled_g = sem("pooled_d"), sem("pooled_g")
        pool_src_d, pool_src_g = sem("pool_src_d"), sem("pool_src_g")
        pool_begun_d, pool_begun_g = sem("pool_begun_d"), sem("pool_begun_g")
        pool_pads_d, pool_pads_g = sem("pool_pads_d"), sem("pool_pads_g")
        pool_hi_d, pool_hi_g = sem("pool_hi_d"), sem("pool_hi_g")
        pool_ready_d, pool_ready_g = sem("pool_ready_d"), sem("pool_ready_g")
        y_stored = [sem(f"y_stored{i}") for i in range(4)]
        states_ready, states_turned, states_out = sem("states_ready"), sem("states_turned"), sem("states_out")
        states_stored = sem("states_stored")
        dve_step, act_step, pool_step = sem("dve_step"), sem("act_step"), sem("pool_step")

        def group(t, g):
            return t[:, :, g * GT:(g + 1) * GT]

        def segments(g):
            return [(0, CTX, CTX_C), (CTX, GT, LAT_C)] if g == 0 else [(g * GT, (g + 1) * GT, LAT_C)]

        def released(w):
            item = next(i for i, n in WEIGHT.items() if n == w)
            if item[0] in ("rec", "branch"):
                return p_ready, P_START[item] + 6
            if item[0] == "gates":
                return p_ready, P_START[item] + 24
            if item[0] == "w_out":
                return out_ready, O_WOUT + 12 * (item[1] // 2 + 1) - 2 * (1 - item[1] % 2)
            if item[0] == "pool":
                return out_ready, O_POOL + 24
            if item[0] in ("gate", "up"):
                return pair_ready, PAIRS[item[1]] + 6 * (item[2] + 1)
            return out_ready, O_FFN[item[1]] + 24 * (item[2] + 1)

        def slot(w):
            return w % 3

        def done_count(m):
            return (MOD_TURNS.index(m) if m < FIRST_MODS else m) + 1

        def mod_sums(m):
            return (mod_sum_branch if 8 <= m < 14 else mod_sum_norms)[:, (m - DIRECT) % 2]

        def grow(base, step, i, odd):
            return base + step * odd if i is None else base + step * odd + i * (2 * step)

        block = ctx.enter_context(nc.Block())

        @block.sync
        def _(sp):
            def source(item, b=None):
                kind = item[0]
                if kind == "mod":
                    c0 = 2 * P * item[2] if b is None else b * (6 * 2 * P) + 2 * P * item[2]
                    return a[f"l{item[1]}_mod_w"][:, bass.ds(c0, 2 * P)].rearrange("(k p) n -> p k n", p=P)
                if kind in ("rec", "branch"):
                    c0 = (D if kind == "rec" else 0) + 2 * P * item[1]
                    return a["l0_w_in"][:, c0:c0 + 2 * P].rearrange("(k p) n -> p k n", p=P)
                if kind == "w_out":
                    c0 = 2 * P * item[1]
                    return a["l0_w_out"][:, c0:c0 + 2 * P].rearrange("(k p) n -> p k n", p=P)
                if kind in ("gate", "up"):
                    c0 = (0 if kind == "gate" else DFF) + 2 * P * item[2]
                    c0 = c0 if b is None else b * (4 * P) + c0
                    return a[f"l{item[1]}_ffn_w_in"][:, bass.ds(c0, 2 * P)].rearrange("(k p) n -> p k n", p=P)
                if kind == "down":
                    r0 = 2 * P * item[2]
                    r0 = r0 if b is None else b * (4 * P) + r0
                    return a[f"l{item[1]}_ffn_w_out"][bass.ds(r0, 2 * P), :].rearrange("(k p) n -> p k n", p=P)
                return a["l1_pool_w"].rearrange("g (k p) e -> p g k e", p=P)

            def load(q, i=None, per_w=0, per_m=0):
                s = q % 2
                if q >= 2:
                    before = STREAM[q - 2]
                    if before[0] == "mod":
                        v = 2 * (MOD[before] - DIRECT + 1)
                        sp.wait_ge(mod_summed, v if i is None else i * per_m + v)
                    else:
                        sp.wait_ge(w_ready, WEIGHT[before] + 1 if i is None else i * per_w + (WEIGHT[before] + 1))
                item = STREAM[q]
                if item[0] == "gates":
                    n = item[1]
                    dst = raw[:, s, :].rearrange("p (x d k e) -> p x d k e", x=2, d=2, k=2)
                    for x, name in enumerate(("l0_gate_a_w", "l0_gate_x_w")):
                        for d in range(2):
                            sp.dma_start(dst[:, x, d], a[name][d, n].rearrange("(k p) e -> p k e", p=P)
                                         ).then_inc(raw_landed[s], 16)
                    return
                src = source(item, i)
                if item[0] == "pool":
                    dst = raw[:, s, :].rearrange("p (g k e) -> p g k e", g=4, k=2)
                elif item[0] == "down":
                    dst = raw[:, s, :].rearrange("p (k n) -> p k n", k=2)
                else:
                    dst = raw[:, s, :].rearrange("p (k n) -> p k n", k=KT)
                sp.dma_start(dst, src).then_inc(raw_landed[s], 16)

            for t in range(T // P):
                src = a["x_prompt"][0] if t == 0 else a["x_sample"][0, (t - 1) * P:t * P, :]
                sp.dma_start(x_stage[:, t, :], src).then_inc(x_landed[t], 16)
            for m in (0, 4, 1, 5, 2, 6, 3, 7):
                if m == 0:
                    for s in range(3):
                        sp.wait_ge(stage_landed[s], 16 * STAGE_DMAS[s])
                if m >= STAGED:
                    load(Q["mod", 0, m])
                else:
                    sp.dma_start(mod_stage[:, m, :].rearrange("p (k n) -> p k n", k=KT), source(("mod", 0, m))
                                 ).then_inc(mod_landed[m], 16)
            q = FIRST_MODS - STAGED
            while q < len(STREAM):
                item = STREAM[q]
                if item[0] == "gate" and item[2] == 1:
                    per_block = 6 if item[1] == 0 else 3
                    with sp.Fori(0, LOOPS) as i:
                        for c in range(2 * per_block):
                            load(q + c, i, 6, 12)
                    q += 2 * per_block * LOOPS
                    continue
                load(q)
                q += 1
                if item == ("w_out", 3):
                    sp.wait_ge(states_out, 1)
                    sp.dma_start(outs[2].rearrange("b s (k p) -> (b s k) p", p=P), states_t[:, :]
                                 ).then_inc(states_stored, 16)
            for t in range(T // P):
                sp.wait_ge(t_freed, 2 * (t + 1))
                dst = outs[0][0] if t == 0 else outs[1][0, (t - 1) * P:t * P, :]
                sp.dma_start(dst, y_stage[:, t % 4, :]).then_inc(y_stored[t % 4], 16)
            for i in range(4):
                sp.wait_ge(y_stored[i], 16 * len(range(i, T // P, 4)))
            sp.wait_ge(states_stored, 16)

        @block.tensor
        def _(pe):
            def parts(w, x):
                return (w[0], x[0]), (w[0], x[1]), (w[1], x[0])

            def product(out, weights, moving, ks, between={}):
                last = None
                steps = [(k, part) for k in ks for part in range(3)]
                for n, (k, part) in enumerate(steps):
                    if part == 0 and k in between:
                        for step in between[k]:
                            step()
                    w, x = parts(weights(k), moving(k))[part]
                    last = pe.matmul(out, w, x, start=n == 0, stop=n == len(steps) - 1)
                return last

            def as_split(n):
                def wait(part):
                    return lambda: pe.wait_ge(mv_ready, 4 * n + part + 1)

                return {2 * part: [wait(part)] for part in range(4)}

            def columns(w_slot, c, tile=None, kt=KT):
                def get(k):
                    v = [t[:, w_slot, :].rearrange("p (k n) -> p k n", k=kt) for t in (w_hi, w_lo)]
                    return [t[:, k, c * P:(c + 1) * P] for t in v]
                return get

            def moving_of(hi, lo, g):
                return lambda k: [t[:, k, g * GT:(g + 1) * GT] for t in (hi, lo)]

            def mod_direct(m):
                pe.wait_ge(mod_landed[m], 16)
                for c in range(2):
                    col = 4 * m + 2 * c
                    for k in range(KT):
                        last = pe.matmul(bank[MOD_BANK][:, col:col + 2],
                                         mod_stage[:, m, k * 2 * P + c * P:k * 2 * P + (c + 1) * P],
                                         cond[:, k, :], start=k == 0, stop=k == KT - 1)
                last.then_inc(mod_done, 1)

            def mod_fold(m, i=None):
                item = next(x for x, n in MOD.items() if n == m)
                v = 2 * (m - DIRECT + 1)
                pe.wait_ge(mod_summed, v if i is None else i * 12 + v)
                for j in range(2):
                    for c in range(2):
                        col = P * item[1] + 4 * item[2] + 2 * j + c
                        if i is not None:
                            col = i * 24 + col
                        last = pe.matmul(bank[MOD_BANK][:, bass.ds(col, 1)], mod_sums(m)[:, c, j * P:(j + 1) * P],
                                         ones[:, 0:1], start=True, stop=True)
                last.then_inc(mod_done, 1)

            sums = [0]

            def norm_sum():
                n = sums[0]
                pe.wait_ge(acc_ready, n + 1)
                if n:
                    pe.wait_ge(rstd_used, n)
                for c in range(GT // P):
                    last = pe.matmul(bank[NORM_BANK][:, c:c + 1], acc[:, c * P:(c + 1) * P], ones[:, 0:1],
                                     start=True, stop=True)
                last.then_inc(sum_ready, 1)
                sums[0] += 1

            spreads = [0]

            def norm_spread():
                n = spreads[0]
                pe.wait_ge(diag_ready, n + 1)
                pe.matmul(bank[NORM_BANK][:, P:P + GT], ones[:, :], diag[:, :], start=True, stop=True
                          ).then_inc(spread_ready, 1)
                spreads[0] += 1

            def norm_both():
                norm_sum()
                norm_spread()

            def out_bank(n, i=None, per=0):
                free = bank_free(n)
                if free > 0:
                    pe.wait_ge(out_taken, free if i is None else i * per + free)
                return bank[out_bank_of(n)]

            def turn_x(t):
                pe.wait_ge(x_landed[t], 16)
                for half in range(2):
                    b = out_bank(2 * t + half)
                    for c in range(4):
                        k = 4 * half + c
                        last = pe.transpose(b[:, c * P:(c + 1) * P], x_stage[:, t, k * P:(k + 1) * P], ident)
                    last.then_inc(out_ready, 1)

            pe.wait_ge(const_landed, 16)
            for t in range(3):
                turn_x(t)
            for s, rows in enumerate((P, 72, 96)):
                pe.wait_ge(stage_landed[s], 16 * STAGE_DMAS[s])
                if s:
                    pe.wait_ge(vec_ready, s)
                pe.transpose(bank[NORM_BANK][:, 0:rows], stage[0:rows, s, :], const[0:rows, 0:rows]
                             ).then_inc(rows_turned, 1)
            for t in range(3, T // P):
                turn_x(t)
            pe.wait_ge(cond_ready, 1)
            pe.wait_ge(ones_ready, 1)
            mod_direct(0)
            norm_both()
            mod_direct(1)
            norm_both()
            mod_direct(2)
            norm_both()
            mod_fold(4)
            mod_direct(3)
            for m in range(5, FIRST_MODS):
                mod_fold(m)
            pe.wait_ge(out_taken, O_WOUT)

            folds = {("branch", 2, 1): 8, ("branch", 2, 2): 9,
                     ("branch", 3, 0): 10, ("branch", 3, 1): 11, ("branch", 3, 2): 12}
            for item in MIX_PHASES:
                kind, n = item
                w = WEIGHT[item]
                pe.wait_ge(w_ready, w + 1)
                p = P_START[item]
                if kind == "gates":
                    pe.wait_ge(u_ready, 2 * (n + 1))
                    for j in range(2):
                        for d in range(2):
                            for x in range(2):
                                for g in range(NG):
                                    pe.wait_ge(p_freed, p - 3)
                                    product(bank[p % 4][:, 0:GT],
                                            lambda k, c=(x * 2 + d) * 2: [
                                                t[:, slot(w), (c + k) * 2 * P + j * P:(c + k) * 2 * P + (j + 1) * P]
                                                for t in (w_hi, w_lo)],
                                            moving_of(u_hi, u_lo, g), range(2)).then_inc(p_ready, 1)
                                    p += 1
                    continue
                for g in range(NG):
                    if (kind, n, g) in folds:
                        mod_fold(folds[kind, n, g])
                    for j in range(2):
                        if p >= 4:
                            pe.wait_ge(p_freed, p - 3)
                        product(bank[p % 4][:, 0:GT], columns(slot(w), j), moving_of(mv_hi, mv_lo, g), range(KT),
                                as_split(g) if item == ("rec", 0) and j == 0 else {}).then_inc(p_ready, 1)
                        p += 1
                if item == ("branch", 3):
                    pe.wait_ge(states_ready, 1)
                    pe.transpose(bank[NORM_BANK][0:16, 0:P], states[:, :], ident).then_inc(states_turned, 1)

            n = O_WOUT
            pe.wait_ge(p_freed, P_TOTAL)
            pe.wait_ge(states_out, 1)
            norms_at = {(1, 1, 5): {3: [norm_sum]}, (1, 1, 6): {0: [norm_spread]},
                        (1, 2, 4): {1: [norm_sum], 6: [norm_spread]},
                        (1, 2, 7): {1: [norm_sum], 6: [norm_spread]}}
            for c in range(2):
                for g in range(NG):
                    for m in range(4 * c, 4 * c + 4):
                        w = WEIGHT["w_out", m // 2]
                        pe.wait_ge(w_ready, w + 1)
                        product(out_bank(n)[:, 0:GT], columns(slot(w), m % 2), moving_of(mv_hi, mv_lo, g), range(KT),
                                as_split(NG + g) if (c, m) == (0, 0) else norms_at.get((c, g, m), {})
                                ).then_inc(out_ready, 1)
                        n += 1
                        done = n - O_WOUT
                        if done % 2 == 0 and 13 + done // 2 - 1 < 20:
                            mod_fold(13 + done // 2 - 1)

            def ffn_in(layer, b, g, j, i=None, gate_norms={}, up_norms={}):
                k = PAIRS[layer] + 6 * b + 2 * g + j
                wg, wu = WEIGHT["gate", layer, b], WEIGHT["up", layer, b]

                def at_round(v, per):
                    return v if i is None else i * per + v

                if g == 0 and j == 0:
                    pe.wait_ge(w_ready, at_round(wg + 1, 6))
                if k >= 2:
                    pe.wait_ge(silu_done, at_round(k - 1, 12))
                product(bank[2 * (k % 2)][:, 0:GT], columns(slot(wg), j), moving_of(mv_hi, mv_lo, g), range(KT),
                        gate_norms).then_inc(gate_ready, 1)
                if g == 0 and j == 0:
                    pe.wait_ge(w_ready, at_round(wu + 1, 6))
                if k >= 2:
                    pe.wait_ge(hid_ready, at_round(k - 1, 12))
                product(bank[2 * (k % 2) + 1][:, 0:GT], columns(slot(wu), j), moving_of(mv_hi, mv_lo, g), range(KT),
                        up_norms).then_inc(pair_ready, 1)

            def ffn_out(layer, b, g, m, i=None):
                n = O_FFN[layer] + 24 * b + KT * g + m
                wd = WEIGHT["down", layer, b]

                def at_round(v, per):
                    return v if i is None else i * per + v

                if m == 0:
                    if g == 0:
                        pe.wait_ge(w_ready, at_round(wd + 1, 6))
                    pe.wait_ge(hid_split, at_round(PAIRS[layer] + 6 * b + 2 * g + 2, 12))
                product(out_bank(n, i, 48)[:, 0:GT], columns(slot(wd), m, kt=HB), moving_of(hid_hi, hid_lo, g),
                        range(HB)).then_inc(out_ready, 1)

            def ffn_block(layer, b, i=None):
                m0, count = block_mods(layer, b)
                for g in range(NG):
                    for j in range(HB):
                        ffn_in(layer, b, g, j, i)
                        nth = 2 * g + j - 3
                        if 0 <= nth < count:
                            mod_fold(m0 + nth, i)
                for g in range(NG):
                    for m in range(KT):
                        ffn_out(layer, b, g, m, i)

            def ffn_first(layer, split):
                norm = {0: [norm_sum], 5: [norm_spread]}
                pe.wait_ge(out_taken, O_FFN[layer] - 4)
                ffn_in(layer, 0, 0, 0, gate_norms=as_split(split), up_norms=norm)
                pe.wait_ge(out_taken, O_FFN[layer])
                ffn_in(layer, 0, 0, 1, up_norms=norm)
                ffn_in(layer, 0, 1, 0, gate_norms=as_split(split + 1))
                ffn_in(layer, 0, 1, 1, gate_norms=norm)
                ffn_in(layer, 0, 2, 0, gate_norms=as_split(split + 2))
                ffn_in(layer, 0, 2, 1)
                for g in range(NG):
                    for m in range(KT):
                        ffn_out(layer, 0, g, m)
                    if layer == 0 and g < 2:
                        mod_fold(20 + g)

            def ffn_rest(layer):
                with pe.Fori(0, LOOPS) as i:
                    ffn_block(layer, 1, i)
                    ffn_block(layer, 2, i)
                ffn_block(layer, NB - 2)

            ffn_first(0, 2 * NG)
            ffn_rest(0)

            for g in range(NG):
                for j in range(HB):
                    ffn_in(0, NB - 1, g, j)

            def two_groups(out):
                for m in range(KT):
                    out(0, m)
                for m in range(3):
                    out(1, m)
                norm_sum()
                for m in range(3, 5):
                    out(1, m)
                norm_spread()
                for m in range(5, KT):
                    out(1, m)

            pe.wait_ge(hid_split, PAIRS[0] + 6 * NB)
            two_groups(lambda g, m: ffn_out(0, NB - 1, g, m))
            norm_both()
            for m in range(KT):
                ffn_out(0, NB - 1, 2, m)
            for g in range(1, NG):
                norm_both()
                norm_both()

            w = WEIGHT["pool",]
            pe.wait_ge(w_ready, w + 1)
            pe.wait_ge(pool_ready_d, len(POOL_D))
            pe.wait_ge(pool_ready_g, len(POOL_G))

            def pool_out(g, m):
                gi, j = m // 2, m % 2
                product(out_bank(O_POOL + KT * g + m)[:, 0:GT],
                        lambda k: [t[:, slot(w), (gi * 2 + k) * 2 * P + j * P:(gi * 2 + k) * 2 * P + (j + 1) * P]
                                   for t in (w_hi, w_lo)],
                        lambda k: [t[:, 2 * gi + k, g * GT:(g + 1) * GT] for t in (mv_hi, mv_lo)],
                        range(2)).then_inc(out_ready, 1)

            two_groups(pool_out)
            norm_both()
            for m in range(KT):
                pool_out(2, m)
            norm_both()
            ffn_first(1, 3 * NG)
            ffn_rest(1)
            for g in range(NG):
                for j in range(HB):
                    ffn_in(1, NB - 1, g, j)
            pe.wait_ge(hid_split, PAIRS[1] + 6 * NB)

            def turn_y(g):
                pe.wait_ge(x_new, KT * (3 * NG + g + 1))
                for t in range(3 * g, 3 * g + 3):
                    for half in range(2):
                        n = 2 * t + half
                        if n >= 3:
                            pe.wait_ge(t_freed, n - 2)
                        b = bank[T_BANKS[n % 3]]
                        for c in range(4):
                            last = pe.transpose(b[:, c * P:(c + 1) * P], y[:, 4 * half + c, t * P:(t + 1) * P], ident)
                        last.then_inc(t_ready, 1)

            for m in range(KT):
                ffn_out(1, NB - 1, 0, m)
            for g in range(1, NG):
                for m in range(4):
                    ffn_out(1, NB - 1, g, m)
                norm_both()
                for m in range(4, KT):
                    ffn_out(1, NB - 1, g, m)
                turn_y(g - 1)
            norm_both()
            turn_y(NG - 1)

        @block.scalar
        def _(act):
            steps = [0]

            def link(ins):
                steps[0] += 1
                ins.then_inc(act_step, 1)
                act.wait_ge(act_step, steps[0])

            act.dma_start(const[:, :], consts[:, 0:NC]).then_inc(const_landed, 16)
            for s in range(3):
                for stage_of, row, src in STAGE_ROWS(a):
                    if stage_of == s:
                        act.dma_start(stage[row:row + src.shape[0], s, :], src).then_inc(stage_landed[s], 16)
                if s == 0:
                    act.dma_start(pos[:, :], consts[:, NC:NC + NPOS]).then_inc(pos_landed, 16)

            for s, (c0, rows) in enumerate(((0, P), (P, 72), (V_MODB, 96))):
                act.wait_ge(rows_turned, s + 1)
                act.activation(vec[:, c0:c0 + rows], bank[NORM_BANK][:, 0:rows], ACT.Copy).then_inc(vec_ready, 1)
            act.wait_ge(vec_ready, 3)
            link(act.activation(cond[:, :, LAT_C], vec[:, V_C:V_C + KT], ACT.Silu))
            act.activation(cond[:, :, CTX_C], vec[:, V_CCTX:V_CCTX + KT], ACT.Silu).then_inc(cond_ready, 1)
            act.wait_ge(lam_abs, 1)
            act.activation(lam[:, 1, :], lam[:, 0, :], ACT.Exp, scale=-1.0).then_inc(lam_exp, 1)

            def split_hi(w, i=None):
                item = next(x for x, n in WEIGHT.items() if n == w)
                q = Q[item]
                per_q = 96 if item[0] in ("gate", "up", "down") and item[1] == 0 else 48
                act.wait_ge(raw_landed[q % 2], LANDED[q] if i is None else i * per_q + LANDED[q])
                if w >= 3:
                    s, v = released(w - 3)
                    act.wait_ge(s, v if i is None else i * (12 if s is pair_ready else 48) + v)
                elif w == 0:
                    act.wait_ge(mod_done, done_count(STAGED - 1))
                act.activation(w_hi[:, slot(w), :], raw[:, q % 2, :], ACT.Copy).then_inc(w_hi_ready, 1)

            stats = [0]

            def norm_squares(g, sem_of, count):
                for m in range(KT):
                    act.wait_ge(sem_of, count(m))
                    act.activation(group(wide, g)[:, m], group(y, g)[:, m], ACT.Square).then_inc(squares, 1)

            def norm_root():
                n = stats[0]
                act.wait_ge(var_ready, n + 1)
                act.activation(var[:, :], var[:, :], ACT.Sqrt).then_inc(rstd_ready, 1)
                stats[0] += 1

            affines = [0]

            def norm_hi(g):
                for part in range(4):
                    affines[0] += 1
                    act.wait_ge(affine_ready, affines[0])
                    v = slice(2 * part, 2 * part + 2)
                    act.activation(group(mv_hi, g)[:, v], group(wide, g)[:, v], ACT.Copy).then_inc(mv_hi_done, 1)

            news = [0]

            def post_norm(g, taken):
                norm_squares(g, out_taken, lambda m: taken(g, m))
                norm_root()

            def pre_norm(g, split=True):
                norm_squares(g, x_new, lambda m, n=news[0]: KT * n + m + 1)
                news[0] += 1
                norm_root()
                if split:
                    norm_hi(g)

            for g in range(NG):
                norm_squares(g, out_taken, lambda m: 6 * (g + 1))
            for g in range(NG):
                norm_root()
            split_hi(0)
            act.wait_ge(out_ready, O_WOUT)
            for g in range(NG):
                norm_hi(g)

            def evacuate(item):
                kind, n = item
                p = P_START[item]
                if item == ("rec", 0):
                    act.wait_ge(pads_ready, 1)
                if kind == "rec" and n:
                    act.wait_ge(conv_done, 2 * n)
                if item == ("branch", 0):
                    act.wait_ge(conv_done, 8)
                if item == ("branch", 3):
                    act.wait_ge(scanned, 16)
                for g in range(NG):
                    if g == 2:
                        for w in NEXT_GRANULES[item]:
                            split_hi(w)
                    for j in range(2):
                        act.wait_ge(p_ready, p + 1)
                        src = bank[p % 4]
                        if kind == "branch":
                            act.activation(mixed[:, MIXED_AT[2 * n + j], g * GT:(g + 1) * GT], src[:, 0:GT],
                                           ACT.Gelu_apprx_tanh).then_inc(p_freed, 1)
                        elif g == 0:
                            act.activation(rec[:, j, CP:CP + CTX], src[:, 0:CTX], ACT.Copy)
                            act.activation(rec[:, j, LP:LP + GT - CTX], src[:, CTX:GT], ACT.Copy
                                           ).then_inc(p_freed, 1)
                        else:
                            c0 = LP + g * GT - CTX
                            act.activation(rec[:, j, c0:c0 + GT], src[:, 0:GT], ACT.Copy).then_inc(p_freed, 1)
                        p += 1

            def u_split_hi(n):
                for j in range(2):
                    act.wait_ge(conv_done, 2 * n + j + 1)
                    act.activation(u_hi[:, j, :], u[:, j, :], ACT.Copy).then_inc(u_hi_done, 1)

            def gates(n):
                p = P_START["gates", n]
                for j in range(2):
                    for d in range(2):
                        s = 4 * n + 2 * j + d
                        col = 8 * d + 2 * n + j
                        if s >= 2:
                            act.wait_ge(scanned, s - 1)
                        if d == 1 and s >= 2:
                            act.wait_ge(h_stored, 16 * (s // 2))
                        for dst, bias in ((lru_a, V_BA), (lru_i, V_BX)):
                            for g in range(NG):
                                act.wait_ge(p_ready, p + 1)
                                act.activation(dst[:, d, g * GT:(g + 1) * GT], bank[p % 4][:, 0:GT], ACT.Sigmoid,
                                               bias=vec[:, bias + col:bias + col + 1]).then_inc(p_freed, 1)
                                p += 1
                        if s == 0:
                            act.wait_ge(rate_ready, 1)
                        act.wait_ge(p_freed, p)
                        link(act.activation(lru_m[:, d, :], lru_a[:, d, :], ACT.Tanh,
                                            scale=half_rate[:, col:col + 1]))
                        act.activation(lru_a[:, d, :], lru_a[:, d, :], ACT.Exp,
                                       scale=neg_rate[:, col:col + 1]).then_inc(gates_ready, 1)
                        act.activation(lru_m[:, d, :], lru_m[:, d, :], ACT.Sqrt).then_inc(gates_ready, 1)

            evacuate(("rec", 0))
            u_split_hi(0)
            evacuate(("rec", 1))
            for n in range(NLB):
                gates(n)
                if n < 3:
                    u_split_hi(n + 1)
                    evacuate(("rec", n + 2) if n < 2 else ("branch", 0))
            for n in range(1, 4):
                evacuate(("branch", n))
            act.wait_ge(states_turned, 1)
            act.activation(states_t[:, :], bank[NORM_BANK][0:16, 0:P], ACT.Copy).then_inc(states_out, 1)

            for g in range(NG):
                for t0, t1 in ((0, 2), (2, 8)):
                    act.wait_ge(mixed_ready, t1)
                    s0 = MIXED_AT[t0]
                    act.activation(group(mv_hi, g)[:, t0:t1], group(mixed, g)[:, s0:s0 + t1 - t0], ACT.Copy
                                   ).then_inc(mv_hi_done, 1)
            split_hi(WEIGHT["w_out", 2])
            split_hi(WEIGHT["w_out", 3])
            split_hi(WEIGHT["gate", 0, 0])

            def ffn_evacuate(layer, b, g, i=None, js=range(HB)):
                def at_round(v, per):
                    return v if i is None else i * per + v

                for j in js:
                    k = PAIRS[layer] + 6 * b + 2 * g + j
                    act.wait_ge(gate_ready, at_round(k + 1, 12))
                    if k >= 2:
                        act.wait_ge(hid_split, at_round(k - 1, 12))
                    act.activation(hid[:, k % 2, :], bank[2 * (k % 2)][:, 0:GT], ACT.Silu).then_inc(silu_done, 1)
                    act.wait_ge(hid_ready, at_round(k + 1, 12))
                    if b:
                        act.wait_ge(out_ready, at_round(O_FFN[layer] + 24 * (b - 1) + KT * (g + 1), 48))
                    act.activation(hid_hi[:, j, g * GT:(g + 1) * GT], hid[:, k % 2, :], ACT.Copy
                                   ).then_inc(hid_hi_done, 1)

            def ffn_block(layer, b, i=None, last=False):
                w = WEIGHT["gate", layer, b]
                split_hi(w + 2, i)
                for g in range(NG):
                    ffn_evacuate(layer, b, g, i)
                if w + 3 in WEIGHTS:
                    split_hi(w + 3, i)
                    split_hi(w + 4, i)

            def ffn_first(layer, taken):
                w = WEIGHT["gate", layer, 0]
                post_norm(0, taken)
                pre_norm(0)
                post_norm(1, taken)
                split_hi(w + 1)
                pre_norm(1)
                split_hi(w + 2)
                ffn_evacuate(layer, 0, 0, js=[0])
                post_norm(2, taken)
                ffn_evacuate(layer, 0, 0, js=[1])
                pre_norm(2)
                ffn_evacuate(layer, 0, 1)
                ffn_evacuate(layer, 0, 2)
                split_hi(w + 3)
                split_hi(w + 4)

            def ffn_rest(layer):
                with act.Fori(0, LOOPS) as i:
                    ffn_block(layer, 1, i)
                    ffn_block(layer, 2, i)
                ffn_block(layer, NB - 2)
                ffn_block(layer, NB - 1)

            ffn_first(0, lambda g, m: O_WOUT + 12 + 4 * (g + 1))
            ffn_rest(0)
            for g in range(NG):
                post_norm(g, lambda g, m: O_LAST[0] + KT * g + m + 1)
                pre_norm(g, split=False)
            affines[0] += 4 * NG
            def pool_source(i, tiles, buf, src, begun):
                if i < len(tiles):
                    if i:
                        act.wait_ge(begun, i)
                    k = tiles[i]
                    scale = 1.0 / WINDOWS[k // 2]
                    act.activation(buf[:, 0, PAD:PAD + CTX], wide[:, k, 0:CTX], ACT.Copy, scale=scale)
                    act.activation(buf[:, 0, 2 * PAD + CTX:2 * PAD + T], wide[:, k, CTX:T], ACT.Copy, scale=scale
                                   ).then_inc(src, 1)

            of_d = (POOL_D, pool_d, pool_src_d, pool_begun_d)
            of_g = (POOL_G, pool_g, pool_src_g, pool_begun_g)
            act.wait_ge(affine_ready, affines[0])
            act.wait_ge(pool_pads_d, 1)
            pool_source(0, *of_d)
            act.wait_ge(pool_pads_g, 1)
            pool_source(0, *of_g)
            for _, eng, i in sorted([(8 * i, "d", i) for i in range(len(POOL_D))] +
                                    [(12 * i, "g", i) for i in range(len(POOL_G))]):
                tiles, done, hi, of = ((POOL_D, pooled_d, pool_hi_d, of_d) if eng == "d" else
                                       (POOL_G, pooled_g, pool_hi_g, of_g))
                pool_source(i + 1, *of)
                act.wait_ge(done, i + 1)
                act.activation(mv_hi[:, tiles[i], :], y[:, tiles[i], :], ACT.Copy).then_inc(hi, 1)
            ffn_first(1, lambda g, m: O_POOL + KT * g + (m | 1) + 1)
            ffn_rest(1)
            act.wait_ge(w_ready, len(WEIGHTS))

            def take_turned(g):
                for t in range(3 * g, 3 * g + 3):
                    if t >= 4:
                        act.wait_ge(y_stored[t % 4], 16 * (t // 4))
                    for half in range(2):
                        n = 2 * t + half
                        act.wait_ge(t_ready, n + 1)
                        act.activation(y_stage[:, t % 4, 4 * half * P:4 * (half + 1) * P], bank[T_BANKS[n % 3]][:, :],
                                       ACT.Copy).then_inc(t_freed, 1)

            for g in range(NG):
                norm_squares(g, out_taken, lambda m: O_LAST[1] + KT * g + m + 1)
                if g:
                    take_turned(g - 1)
                norm_root()
            take_turned(NG - 1)

        @block.vector
        def _(dve):
            steps = [0]

            def link(ins):
                steps[0] += 1
                ins.then_inc(dve_step, 1)
                dve.wait_ge(dve_step, steps[0])

            dve.memset(ones[:, :], 1.0).then_inc(ones_ready, 1)

            def mod_take(layer, t0, t1, used):
                dve.wait_ge(mod_done, used)
                c0 = P * layer
                b0 = V_MODB + 48 * layer
                link(dve.tensor_tensor(
                    modv[:, layer, t0:t1, :],
                    bank[MOD_BANK][:, c0 + 2 * t0:c0 + 2 * t1].rearrange("p (t c) -> p t c", c=2),
                    vec[:, b0 + t0:b0 + t1].unsqueeze(2).to_broadcast([P, t1 - t0, 2]), ALU.add))

            def mod_sum(m, i=None):
                item = next(x for x, n in MOD.items() if n == m)
                n = m - DIRECT
                if m < STAGED:
                    dve.wait_ge(mod_landed[m], 16)
                    src = mod_stage[:, m, :]
                else:
                    q = Q[item]
                    dve.wait_ge(raw_landed[q % 2], LANDED[q] if i is None else i * 96 + LANDED[q])
                    src = raw[:, q % 2, :]
                if n >= 2:
                    dve.wait_ge(mod_done, done_count(m - 2) if i is None else i * 6 + done_count(m - 2))
                for k in range(KT):
                    for c in range(2):
                        dst, src_k = mod_sums(m)[:, c, :], src[:, k * 2 * P:(k + 1) * 2 * P]
                        if k == 0:
                            ins = dve.tensor_scalar(dst, src_k, cond[:, k, c:c + 1], None, ALU.mult)
                        else:
                            v = 2 * (KT - 1) * n + 2 * (k - 1) + c + 1
                            dve.wait_ge(mod_step, v if i is None else i * (12 * (KT - 1)) + v)
                            ins = dve.scalar_tensor_tensor(out=dst, in0=src_k, scalar=cond[:, k, c:c + 1], in1=dst,
                                                           op0=ALU.mult, op1=ALU.add)
                        ins.then_inc(mod_summed if k == KT - 1 else mod_step, 1)

            def gain(layer, which):
                c0 = V_GAIN + 32 * layer + which
                return vec[:, c0:c0 + KT].unsqueeze(2).to_broadcast([P, KT, 2])

            def scale_coef(layer, n, tile, which):
                link(dve.scalar_tensor_tensor(out=coef[:, layer, n], in0=modv[:, layer, tile:tile + KT, :], scalar=1.0,
                                              in1=gain(layer, which), op0=ALU.add, op1=ALU.mult))

            def gate_coef(layer, n, tile, which):
                link(dve.tensor_tensor(coef[:, layer, n], modv[:, layer, tile:tile + KT, :], gain(layer, which),
                                       ALU.mult))

            stats = [0]

            def norm_stats(g):
                n = stats[0]
                dve.wait_ge(sum_ready, n + 1)
                link(dve.tensor_scalar(var[:, :], bank[NORM_BANK][:, 0:GT // P], 1.0 / D, EPS, ALU.mult, ALU.add))
                dve.reciprocal(var[:, :], var[:, :]).then_inc(var_ready, 1)
                dve.wait_ge(rstd_ready, n + 1)
                if n:
                    dve.wait_ge(spread_ready, n)
                dve.tensor_tensor(diag[:, :].rearrange("p (c t) -> p c t", t=P),
                                  ident.unsqueeze(1).to_broadcast([P, GT // P, P]),
                                  var[:, :].unsqueeze(2).to_broadcast([P, GT // P, P]), ALU.mult).then_inc(diag_ready, 1)
                dve.wait_ge(spread_ready, n + 1)
                stats[0] += 1

            rstd = bank[NORM_BANK][:, P:P + GT]

            def mark(ins):
                steps[0] += 1
                ins.then_inc(dve_step, 1)
                return steps[0]

            def times_rstd(out, g, then=lambda m: None):
                done = None
                for m in range(KT + 1):
                    if m < KT:
                        ins = dve.tensor_tensor(group(out, g)[:, m], group(y, g)[:, m], rstd, ALU.mult)
                        if m == KT - 1:
                            ins.then_inc(rstd_used, 1)
                            after = None
                        else:
                            after = mark(ins)
                    if m:
                        if done is None:
                            dve.wait_ge(rstd_used, stats[0])
                        else:
                            dve.wait_ge(dve_step, done)
                        then(m - 1)
                    done = after

            loads = [0] * NG

            def post_norm(g, layer, n):
                norm_stats(g)
                loads[g] += 1
                dve.wait_ge(x_loaded[g], 16 * loads[g])

                def residual(k):
                    for t0, t1, c in segments(g):
                        ins = dve.scalar_tensor_tensor(out=y[:, k, t0:t1], in0=y[:, k, t0:t1],
                                                       scalar=coef[:, layer, n, k, c:c + 1], in1=x_old[:, k, t0:t1],
                                                       op0=ALU.mult, op1=ALU.add)
                    ins.then_inc(x_new, 1)

                times_rstd(y, g, residual)

            def affine(g, layer, n, shift, k):
                for t0, t1, c in segments(g):
                    ins = dve.tensor_scalar(wide[:, k, t0:t1], wide[:, k, t0:t1], coef[:, layer, n, k, c:c + 1],
                                            modv[:, layer, shift + k, c:c + 1], ALU.mult, ALU.add)
                if k % 2:
                    ins.then_inc(affine_ready, 1)

            def pre_norm(g, layer, n, shift):
                norm_stats(g)

                times_rstd(wide, g, lambda k: affine(g, layer, n, shift, k))

            def take_x(t):
                for half in range(2):
                    n = 2 * t + half
                    dve.wait_ge(out_ready, n + 1)
                    src = bank[out_bank_of(n)][:, :].rearrange("p (k t) -> p k t", k=4)
                    dst = y[:, 4 * half:4 * half + 4, t * P:(t + 1) * P]
                    if t == 0:
                        ins = dve.tensor_copy(dst, src)
                    elif half == 0:
                        if t == 1:
                            dve.wait_ge(pos_landed, 16)
                        rows = pos[:, 0:4 * GRID_H].rearrange("p (k r) -> p k r", k=4)
                        r0 = (t - 1) * P // GRID_W
                        for r in range(P // GRID_W):
                            v = slice(r * GRID_W, (r + 1) * GRID_W)
                            ins = dve.tensor_tensor(dst[:, :, v], src[:, :, v],
                                                    rows[:, :, r0 + r:r0 + r + 1].to_broadcast([P, 4, GRID_W]),
                                                    ALU.add)
                    else:
                        cols = pos[:, 4 * GRID_H:NPOS].rearrange("p (k c) -> p k c", k=4)
                        for r in range(P // GRID_W):
                            v = slice(r * GRID_W, (r + 1) * GRID_W)
                            ins = dve.tensor_tensor(dst[:, :, v], src[:, :, v], cols, ALU.add)
                    ins.then_inc(out_taken, 1)

            for t in range(3):
                take_x(t)
            dve.wait_ge(vec_ready, 3)
            lv = vec[:, V_LAM:V_LAM + 16]
            link(dve.tensor_scalar(lam[:, 2, :], lv, -1.0, None, ALU.mult))
            dve.tensor_tensor(lam[:, 0, :], lam[:, 2, :], lv, ALU.max).then_inc(lam_abs, 1)
            for t in range(3, T // P):
                take_x(t)
            dve.wait_ge(out_taken, O_WOUT)
            dve.wait_ge(cond_ready, 1)
            for g in range(NG):
                norm_stats(g)
                times_rstd(wide, g)
                mod_sum(DIRECT + g)
            mod_sum(FIRST_MODS - 1)
            mod_take(0, 0, 16, FIRST_MODS)
            scale_coef(0, 0, 8, G_MIXPRE)
            for g in range(NG):
                for k in range(KT):
                    affine(g, 0, 0, 0, k)
            dve.wait_ge(lam_exp, 1)
            z, s, s2, t = lam[:, 1, :], lam[:, 3, :], lam[:, 4, :], lam[:, 5, :]
            link(dve.tensor_scalar(s, z, 2.0, None, ALU.add))
            link(dve.reciprocal(s, s))
            link(dve.tensor_tensor(s, s, z, ALU.mult))
            link(dve.tensor_tensor(s2, s, s, ALU.mult))
            link(dve.tensor_scalar(t, s2, 1.0 / 17, 1.0 / 15, ALU.mult, ALU.add))
            for odd in (13, 11, 9, 7, 5, 3, 1):
                link(dve.tensor_tensor(t, t, s2, ALU.mult))
                link(dve.tensor_scalar(t, t, 1.0 / odd, None, ALU.add))
            link(dve.tensor_tensor(t, t, s, ALU.mult))
            link(dve.tensor_scalar(lam[:, 2, :], lam[:, 2, :], 0.0, 0.5, ALU.max, ALU.mult))
            link(dve.tensor_tensor(s, t, lam[:, 2, :], ALU.add))
            link(dve.tensor_scalar(neg_rate, s, -16.0, None, ALU.mult))
            dve.tensor_scalar(half_rate, s, 8.0, None, ALU.mult).then_inc(rate_ready, 1)


            for g in range(NG):
                dve.wait_ge(x_stored[g], 16)
            dve.memset(rec[:, :, :], 0.0).then_inc(pads_ready, 1)

            def conv(n, j):
                k = 2 * n + j
                dve.wait_ge(p_freed, P_START["rec", n] + 5 + j)
                if k >= 2:
                    dve.wait_ge(scanned, 4 * (n - 1) + 2 * j + 2)
                for seq, (t0, p0, size) in enumerate(((0, CP, CTX), (CTX, LP, LAT))):
                    dst = u[:, j, t0:t0 + size]

                    def tap(i):
                        return rec[:, j, p0 - 2 + i:p0 - 2 + i + size], vec[:, V_CONVW + 8 * i + k:V_CONVW + 8 * i + k + 1]

                    link(dve.tensor_scalar(dst, tap(0)[0], tap(0)[1], vec[:, V_CONVB + k:V_CONVB + k + 1],
                                           ALU.mult, ALU.add))
                    for i in range(1, 4):
                        ins = dve.scalar_tensor_tensor(out=dst, in0=tap(i)[0], scalar=tap(i)[1], in1=dst,
                                                       op0=ALU.mult, op1=ALU.add)
                        if (seq, i) == (1, 3):
                            ins.then_inc(conv_done, 1)
                        else:
                            link(ins)

            def lru_step(s):
                n, j, d = s // 4, s // 2 % 2, s % 2
                k = 2 * n + j
                dve.wait_ge(gates_ready, 2 * s + 2)
                av, iv, mv = lru_a[:, d, :], lru_i[:, d, :], lru_m[:, d, :]
                dve.scalar_tensor_tensor(out=mv, in0=av, scalar=1.0, in1=mv, op0=ALU.add, op1=ALU.mult)
                link(dve.tensor_tensor(iv, iv, u[:, j, :], ALU.mult))
                link(dve.tensor_tensor(mv, mv, iv, ALU.mult))
                dst = lru_f[:, :] if d == 0 else iv
                h0 = vec[:, V_STATE + 8 * d + k:V_STATE + 8 * d + k + 1]
                for (t0, t1), start in (((0, CTX), 0.0), ((CTX, T), h0)):
                    v = slice(t0, t1) if d == 0 else slice(t1 - 1, t0 - 1 if t0 else None, -1)
                    ins = dve.tensor_tensor_scan(dst[:, v], av[:, v], mv[:, v], start, ALU.mult, ALU.add)
                ins.then_inc(scanned, 1)
                dve.wait_ge(scanned, s + 1)
                col = 8 * d + k
                end = CTX - 1 if d == 0 else 0
                ins = dve.tensor_copy(states[:, col:col + 1], dst[:, end:end + 1])
                if s == 15:
                    ins.then_inc(states_ready, 1)
                    dve.wait_ge(states_ready, 1)
                else:
                    link(ins)
                if d == 1:
                    dve.tensor_tensor(iv, lru_f[:, :], iv, ALU.add).then_inc(h_ready, 1)
                    dve.wait_ge(h_ready, k + 1)

            conv(0, 0)
            conv(0, 1)
            for n in range(NLB):
                for j in range(2):
                    lru_step(4 * n + 2 * j)
                    lru_step(4 * n + 2 * j + 1)
                    if n < NLB - 1:
                        conv(n + 1, j)

            for n in range(4):
                dve.wait_ge(h_loaded[n], 16)
                dve.wait_ge(p_freed, P_START["branch", n] + 6)
                for j in range(2):
                    k = MIXED_AT[2 * n + j]
                    dve.tensor_tensor(mixed[:, k, :], mixed[:, k, :], h_sum[:, 2 * (n % 3) + j, :], ALU.mult
                                      ).then_inc(mixed_ready, 1)
                for m in ((8, 9), (10, 11), (12,), (13, 14))[n]:
                    if m == 14:
                        dve.wait_ge(mixed_ready, KT)
                    mod_sum(m)

            def take_y(n, m, g):
                dve.wait_ge(out_ready, n + 1)
                dve.tensor_copy(y[:, m, g * GT:(g + 1) * GT], bank[out_bank_of(n)][:, 0:GT]).then_inc(out_taken, 1)

            def wout(c, g, ms=range(4)):
                for m in ms:
                    take_y(O_WOUT + 12 * c + 4 * g + m, 4 * c + m, g)

            def ffn_hidden(layer, b, g, i=None, js=range(HB)):
                def at_round(v, per):
                    return v if i is None else i * per + v

                for j in js:
                    k = PAIRS[layer] + 6 * b + 2 * g + j
                    dve.wait_ge(silu_done, at_round(k + 1, 12))
                    dve.wait_ge(pair_ready, at_round(k + 1, 12))
                    h = hid[:, k % 2, :]
                    dve.tensor_tensor(h, h, bank[2 * (k % 2) + 1][:, 0:GT], ALU.mult).then_inc(hid_ready, 1)
                    dve.wait_ge(hid_hi_done, at_round(k + 1, 12))
                    v = slice(g * GT, (g + 1) * GT)
                    dve.tensor_tensor(hid_lo[:, j, v], h, hid_hi[:, j, v].bitcast(F32), ALU.subtract
                                      ).then_inc(hid_split, 1)

            def ffn_add(layer, b, g, i=None):
                def at_round(v, per):
                    return v if i is None else i * per + v

                for m in range(KT):
                    n = O_FFN[layer] + 24 * b + KT * g + m
                    dve.wait_ge(out_ready, at_round(n + 1, 48))
                    dst, src = y[:, m, g * GT:(g + 1) * GT], bank[out_bank_of(n)][:, 0:GT]
                    if b == 0:
                        if m == 0:
                            dve.wait_ge(x_stored[g], 16 * (2 if layer == 0 else 4))
                        dve.tensor_copy(dst, src).then_inc(out_taken, 1)
                    else:
                        dve.wait_ge(out_taken, at_round(n - 23, 48))
                        dve.tensor_tensor(dst, dst, src, ALU.add).then_inc(out_taken, 1)

            def ffn_block(layer, b, i=None):
                m0, count = block_mods(layer, b)
                for g in range(NG):
                    for j in range(HB):
                        ffn_hidden(layer, b, g, i, js=[j])
                        nth = 2 * g + j - 1
                        if 0 <= nth < count:
                            mod_sum(m0 + nth, i)
                for g in range(NG):
                    ffn_add(layer, b, g, i)

            def ffn(layer, taking):
                taking("post 0")
                post_norm(0, layer, 1)
                taking("pre 0")
                pre_norm(0, layer, 2, 24)
                taking("post 1")
                post_norm(1, layer, 1)
                taking("pre 1")
                pre_norm(1, layer, 2, 24)
                ffn_hidden(layer, 0, 0, js=[0])
                post_norm(2, layer, 1)
                ffn_hidden(layer, 0, 0, js=[1])
                pre_norm(2, layer, 2, 24)
                ffn_hidden(layer, 0, 1)
                if layer == 0:
                    mod_sum(20)
                ffn_hidden(layer, 0, 2)
                if layer == 0:
                    mod_sum(21)
                for g in range(NG):
                    ffn_add(layer, 0, g)
                with dve.Fori(0, LOOPS) as i:
                    ffn_block(layer, 1, i)
                    ffn_block(layer, 2, i)
                ffn_block(layer, NB - 2)
                for g in range(NG):
                    ffn_hidden(layer, NB - 1, g)

            for g in range(NG):
                for half in range(2):
                    wout(0, g, [2 * half, 2 * half + 1])
                    m = 15 + 2 * g + half
                    if m < 20:
                        mod_sum(m)

            def taking_wout(norm):
                if norm == "post 0":
                    wout(1, 0)
                    mod_take(0, 16, 40, 20)
                    gate_coef(0, 1, 16, G_MIXPOST)
                    scale_coef(0, 2, 32, G_FFNPRE)
                elif norm == "pre 0":
                    wout(1, 1, [0, 1])
                elif norm == "post 1":
                    wout(1, 1, [2, 3])
                elif norm == "pre 1":
                    wout(1, 2)

            ffn(0, taking_wout)
            mod_take(0, 40, 48, 48)
            gate_coef(0, 3, 40, G_FFNPOST)
            mod_take(1, 0, 48, 48)
            scale_coef(1, 0, 8, G_MIXPRE)
            gate_coef(1, 1, 16, G_MIXPOST)
            scale_coef(1, 2, 32, G_FFNPRE)
            gate_coef(1, 3, 40, G_FFNPOST)
            ffn_add(0, NB - 1, 0)
            post_norm(0, 0, 3)
            ffn_add(0, NB - 1, 1)
            pre_norm(0, 1, 0, 0)
            ffn_add(0, NB - 1, 2)
            for g in range(1, NG):
                post_norm(g, 0, 3)
                pre_norm(g, 1, 0, 0)
            for g in range(NG):
                dve.wait_ge(x_stored[g], 16 * 3)

            def pool_split(i):
                k = POOL_D[i]
                dve.wait_ge(pool_hi_d, i + 1)
                dve.tensor_tensor(mv_lo[:, k, :], y[:, k, :], mv_hi[:, k, :].bitcast(F32), ALU.subtract
                                  ).then_inc(pool_ready_d, 1)

            dve.memset(pool_d[:, 0, :], 0.0).then_inc(pool_pads_d, 1)
            for i, k in enumerate(POOL_D):
                dve.wait_ge(pool_src_d, i + 1)
                pool_tile(dve, pool_d, wide, y, const, k, link, pool_begun_d, i + 1, pooled_d)
                if i:
                    pool_split(i - 1)
            pool_split(len(POOL_D) - 1)

            def take_pooled(g):
                for m in range(KT):
                    n = O_POOL + KT * g + m
                    dve.wait_ge(out_ready, n + 1)
                    dve.tensor_scalar(y[:, m, g * GT:(g + 1) * GT], bank[out_bank_of(n)][:, 0:GT],
                                      vec[:, V_POOLB + m:V_POOLB + m + 1], vec[:, V_PSCALE + m:V_PSCALE + m + 1],
                                      ALU.add, ALU.mult).then_inc(out_taken, 1)

            def taking_pooled(norm):
                if norm == "post 0":
                    take_pooled(0)
                elif norm == "pre 0":
                    take_pooled(1)
                elif norm == "post 1":
                    take_pooled(2)

            ffn(1, taking_pooled)
            ffn_add(1, NB - 1, 0)
            post_norm(0, 1, 3)
            ffn_add(1, NB - 1, 1)
            post_norm(1, 1, 3)
            ffn_add(1, NB - 1, 2)
            post_norm(2, 1, 3)

        @block.gpsimd
        def _(pool):
            steps = [0]

            def link(ins):
                steps[0] += 1
                ins.then_inc(pool_step, 1)
                pool.wait_ge(pool_step, steps[0])

            def split_lo(w, i=None):
                item = next(x for x, n in WEIGHT.items() if n == w)
                q = Q[item]
                pool.wait_ge(w_hi_ready, w + 1 if i is None else i * 6 + (w + 1))
                pool.tensor_tensor(w_lo[:, slot(w), :], raw[:, q % 2, :], w_hi[:, slot(w), :].bitcast(F32),
                                   ALU.subtract).then_inc(w_ready, 1)

            his = [0]

            sums = [0]

            def norm_acc(g):
                n = sums[0]
                for m in range(1, KT):
                    pool.wait_ge(squares, KT * n + m + 1)
                    if m == 1 and n:
                        pool.wait_ge(sum_ready, n)
                    ins = pool.tensor_tensor(acc[:, :], group(wide, g)[:, 0] if m == 1 else acc[:, :],
                                             group(wide, g)[:, m], ALU.add)
                    if m == KT - 1:
                        ins.then_inc(acc_ready, 1)
                    else:
                        link(ins)
                sums[0] += 1

            def norm_lo(g):
                for part in range(4):
                    his[0] += 1
                    pool.wait_ge(mv_hi_done, his[0])
                    v = slice(2 * part, 2 * part + 2)
                    pool.tensor_tensor(group(mv_lo, g)[:, v], group(wide, g)[:, v],
                                       group(mv_hi, g)[:, v].bitcast(F32), ALU.subtract).then_inc(mv_ready, 1)

            stores = [0] * NG
            news = [0]

            def store_x(g, first=False):
                if first:
                    pool.wait_ge(out_taken, 6 * (g + 1))
                else:
                    news[0] += KT
                    pool.wait_ge(x_new, news[0])
                pool.dma_start(group(scratch_x, g), group(y, g)).then_inc(x_stored[g], 16)
                stores[g] += 1

            def load_x(g, free):
                pool.wait_ge(x_stored[g], 16 * stores[g])
                pool.wait_ge(out_ready, free)
                pool.dma_start(group(x_old, g), group(scratch_x, g)).then_inc(x_loaded[g], 16)

            for g in range(NG):
                norm_acc(g)
                store_x(g, first=True)
            split_lo(0)
            for g in range(NG):
                norm_lo(g)

            def u_split_lo(n, j):
                pool.wait_ge(u_hi_done, 2 * n + j + 1)
                pool.tensor_tensor(u_lo[:, j, :], u[:, j, :], u_hi[:, j, :].bitcast(F32), ALU.subtract
                                   ).then_inc(u_ready, 1)

            def store_h(k):
                pool.wait_ge(h_ready, k + 1)
                pool.dma_start(scratch_h[:, k, :], lru_i[:, 1, :]).then_inc(h_stored, 16)

            def split_next(item):
                for w in NEXT_GRANULES[item]:
                    split_lo(w)

            split_next(("rec", 0))
            u_split_lo(0, 0)
            u_split_lo(0, 1)
            split_next(("rec", 1))
            for n in range(NLB):
                for j in range(2):
                    store_h(2 * n + j)
                    if n < NLB - 1:
                        u_split_lo(n + 1, j)
                if n < NLB - 1:
                    split_next(("rec", n + 2) if n < 2 else ("branch", 0))
            pool.wait_ge(h_stored, 16 * KT)
            pool.wait_ge(scanned, 16)
            for n in range(3):
                pool.dma_start(h_sum[:, 2 * n:2 * n + 2, :], scratch_h[:, 2 * n:2 * n + 2, :]).then_inc(h_loaded[n], 16)
            split_next(("branch", 1))
            split_next(("branch", 2))
            pool.wait_ge(mixed_ready, 2)
            pool.dma_start(h_sum[:, 0:2, :], scratch_h[:, 6:8, :]).then_inc(h_loaded[3], 16)
            split_next(("branch", 3))
            for g in range(NG):
                for t0, t1 in ((0, 2), (2, 8)):
                    his[0] += 1
                    pool.wait_ge(mv_hi_done, his[0])
                    s0 = MIXED_AT[t0]
                    ins = pool.tensor_tensor(group(mv_lo, g)[:, t0:t1], group(mixed, g)[:, s0:s0 + t1 - t0],
                                             group(mv_hi, g)[:, t0:t1].bitcast(F32), ALU.subtract)
                    ins.then_inc(mv_ready, (t1 - t0) // 2)
            split_lo(WEIGHT["w_out", 2])
            split_lo(WEIGHT["w_out", 3])
            split_lo(WEIGHT["gate", 0, 0])

            def ffn_first(layer, free):
                w = WEIGHT["gate", layer, 0]
                for g in range(NG):
                    load_x(g, free(g))
                    norm_acc(g)
                    if g == 1:
                        split_lo(w + 1)
                    norm_acc(g)
                    store_x(g)
                    norm_lo(g)
                    if g == 1:
                        split_lo(w + 2)
                split_lo(w + 3)
                split_lo(w + 4)

            def ffn_block(layer, b, i=None):
                w = WEIGHT["gate", layer, b]
                split_lo(w + 2, i)
                if w + 3 in WEIGHTS:
                    split_lo(w + 3, i)
                    split_lo(w + 4, i)

            def ffn_rest(layer):
                with pool.Fori(0, LOOPS) as i:
                    ffn_block(layer, 1, i)
                    ffn_block(layer, 2, i)
                ffn_block(layer, NB - 2)
                ffn_block(layer, NB - 1)

            ffn_first(0, lambda g: O_WOUT + 12 + 4 * (g + 1))
            ffn_rest(0)
            for g in range(NG):
                load_x(g, O_LAST[0] + KT * (g + 1))
                norm_acc(g)
                norm_acc(g)
                store_x(g)

            for g in range(NG):
                pool.wait_ge(x_stored[g], 16 * 3)
            pool.wait_ge(states_stored, 16)

            def pool_split(i):
                k = POOL_G[i]
                pool.wait_ge(pool_hi_g, i + 1)
                pool.tensor_tensor(mv_lo[:, k, :], y[:, k, :], mv_hi[:, k, :].bitcast(F32), ALU.subtract
                                   ).then_inc(pool_ready_g, 1)

            pool.memset(pool_g[:, 0, :], 0.0).then_inc(pool_pads_g, 1)
            for i, k in enumerate(POOL_G):
                pool.wait_ge(pool_src_g, i + 1)
                pool_tile(pool, pool_g, wide, y, const, k, link, pool_begun_g, i + 1, pooled_g)
                if i:
                    pool_split(i - 1)
            pool_split(len(POOL_G) - 1)
            ffn_first(1, lambda g: O_POOL + KT * (g + 1))
            ffn_rest(1)
            for g in range(NG):
                load_x(g, O_LAST[1] + KT * (g + 1))
                norm_acc(g)


NEXT_GRANULES = {("rec", 0): [1], ("rec", 1): [2, 3], ("rec", 2): [4, 5], ("rec", 3): [6, 7],
                 ("branch", 0): [8, 9], ("branch", 1): [10], ("branch", 2): [11, 12], ("branch", 3): [13]}
WEIGHTS = set(WEIGHT.values())
MIXED_AT = [6, 7, 0, 1, 2, 3, 4, 5]
POOL_D, POOL_G = (7, 6, 5, 3, 1), (4, 2, 0)


def pool_tile(eng, buf, h, out, const, k, link, begun, nth, done):
    w = WINDOWS[k // 2]
    c0, l0 = PAD, 2 * PAD + CTX
    src, dst, span, size = 0, 1, 1, PL
    if nth > 1:
        eng.wait_ge(done, nth - 1)
    while span < w:
        size -= span
        ins = eng.tensor_tensor(buf[:, dst, 0:size], buf[:, src, 0:size], buf[:, src, span:span + size], ALU.add)
        if src == 0:
            ins.then_inc(begun, 1)
            eng.wait_ge(begun, nth)
        else:
            link(ins)
        src, dst, span = dst, 3 - dst if src else 2, span * 2
    e0 = C_EDGE + sum(a + b for v, a, b in EDGES if v < w)
    left, right = w // 2, w // 2 - 1
    for start, size in ((c0, CTX), (l0, LAT)):
        first = start - w // 2
        ins = eng.tensor_tensor(buf[:, src, first:first + left], buf[:, src, first:first + left],
                                const[:, e0:e0 + left], ALU.mult)
        if right:
            ins = eng.tensor_tensor(buf[:, src, first + size - right:first + size],
                                    buf[:, src, first + size - right:first + size],
                                    const[:, e0 + left:e0 + left + right], ALU.mult)
    link(ins)
    for start, t0, size in ((c0, 0, CTX), (l0, CTX, LAT)):
        first = start - w // 2
        ins = eng.tensor_tensor(out[:, k, t0:t0 + size], buf[:, src, first:first + size], h[:, k, t0:t0 + size],
                                ALU.subtract)
    ins.then_inc(done, 1)


def block_mods(layer, b):
    if layer == 1 or b == NB - 1:
        return 0, 0
    if b == 0:
        return 20, 2
    return (22 + 3 * (b - 1), 3) if b <= 2 * LOOPS else (22 + 6 * LOOPS, 2)


def STAGE_ROWS(a):
    rows = []
    for base, name in ((V_C, "c"), (V_CCTX, "c_ctx"), (V_CONVW, "l0_conv_w"), (V_CONVB, "l0_conv_b"),
                       (V_BA, "l0_gate_a_b"), (V_BX, "l0_gate_x_b"), (V_LAM, "l0_lambda"),
                       (V_STATE, "state_l0_rglru"), (V_POOLB, "l1_pool_b")):
        rows.append((0, base, name))
    for layer in range(2):
        for which, name in ((G_MIXPRE, "mix_pre_g"), (G_MIXPOST, "mix_post_g"), (G_FFNPRE, "ffn_pre_g"),
                            (G_FFNPOST, "ffn_post_g")):
            rows.append((1, V_GAIN - P + 32 * layer + which, f"l{layer}_{name}"))
    rows.append((1, V_PSCALE - P, "l1_pool_scale"))
    for layer in range(2):
        rows.append((2, 48 * layer, f"l{layer}_mod_b"))

    def flat(v):
        while len(v.shape) > 2:
            v = v.rearrange("a b c -> (a b) c")
        if len(v.shape) == 2:
            v = v.rearrange("a b -> (a b)")
        return v.rearrange("(r p) -> r p", p=P)

    return [(s, row, flat(a[name])) for s, row, name in rows]


STAGE_DMAS = (9, 9, 2)


def constants():
    quarter = D // 4
    omega = (1.0 / (10000.0 ** (np.arange(quarter, dtype=np.float32) / np.float32(quarter)))).astype(np.float32)

    def emb(n):
        ang = np.arange(n, dtype=np.float32)[:, None] * omega[None, :]
        e = np.concatenate([np.sin(ang), np.cos(ang)], axis=-1).astype(np.float32)
        return e.T.reshape(4, P, n).transpose(1, 0, 2).reshape(P, 4 * n)

    edge = []
    for w, left, right in EDGES:
        edge += [w / (w // 2 + t) for t in range(left)]
        edge += [w / (w - t) for t in range(1, right + 1)]
    out = np.concatenate([np.eye(P), np.tile(np.array(edge)[None], (P, 1)), emb(GRID_H), emb(GRID_W)], axis=1)
    return np.ascontiguousarray(out.astype(np.float32))


_INS = ['x_prompt', 'x_sample', 'state_l0_rglru', 'c', 'c_ctx', 'l0_mod_w', 'l0_mod_b', 'l0_mix_pre_g',
        'l0_mix_post_g', 'l0_w_in', 'l0_conv_w', 'l0_conv_b', 'l0_gate_a_w', 'l0_gate_a_b', 'l0_gate_x_w',
        'l0_gate_x_b', 'l0_lambda', 'l0_w_out', 'l0_ffn_pre_g', 'l0_ffn_post_g', 'l0_ffn_w_in', 'l0_ffn_w_out',
        'l1_mod_w', 'l1_mod_b', 'l1_mix_pre_g', 'l1_mix_post_g', 'l1_pool_w', 'l1_pool_b', 'l1_pool_scale',
        'l1_ffn_pre_g', 'l1_ffn_post_g', 'l1_ffn_w_in', 'l1_ffn_w_out']
_OUTS = [(1, CTX, D), (1, LAT, D), (1, 2, D)]


def kernel(**inputs):
    import concourse.bacc as _bacc
    from concourse.bass_utils import run_bass_kernel_spmd as _run

    nc = _bacc.Bacc("TRN2", target_bir_lowering=False, num_devices=1)
    arrays, aps = {}, {}
    for name in _INS:
        arrays[f"in_{name}"] = np.ascontiguousarray(inputs[name])
        aps[name] = nc.dram_tensor(f"in_{name}", arrays[f"in_{name}"].shape, F32, kind="ExternalInput").ap()
    arrays["in_constants"] = constants()
    consts = nc.dram_tensor("in_constants", arrays["in_constants"].shape, F32, kind="ExternalInput").ap()
    scratch_x = nc.dram_tensor("residual", [P, KT, T], F32).ap()
    scratch_h = nc.dram_tensor("recurrence", [P, KT, T], F32).ap()
    outs = [nc.dram_tensor(f"out_{i}", shape, F32, kind="ExternalOutput").ap() for i, shape in enumerate(_OUTS)]
    program(nc, aps, scratch_x, scratch_h, consts, outs)
    r = _run(nc, [arrays], core_ids=[0])
    return tuple(r.results[0][f"out_{i}"] for i in range(len(_OUTS)))
```

```python
from contextlib import ExitStack

import numpy as np

import concourse.bass as bass
from concourse import mybir

F32 = mybir.dt.float32
F32R = mybir.dt.float32r
ALU = mybir.AluOpType
ACT = mybir.ActivationFunctionType

P = 128
D = 1024
KT = D // P
CTX = 128
LAT = 1024
T = CTX + LAT
NG = 3
GT = T // NG
DFF = 2816
HB = 2
NB = DFF // (HB * P)
NLB = 4
GRID_W = 64
GRID_H = LAT // GRID_W
WINDOWS = (2, 4, 8, 16)
EPS = 1e-6
GC = 2048
PAD = 8
PL = 3 * PAD + T
CP, LP = 2, CTX + 5
RL = T + 8
CTX_C, LAT_C = 1, 0

V_C, V_CCTX, V_CONVW, V_CONVB, V_BA, V_BX, V_LAM, V_STATE, V_POOLB = 0, 8, 16, 48, 56, 72, 88, 104, 120
V_GAIN, V_PSCALE = 128, 192
V_MODB = 200
NV = 296
G_MIXPRE, G_MIXPOST, G_FFNPRE, G_FFNPOST = 0, 8, 16, 24

C_ID, C_EDGE = 0, P
EDGES = [(w, w // 2, w // 2 - 1) for w in WINDOWS]
NC = C_EDGE + sum(a + b for _, a, b in EDGES)
NPOS = 4 * GRID_H + 4 * GRID_W


LOOPS = (NB - 3) // 2
FIRST_MODS = 8
DIRECT = 5
STAGED = 6
MOD_TURNS = [0, 1, 2, 3, 5, 4, 6, 7]


def stream_order():
    def mods(layer, m0, m1):
        return [("mod", layer, m) for m in range(m0, m1)]

    order = mods(0, STAGED, FIRST_MODS)
    order += MIX_PHASES[:-1] + mods(0, 8, 10) + MIX_PHASES[-1:]
    order += [("w_out", 0)] + mods(0, 10, 12) + [("w_out", 1)] + mods(0, 12, 14) + [("w_out", 2)]
    order += mods(0, 14, 20) + [("w_out", 3)]
    for b in range(NB):
        order += [("gate", 0, b), ("up", 0, b), ("down", 0, b)]
        if b == 0:
            order += mods(0, 20, 22)
        elif b <= 2 * LOOPS:
            order += mods(1, 3 * (b - 1), 3 * b)
        elif b == NB - 2:
            order += mods(0, 22, 24)
    order.append(("pool",))
    for b in range(NB):
        order += [("gate", 1, b), ("up", 1, b), ("down", 1, b)]
    return order


MIX_PHASES = [("rec", 0), ("rec", 1), ("gates", 0), ("rec", 2), ("gates", 1), ("rec", 3), ("gates", 2),
              ("branch", 0), ("gates", 3), ("branch", 1), ("branch", 2), ("branch", 3)]
STREAM = stream_order()
Q = {item: q for q, item in enumerate(STREAM)}
WEIGHT = {item: w for w, item in enumerate(i for i in STREAM if i[0] != "mod")}
MOD = {item: STAGED + m for m, item in enumerate(i for i in STREAM if i[0] == "mod")}
MOD.update({("mod", 0, m): m for m in range(STAGED)})


def landed_values():
    count, out = [0, 0], []
    for q, item in enumerate(STREAM):
        count[q % 2] += 64 if item[0] == "gates" else 16
        out.append(count[q % 2])
    return out


LANDED = landed_values()

P_START = {}
_n = 0
for _item in MIX_PHASES:
    P_START[_item] = _n
    _n += 24 if _item[0] == "gates" else 6
P_TOTAL = _n
P_BANKS = 6
O_XIN = 0
O_WOUT = O_XIN + 2 * T // P
O_FFN = [O_WOUT + 24, 0]
O_POOL = O_FFN[0] + 24 * NB
O_FFN[1] = O_POOL + 24
O_LAST = [start + 24 * (NB - 1) for start in O_FFN]
PAIRS = [0, 6 * NB]


def out_bank_of(n):
    if n >= O_LAST[1]:
        return n % 4
    beside = any(start <= n < last for start, last in zip(O_FFN, O_LAST))
    return 4 + n % 2 if beside else n % 6


def phase_start(n):
    return max(start for start in (O_XIN, O_WOUT, O_FFN[0], O_LAST[0], O_POOL, O_FFN[1], O_LAST[1]) if start <= n)


def bank_free(n):
    last = next((v for v in range(n - 1, phase_start(n) - 1, -1) if out_bank_of(v) == out_bank_of(n)), -1)
    return max(last + 1, phase_start(n))


def program(nc, a, scratch_x, scratch_h, consts, outs):
    ctx = ExitStack()
    at = [(nc.sbuf_base + 31) // 32 * 32]

    def place(name, shape, dt, offset):
        return nc.alloc_sbuf_tensor_at(name, shape, dt, offset=offset)

    def region(nbytes):
        here = at[0]
        at[0] += (nbytes + 31) // 32 * 32
        return here

    r_raw = region(2 * GC * 4)
    raw = place("raw", [P, 2, GC], F32, r_raw)
    w_hi = place("w_hi", [P, 3, GC], F32R, at[0])
    mod_stage = place("mod_stage", [P, STAGED, GC], F32, region(3 * GC * 4))
    w_lo = place("w_lo", [P, 3, GC], F32R, region(3 * GC * 4))
    r_hi = region(KT * T * 4)
    r_lo = region(KT * T * 4)
    mv_hi = place("mv_hi", [P, KT, T], F32R, r_hi)
    mv_lo = place("mv_lo", [P, KT, T], F32R, r_lo)
    x_old = place("x_old", [P, KT, T], F32, r_hi)
    wide = place("wide", [P, KT, T], F32, r_lo)
    x_stage = place("x_stage", [P, T // P, D], F32, r_hi)
    r_y = region(6 * T * 4 + 2 * RL * 4)
    y = place("y", [P, KT, T], F32, r_y)
    mixed = place("mixed", [P, KT, T], F32, r_y)
    u_hi = place("u_hi", [P, 2, T], F32R, r_y)
    u_lo = place("u_lo", [P, 2, T], F32R, r_y + 2 * T * 4)
    u = place("u", [P, 2, T], F32, r_y + 4 * T * 4)
    rec = place("rec", [P, 2, RL], F32, r_y + 6 * T * 4)
    r_z = region(7 * T * 4)
    lru_a = place("lru_a", [P, 2, T], F32, r_z)
    lru_i = place("lru_i", [P, 2, T], F32, r_z + 2 * T * 4)
    lru_m = place("lru_m", [P, 2, T], F32, r_z + 4 * T * 4)
    lru_f = place("lru_f", [P, T], F32, r_z + 6 * T * 4)
    h_sum = place("h_sum", [P, 6, T], F32, r_z)
    hid_hi = place("hid_hi", [P, HB, T], F32R, r_z)
    hid_lo = place("hid_lo", [P, HB, T], F32R, r_z + HB * T * 4)
    hid = place("hid", [P, 2, GT], F32, r_z + 2 * HB * T * 4)
    stage = place("stage", [P, 3, P], F32, r_z)
    first_squares = place("first_squares", [P, KT, GT], F32, r_z)
    mod_sum_norms = place("mod_sum_norms", [P, 2, 2, 2 * P], F32, r_z + 2 * HB * T * 4 + 2 * GT * 4)
    mod_sum_branch = place("mod_sum_branch", [P, 2, 2, 2 * P], F32, r_z + 6 * T * 4 + P * 4)
    y_stage = place("y_stage", [P, 4, D], F32, r_raw)
    pool_d = place("pool_d", [P, 3, PL], F32, r_z)
    pool_g = place("pool_g", [P, 3, PL], F32, r_z + 3 * PL * 4)
    pos = place("pos", [P, NPOS], F32, r_z + 4 * D * 4)
    states_t = place("states_t", [16, P], F32, r_z + 6 * T * 4)
    acc = place("acc", [P, GT], F32, r_z + 7 * T * 4 - 2 * GT * 4)
    diag = place("diag", [P, GT], F32, r_z + 7 * T * 4 - GT * 4)
    const = place("const", [P, NC], F32, region(NC * 4))
    ones = place("ones", [P, P], F32, region(P * 4))
    vec = place("vec", [P, NV], F32, region(NV * 4))
    cond = place("cond", [P, KT, 2], F32, region(KT * 2 * 4))
    modv = place("modv", [P, 2, 48, 2], F32, region(2 * 96 * 4))
    coef = place("coef", [P, 2, 4, KT, 2], F32, region(2 * 4 * KT * 2 * 4))
    lam = place("lam", [P, 6, 16], F32, region(6 * 16 * 4))
    var = place("var", [P, GT // P], F32, region(GT // P * 4))
    states = place("states", [P, 16], F32, region(16 * 4))
    assert at[0] <= nc.sbuf_usable_end, at[0] - nc.sbuf_usable_end

    ident = const[:, C_ID:C_ID + P]
    neg_rate, half_rate = lam[:, 4, :], lam[:, 5, :]

    with ctx:
        bank = [ctx.enter_context(nc.psum_tensor(f"bank{i}", [P, 512], F32)) for i in range(8)]
        NORM_BANK, MOD_BANK, T_BANKS = 6, 7, (4, 5, 7)

        def sem(name):
            return ctx.enter_context(nc.semaphore(name))

        raw_landed = [sem("raw_landed0"), sem("raw_landed1")]
        stage_landed = [sem(f"stage_landed{s}") for s in range(3)]
        const_landed = sem("const_landed")
        pos_landed = sem("pos_landed")
        pads_ready = sem("pads_ready")
        x_landed = [sem(f"x_landed{t}") for t in range(T // P)]
        rows_turned = sem("rows_turned")
        vec_ready = sem("vec_ready")
        cond_ready = sem("cond_ready")
        ones_ready = sem("ones_ready")
        w_hi_ready = sem("w_hi_ready")
        w_ready = sem("w_ready")
        mod_landed = [sem(f"mod_landed{m}") for m in range(STAGED)]
        mod_step, mod_summed, mod_done = sem("mod_step"), sem("mod_summed"), sem("mod_done")
        lam_exp = sem("lam_exp")
        lam_abs = sem("lam_abs")
        rate_ready = sem("rate_ready")
        p_ready = sem("p_ready")
        p_freed = sem("p_freed")
        out_ready = sem("out_ready")
        out_taken = sem("out_taken")
        squares = sem("squares")
        acc_ready = sem("acc_ready")
        sum_ready = sem("sum_ready")
        var_ready = sem("var_ready")
        diag_ready = sem("diag_ready")
        spread_ready = sem("spread_ready")
        rstd_used = sem("rstd_used")
        t_ready, t_freed = sem("t_ready"), sem("t_freed")
        rstd_ready = sem("rstd_ready")
        x_new = sem("x_new")
        affine_ready = sem("affine_ready")
        product_ready, h_affine = sem("product_ready"), sem("h_affine")
        mv_hi_done = sem("mv_hi_done")
        mv_ready = sem("mv_ready")
        x_stored = [sem(f"x_stored{g}") for g in range(NG)]
        x_loaded = [sem(f"x_loaded{g}") for g in range(NG)]
        conv_done = sem("conv_done")
        u_hi_done = sem("u_hi_done")
        u_ready = sem("u_ready")
        gates_ready = sem("gates_ready")
        scanned = sem("scanned")
        h_ready = sem("h_ready")
        h_stored = sem("h_stored")
        h_loaded = [sem(f"h_loaded{n}") for n in range(4)]
        mixed_ready, mixed_last = sem("mixed_ready"), sem("mixed_last")
        gate_ready = sem("gate_ready")
        pair_ready = sem("pair_ready")
        silu_done = sem("silu_done")
        hid_ready = sem("hid_ready")
        hid_hi_done = sem("hid_hi_done")
        hid_split = sem("hid_split")
        pooled_d, pooled_g = sem("pooled_d"), sem("pooled_g")
        pool_src_d, pool_src_g = sem("pool_src_d"), sem("pool_src_g")
        pool_begun_d, pool_begun_g = sem("pool_begun_d"), sem("pool_begun_g")
        pool_pads_d, pool_pads_g = sem("pool_pads_d"), sem("pool_pads_g")
        pool_hi_d, pool_hi_g = sem("pool_hi_d"), sem("pool_hi_g")
        pool_ready_d, pool_ready_g = sem("pool_ready_d"), sem("pool_ready_g")
        y_stored = [sem(f"y_stored{i}") for i in range(4)]
        states_ready, states_turned, states_out = sem("states_ready"), sem("states_turned"), sem("states_out")
        states_stored = sem("states_stored")
        dve_step, act_step, pool_step = sem("dve_step"), sem("act_step"), sem("pool_step")

        def group(t, g):
            return t[:, :, g * GT:(g + 1) * GT]

        def segments(g):
            return [(0, CTX, CTX_C), (CTX, GT, LAT_C)] if g == 0 else [(g * GT, (g + 1) * GT, LAT_C)]

        def released(w):
            item = next(i for i, n in WEIGHT.items() if n == w)
            if item[0] in ("rec", "branch"):
                return p_ready, P_START[item] + 6
            if item[0] == "gates":
                return p_ready, P_START[item] + 24
            if item[0] == "w_out":
                return out_ready, O_WOUT + 12 * (item[1] // 2 + 1) - 2 * (1 - item[1] % 2)
            if item[0] == "pool":
                return out_ready, O_POOL + 24
            if item[0] in ("gate", "up"):
                return pair_ready, PAIRS[item[1]] + 6 * (item[2] + 1)
            return out_ready, O_FFN[item[1]] + 24 * (item[2] + 1)

        def slot(w):
            return w % 3

        def done_count(m):
            return (MOD_TURNS.index(m) if m < FIRST_MODS else m) + 1

        def mod_sums(m):
            return (mod_sum_branch if 8 <= m < 14 else mod_sum_norms)[:, (m - DIRECT) % 2]

        def norm_bank(n):
            return bank[MOD_BANK if LAST_NORMS <= n < LAST_NORMS + 2 * NG and (n - LAST_NORMS) % 2 else NORM_BANK]

        def norm_squares_of(g, first):
            return first_squares if first else group(wide, g)

        def grow(base, step, i, odd):
            return base + step * odd if i is None else base + step * odd + i * (2 * step)

        block = ctx.enter_context(nc.Block())

        @block.sync
        def _(sp):
            def source(item, b=None):
                kind = item[0]
                if kind == "mod":
                    c0 = 2 * P * item[2] if b is None else b * (6 * 2 * P) + 2 * P * item[2]
                    return a[f"l{item[1]}_mod_w"][:, bass.ds(c0, 2 * P)].rearrange("(k p) n -> p k n", p=P)
                if kind in ("rec", "branch"):
                    c0 = (D if kind == "rec" else 0) + 2 * P * item[1]
                    return a["l0_w_in"][:, c0:c0 + 2 * P].rearrange("(k p) n -> p k n", p=P)
                if kind == "w_out":
                    c0 = 2 * P * item[1]
                    return a["l0_w_out"][:, c0:c0 + 2 * P].rearrange("(k p) n -> p k n", p=P)
                if kind in ("gate", "up"):
                    c0 = (0 if kind == "gate" else DFF) + 2 * P * item[2]
                    c0 = c0 if b is None else b * (4 * P) + c0
                    return a[f"l{item[1]}_ffn_w_in"][:, bass.ds(c0, 2 * P)].rearrange("(k p) n -> p k n", p=P)
                if kind == "down":
                    r0 = 2 * P * item[2]
                    r0 = r0 if b is None else b * (4 * P) + r0
                    return a[f"l{item[1]}_ffn_w_out"][bass.ds(r0, 2 * P), :].rearrange("(k p) n -> p k n", p=P)
                return a["l1_pool_w"].rearrange("g (k p) e -> p g k e", p=P)

            def load(q, i=None, per_w=0, per_m=0):
                s = q % 2
                if q >= 2:
                    before = STREAM[q - 2]
                    if before[0] == "mod":
                        v = 2 * (MOD[before] - DIRECT + 1)
                        sp.wait_ge(mod_summed, v if i is None else i * per_m + v)
                    else:
                        sp.wait_ge(w_ready, WEIGHT[before] + 1 if i is None else i * per_w + (WEIGHT[before] + 1))
                item = STREAM[q]
                if item[0] == "gates":
                    n = item[1]
                    dst = raw[:, s, :].rearrange("p (x d k e) -> p x d k e", x=2, d=2, k=2)
                    for x, name in enumerate(("l0_gate_a_w", "l0_gate_x_w")):
                        for d in range(2):
                            sp.dma_start(dst[:, x, d], a[name][d, n].rearrange("(k p) e -> p k e", p=P)
                                         ).then_inc(raw_landed[s], 16)
                    return
                src = source(item, i)
                if item[0] == "pool":
                    dst = raw[:, s, :].rearrange("p (g k e) -> p g k e", g=4, k=2)
                elif item[0] == "down":
                    dst = raw[:, s, :].rearrange("p (k n) -> p k n", k=2)
                else:
                    dst = raw[:, s, :].rearrange("p (k n) -> p k n", k=KT)
                sp.dma_start(dst, src).then_inc(raw_landed[s], 16)

            for t in range(T // P):
                src = a["x_prompt"][0] if t == 0 else a["x_sample"][0, (t - 1) * P:t * P, :]
                sp.dma_start(x_stage[:, t, :], src).then_inc(x_landed[t], 16)
            for m in (0, 5, 1, 6, 2, 7, 3, 4):
                if m == 0:
                    for s in range(3):
                        sp.wait_ge(stage_landed[s], 16 * STAGE_DMAS[s])
                if m >= STAGED:
                    load(Q["mod", 0, m])
                else:
                    sp.dma_start(mod_stage[:, m, :].rearrange("p (k n) -> p k n", k=KT), source(("mod", 0, m))
                                 ).then_inc(mod_landed[m], 16)
            q = FIRST_MODS - STAGED
            while q < len(STREAM):
                item = STREAM[q]
                if item[0] == "gate" and item[2] == 1:
                    per_block = 6 if item[1] == 0 else 3
                    with sp.Fori(0, LOOPS) as i:
                        for c in range(2 * per_block):
                            load(q + c, i, 6, 12)
                    q += 2 * per_block * LOOPS
                    continue
                load(q)
                q += 1
                if item == ("w_out", 3):
                    sp.wait_ge(states_out, 1)
                    sp.dma_start(outs[2].rearrange("b s (k p) -> (b s k) p", p=P), states_t[:, :]
                                 ).then_inc(states_stored, 16)
            for t in range(T // P):
                sp.wait_ge(t_freed, 6 * (t // 3) + 4 + t % 3)
                dst = outs[0][0] if t == 0 else outs[1][0, (t - 1) * P:t * P, :]
                sp.dma_start(dst, y_stage[:, t % 4, :]).then_inc(y_stored[t % 4], 16)
            for i in range(4):
                sp.wait_ge(y_stored[i], 16 * len(range(i, T // P, 4)))
            sp.wait_ge(states_stored, 16)

        @block.tensor
        def _(pe):
            def parts(w, x):
                return (w[0], x[0]), (w[0], x[1]), (w[1], x[0])

            def product(out, weights, moving, ks, between={}):
                last = None
                steps = [(k, part) for k in ks for part in range(3)]
                for n, (k, part) in enumerate(steps):
                    if part == 0 and k in between:
                        for step in between[k]:
                            step()
                    w, x = parts(weights(k), moving(k))[part]
                    last = pe.matmul(out, w, x, start=n == 0, stop=n == len(steps) - 1)
                return last

            def as_split(n):
                def wait(part):
                    return lambda: pe.wait_ge(mv_ready, 4 * n + part + 1)

                return {2 * part: [wait(part)] for part in range(4)}

            def columns(w_slot, c, tile=None, kt=KT):
                def get(k):
                    v = [t[:, w_slot, :].rearrange("p (k n) -> p k n", k=kt) for t in (w_hi, w_lo)]
                    return [t[:, k, c * P:(c + 1) * P] for t in v]
                return get

            def moving_of(hi, lo, g):
                return lambda k: [t[:, k, g * GT:(g + 1) * GT] for t in (hi, lo)]

            def mod_direct(m, halves=(0, 1)):
                pe.wait_ge(mod_landed[m], 16)
                for c in halves:
                    col = 4 * m + 2 * c
                    for k in range(KT):
                        last = pe.matmul(bank[MOD_BANK][:, col:col + 2],
                                         mod_stage[:, m, k * 2 * P + c * P:k * 2 * P + (c + 1) * P],
                                         cond[:, k, :], start=k == 0, stop=k == KT - 1)
                if 1 in halves:
                    last.then_inc(mod_done, 1)

            def mod_fold(m, i=None):
                item = next(x for x, n in MOD.items() if n == m)
                v = 2 * (m - DIRECT + 1)
                pe.wait_ge(mod_summed, v if i is None else i * 12 + v)
                for j in range(2):
                    for c in range(2):
                        col = P * item[1] + 4 * item[2] + 2 * j + c
                        if i is not None:
                            col = i * 24 + col
                        last = pe.matmul(bank[MOD_BANK][:, bass.ds(col, 1)], mod_sums(m)[:, c, j * P:(j + 1) * P],
                                         ones[:, 0:1], start=True, stop=True)
                last.then_inc(mod_done, 1)

            sums = [0]

            def norm_sum():
                n = sums[0]
                pe.wait_ge(acc_ready, n + 1)
                if n:
                    pe.wait_ge(rstd_used, n - 1 if LAST_NORMS < n < LAST_NORMS + 2 * NG else n)
                for c in range(GT // P):
                    last = pe.matmul(norm_bank(n)[:, c:c + 1], acc[:, c * P:(c + 1) * P], ones[:, 0:1],
                                     start=True, stop=True)
                last.then_inc(sum_ready, 1)
                sums[0] += 1

            spreads = [0]

            def norm_spread():
                n = spreads[0]
                pe.wait_ge(diag_ready, n + 1)
                pe.matmul(norm_bank(n)[:, P:P + GT], ones[:, :], diag[:, :], start=True, stop=True
                          ).then_inc(spread_ready, 1)
                spreads[0] += 1

            def norm_both():
                norm_sum()
                norm_spread()

            def out_bank(n, i=None, per=0):
                free = bank_free(n)
                if free > 0:
                    pe.wait_ge(out_taken, free if i is None else i * per + free)
                return bank[out_bank_of(n)]

            def turn_x(t):
                pe.wait_ge(x_landed[t], 16)
                for half in range(2):
                    b = out_bank(2 * t + half)
                    for c in range(4):
                        k = 4 * half + c
                        last = pe.transpose(b[:, c * P:(c + 1) * P], x_stage[:, t, k * P:(k + 1) * P], ident)
                    last.then_inc(out_ready, 1)

            pe.wait_ge(const_landed, 16)
            for t in range(3):
                turn_x(t)
            for s, rows in enumerate((P, 72, 96)):
                pe.wait_ge(stage_landed[s], 16 * STAGE_DMAS[s])
                if s:
                    pe.wait_ge(vec_ready, s)
                pe.transpose(bank[NORM_BANK][:, 0:rows], stage[0:rows, s, :], const[0:rows, 0:rows]
                             ).then_inc(rows_turned, 1)
            for t in range(3, T // P):
                turn_x(t)
            pe.wait_ge(cond_ready, 1)
            pe.wait_ge(ones_ready, 1)
            mod_direct(0)
            for g in range(NG):
                norm_sum()
                mod_direct(g + 1, halves=(0,))
                norm_spread()
                mod_direct(g + 1, halves=(1,))
            mod_fold(5)
            mod_direct(4)
            mod_fold(6)
            mod_fold(7)
            pe.wait_ge(out_taken, O_WOUT)

            folds = {("branch", 2, 2): 8, ("branch", 3, 0): 9, ("branch", 3, 1): 10, ("branch", 3, 2): 11}
            for item in MIX_PHASES:
                kind, n = item
                w = WEIGHT[item]
                pe.wait_ge(w_ready, w + 1)
                p = P_START[item]
                if kind == "gates":
                    pe.wait_ge(u_ready, 2 * (n + 1))
                    for j in range(2):
                        for d in range(2):
                            for x in range(2):
                                for g in range(NG):
                                    pe.wait_ge(p_freed, p - P_BANKS + 1)
                                    product(bank[p % P_BANKS][:, 0:GT],
                                            lambda k, c=(x * 2 + d) * 2: [
                                                t[:, slot(w), (c + k) * 2 * P + j * P:(c + k) * 2 * P + (j + 1) * P]
                                                for t in (w_hi, w_lo)],
                                            moving_of(u_hi, u_lo, g), range(2)).then_inc(p_ready, 1)
                                    p += 1
                    continue
                for g in range(NG):
                    if (kind, n, g) in folds:
                        mod_fold(folds[kind, n, g])
                    for j in range(2):
                        if p >= P_BANKS:
                            pe.wait_ge(p_freed, p - P_BANKS + 1)
                        product(bank[p % P_BANKS][:, 0:GT], columns(slot(w), j), moving_of(mv_hi, mv_lo, g), range(KT),
                                as_split(g) if item == ("rec", 0) and j == 0 else {}).then_inc(p_ready, 1)
                        p += 1
                if item == ("branch", 3):
                    pe.wait_ge(states_ready, 1)
                    pe.transpose(bank[NORM_BANK][0:16, 0:P], states[:, :], ident).then_inc(states_turned, 1)

            n = O_WOUT
            pe.wait_ge(p_freed, P_TOTAL)
            pe.wait_ge(states_out, 1)
            norms_at = {(1, 1, 4): {6: [norm_sum]}, (1, 1, 5): {1: [norm_spread]},
                        (1, 2, 4): {2: [norm_sum], 6: [norm_spread]},
                        (1, 2, 6): {5: [norm_sum]}, (1, 2, 7): {1: [norm_spread]}}
            for c in range(2):
                for g in range(NG):
                    for m in range(4 * c, 4 * c + 4):
                        w = WEIGHT["w_out", m // 2]
                        pe.wait_ge(w_ready, w + 1)
                        product(out_bank(n)[:, 0:GT], columns(slot(w), m % 2), moving_of(mv_hi, mv_lo, g), range(KT),
                                as_split(NG + g) if (c, m) == (0, 0) else norms_at.get((c, g, m), {})
                                ).then_inc(out_ready, 1)
                        n += 1
                        done = n - O_WOUT
                        if done % 2 == 0 and 12 <= 11 + done // 2 < 20:
                            mod_fold(11 + done // 2)

            def ffn_in(layer, b, g, j, i=None, gate_norms={}, up_norms={}):
                k = PAIRS[layer] + 6 * b + 2 * g + j
                wg, wu = WEIGHT["gate", layer, b], WEIGHT["up", layer, b]

                def at_round(v, per):
                    return v if i is None else i * per + v

                if g == 0 and j == 0:
                    pe.wait_ge(w_ready, at_round(wg + 1, 6))
                if k >= 2:
                    pe.wait_ge(silu_done, at_round(k - 1, 12))
                product(bank[2 * (k % 2)][:, 0:GT], columns(slot(wg), j), moving_of(mv_hi, mv_lo, g), range(KT),
                        gate_norms).then_inc(gate_ready, 1)
                if g == 0 and j == 0:
                    pe.wait_ge(w_ready, at_round(wu + 1, 6))
                if k >= 2:
                    pe.wait_ge(hid_ready, at_round(k - 1, 12))
                product(bank[2 * (k % 2) + 1][:, 0:GT], columns(slot(wu), j), moving_of(mv_hi, mv_lo, g), range(KT),
                        up_norms).then_inc(pair_ready, 1)

            def ffn_out(layer, b, g, m, i=None):
                n = O_FFN[layer] + 24 * b + KT * g + m
                wd = WEIGHT["down", layer, b]

                def at_round(v, per):
                    return v if i is None else i * per + v

                if m == 0:
                    if g == 0:
                        pe.wait_ge(w_ready, at_round(wd + 1, 6))
                    pe.wait_ge(hid_split, at_round(PAIRS[layer] + 6 * b + 2 * g + 2, 12))
                product(out_bank(n, i, 48)[:, 0:GT], columns(slot(wd), m, kt=HB), moving_of(hid_hi, hid_lo, g),
                        range(HB)).then_inc(out_ready, 1)

            def ffn_block(layer, b, i=None):
                m0, count = block_mods(layer, b)
                for g in range(NG):
                    for j in range(HB):
                        ffn_in(layer, b, g, j, i)
                        nth = 2 * g + j - 3
                        if 0 <= nth < count:
                            mod_fold(m0 + nth, i)
                for g in range(NG):
                    for m in range(KT):
                        ffn_out(layer, b, g, m, i)

            def ffn_first(layer, split, up0={}, gate1={}, up1={}):
                pe.wait_ge(out_taken, O_FFN[layer] - 4)
                ffn_in(layer, 0, 0, 0, gate_norms=as_split(split), up_norms=up0)
                pe.wait_ge(out_taken, O_FFN[layer] - 2)
                ffn_in(layer, 0, 0, 1, gate_norms=gate1, up_norms=up1)
                norm_both()
                ffn_in(layer, 0, 1, 0, gate_norms=as_split(split + 1), up_norms={6: [norm_sum]})
                ffn_in(layer, 0, 1, 1, gate_norms={3: [norm_spread]})
                ffn_in(layer, 0, 2, 0, gate_norms=as_split(split + 2))
                ffn_in(layer, 0, 2, 1)
                for g in range(NG):
                    if layer == 0 and g:
                        mod_fold(19 + g)
                    for m in range(KT):
                        ffn_out(layer, 0, g, m)

            def ffn_rest(layer):
                with pe.Fori(0, LOOPS) as i:
                    ffn_block(layer, 1, i)
                    ffn_block(layer, 2, i)
                ffn_block(layer, NB - 2)

            ffn_first(0, 2 * NG, gate1={2: [norm_sum], 6: [norm_spread]})
            ffn_rest(0)

            for g in range(NG):
                for j in range(HB):
                    ffn_in(0, NB - 1, g, j)

            def outputs_and_norms(out):
                for m in range(KT):
                    out(0, m)
                for m in range(6):
                    out(1, m)
                norm_both()
                for m in range(6, KT):
                    out(1, m)
                for m in range(6):
                    out(2, m)
                norm_both()
                for m in range(6, KT):
                    out(2, m)

            pe.wait_ge(hid_split, PAIRS[0] + 6 * NB)
            outputs_and_norms(lambda g, m: ffn_out(0, NB - 1, g, m))
            for norm in range(4):
                norm_both()

            w = WEIGHT["pool",]
            pe.wait_ge(w_ready, w + 1)
            pe.wait_ge(pool_ready_d, len(POOL_D))
            pe.wait_ge(pool_ready_g, len(POOL_G))

            def pool_out(g, m):
                gi, j = m // 2, m % 2
                product(out_bank(O_POOL + KT * g + m)[:, 0:GT],
                        lambda k: [t[:, slot(w), (gi * 2 + k) * 2 * P + j * P:(gi * 2 + k) * 2 * P + (j + 1) * P]
                                   for t in (w_hi, w_lo)],
                        lambda k: [t[:, 2 * gi + k, g * GT:(g + 1) * GT] for t in (mv_hi, mv_lo)],
                        range(2)).then_inc(out_ready, 1)

            outputs_and_norms(pool_out)
            ffn_first(1, 3 * NG, up0={0: [norm_sum], 4: [norm_spread]}, up1={3: [norm_sum], 7: [norm_spread]})
            ffn_rest(1)
            for g in range(NG):
                for j in range(HB):
                    ffn_in(1, NB - 1, g, j)
            pe.wait_ge(hid_split, PAIRS[1] + 6 * NB)

            def turn_y(g):
                for half in range(2):
                    pe.wait_ge(x_new, KT * (3 * NG + g) + 4 * (half + 1))
                    for t in range(3 * g, 3 * g + 3):
                        n = 6 * g + 3 * half + t % 3
                        if n >= 3:
                            pe.wait_ge(t_freed, n - 2)
                        b = bank[T_BANKS[n % 3]]
                        for c in range(4):
                            last = pe.transpose(b[:, c * P:(c + 1) * P], y[:, 4 * half + c, t * P:(t + 1) * P], ident)
                        last.then_inc(t_ready, 1)

            def out_half(g, half):
                for m in range(4 * half, 4 * half + 4):
                    ffn_out(1, NB - 1, g, m)

            out_half(0, 0)
            out_half(0, 1)
            out_half(1, 0)
            norm_both()
            out_half(1, 1)
            out_half(2, 0)
            norm_both()
            turn_y(0)
            out_half(2, 1)
            norm_both()
            turn_y(1)
            turn_y(2)

        @block.scalar
        def _(act):
            steps = [0]

            def link(ins):
                steps[0] += 1
                ins.then_inc(act_step, 1)
                act.wait_ge(act_step, steps[0])

            act.dma_start(const[:, :], consts[:, 0:NC]).then_inc(const_landed, 16)
            for s in range(3):
                for stage_of, row, src in STAGE_ROWS(a):
                    if stage_of == s:
                        act.dma_start(stage[row:row + src.shape[0], s, :], src).then_inc(stage_landed[s], 16)
                if s == 0:
                    act.dma_start(pos[:, :], consts[:, NC:NC + NPOS]).then_inc(pos_landed, 16)

            for s, (c0, rows) in enumerate(((0, P), (P, 72), (V_MODB, 96))):
                act.wait_ge(rows_turned, s + 1)
                act.activation(vec[:, c0:c0 + rows], bank[NORM_BANK][:, 0:rows], ACT.Copy).then_inc(vec_ready, 1)
            act.wait_ge(vec_ready, 3)
            link(act.activation(cond[:, :, LAT_C], vec[:, V_C:V_C + KT], ACT.Silu))
            act.activation(cond[:, :, CTX_C], vec[:, V_CCTX:V_CCTX + KT], ACT.Silu).then_inc(cond_ready, 1)
            act.wait_ge(lam_abs, 1)
            act.activation(lam[:, 1, :], lam[:, 0, :], ACT.Exp, scale=-1.0).then_inc(lam_exp, 1)

            def split_hi(w, i=None):
                item = next(x for x, n in WEIGHT.items() if n == w)
                q = Q[item]
                per_q = 96 if item[0] in ("gate", "up", "down") and item[1] == 0 else 48
                act.wait_ge(raw_landed[q % 2], LANDED[q] if i is None else i * per_q + LANDED[q])
                if w >= 3:
                    s, v = released(w - 3)
                    act.wait_ge(s, v if i is None else i * (12 if s is pair_ready else 48) + v)
                else:
                    act.wait_ge(mod_done, max(done_count(w), done_count(w + 3)))
                act.activation(w_hi[:, slot(w), :], raw[:, q % 2, :], ACT.Copy).then_inc(w_hi_ready, 1)

            stats = [0]

            def norm_squares(g, sem_of, count, first=False):
                for m in range(KT):
                    act.wait_ge(sem_of, count(m))
                    act.activation(norm_squares_of(g, first)[:, m], group(y, g)[:, m], ACT.Square).then_inc(squares, 1)

            def norm_root():
                n = stats[0]
                act.wait_ge(var_ready, n + 1)
                act.activation(var[:, :], var[:, :], ACT.Sqrt).then_inc(rstd_ready, 1)
                stats[0] += 1

            affines = [0]

            def norm_hi(g):
                for part in range(4):
                    affines[0] += 1
                    act.wait_ge(affine_ready, affines[0])
                    v = slice(2 * part, 2 * part + 2)
                    act.activation(group(mv_hi, g)[:, v], group(wide, g)[:, v], ACT.Copy).then_inc(mv_hi_done, 1)

            news = [0]

            stores = [0] * NG

            def store_x(g):
                act.dma_start(group(scratch_x, g), group(y, g)).then_inc(x_stored[g], 16)
                stores[g] += 1

            def load_x(g, free, count):
                act.wait_ge(x_stored[g], 16 * stores[g])
                act.wait_ge(free, count)
                act.dma_start(group(x_old, g), group(scratch_x, g)).then_inc(x_loaded[g], 16)

            def new_squares(g):
                norm_squares(g, x_new, lambda m, n=news[0]: KT * n + m + 1)
                news[0] += 1
                store_x(g)

            def norm_hi_shifted(g, layer, shift):
                for k in range(KT):
                    affines[0] += 1
                    act.wait_ge(affine_ready, affines[0])
                    for t0, t1, c in segments(g):
                        ins = act.activation(mv_hi[:, k, t0:t1], wide[:, k, t0:t1], ACT.Identity,
                                             bias=modv[:, layer, shift + k, c:c + 1])
                    ins.then_inc(mv_hi_done, 1)

            for g in range(NG):
                norm_squares(g, out_taken, lambda m: 6 * (g + 1))
                store_x(g)
            for g in range(NG):
                norm_root()
            split_hi(0)
            act.wait_ge(out_ready, O_WOUT)
            for g in range(NG):
                norm_hi(g)

            def evacuate(item):
                kind, n = item
                p = P_START[item]
                if item == ("rec", 0):
                    act.wait_ge(pads_ready, 1)
                if kind == "rec" and n:
                    act.wait_ge(conv_done, 2 * n)
                if item == ("branch", 0):
                    act.wait_ge(conv_done, 8)
                if item == ("branch", 3):
                    act.wait_ge(scanned, 16)
                for g in range(NG):
                    if g == 2:
                        for w in NEXT_GRANULES[item]:
                            split_hi(w)
                    for j in range(2):
                        act.wait_ge(p_ready, p + 1)
                        src = bank[p % P_BANKS]
                        if kind == "branch":
                            act.activation(mixed[:, MIXED_AT[2 * n + j], g * GT:(g + 1) * GT], src[:, 0:GT],
                                           ACT.Gelu_apprx_tanh).then_inc(p_freed, 1)
                        elif g == 0:
                            act.activation(rec[:, j, CP:CP + CTX], src[:, 0:CTX], ACT.Copy)
                            act.activation(rec[:, j, LP:LP + GT - CTX], src[:, CTX:GT], ACT.Copy
                                           ).then_inc(p_freed, 1)
                        else:
                            c0 = LP + g * GT - CTX
                            act.activation(rec[:, j, c0:c0 + GT], src[:, 0:GT], ACT.Copy).then_inc(p_freed, 1)
                        p += 1
                    if (kind, n, g) == ("branch", 3, 1):
                        mixed_hi(0, 0)
                        mixed_hi(0, 1)

            def mixed_hi(g, part):
                t0, t1 = MIXED_PARTS[part]
                if part < 2:
                    act.wait_ge(mixed_ready, t1)
                elif g < NG - 1:
                    act.wait_ge(mixed_last, 2 * (g + 1))
                else:
                    act.wait_ge(mixed_ready, KT)
                if part == 0:
                    act.wait_ge(p_ready, P_START["branch", 3] + 2 * (g + 1))
                s0 = MIXED_AT[t0]
                act.activation(group(mv_hi, g)[:, t0:t1], group(mixed, g)[:, s0:s0 + t1 - t0], ACT.Copy
                               ).then_inc(mv_hi_done, 1)

            def u_split_hi(n):
                for j in range(2):
                    act.wait_ge(conv_done, 2 * n + j + 1)
                    act.activation(u_hi[:, j, :], u[:, j, :], ACT.Copy).then_inc(u_hi_done, 1)

            def gates(n):
                p = P_START["gates", n]
                for j in range(2):
                    for d in range(2):
                        s = 4 * n + 2 * j + d
                        col = 8 * d + 2 * n + j
                        if s >= 2:
                            act.wait_ge(scanned, s - 1)
                        if d == 1 and s >= 2:
                            act.wait_ge(h_stored, 16 * (s // 2))
                        for dst, bias in ((lru_a, V_BA), (lru_i, V_BX)):
                            for g in range(NG):
                                act.wait_ge(p_ready, p + 1)
                                act.activation(dst[:, d, g * GT:(g + 1) * GT], bank[p % P_BANKS][:, 0:GT], ACT.Sigmoid,
                                               bias=vec[:, bias + col:bias + col + 1]).then_inc(p_freed, 1)
                                p += 1
                        if s == 0:
                            act.wait_ge(rate_ready, 1)
                        act.wait_ge(p_freed, p)
                        link(act.activation(lru_m[:, d, :], lru_a[:, d, :], ACT.Tanh,
                                            scale=half_rate[:, col:col + 1]))
                        act.activation(lru_a[:, d, :], lru_a[:, d, :], ACT.Exp,
                                       scale=neg_rate[:, col:col + 1]).then_inc(gates_ready, 1)
                        act.activation(lru_m[:, d, :], lru_m[:, d, :], ACT.Sqrt).then_inc(gates_ready, 1)

            evacuate(("rec", 0))
            u_split_hi(0)
            evacuate(("rec", 1))
            for n in range(NLB):
                gates(n)
                if n < 3:
                    u_split_hi(n + 1)
                    evacuate(("rec", n + 2) if n < 2 else ("branch", 0))
            for n in range(1, 4):
                evacuate(("branch", n))
            mixed_hi(0, 2)
            act.wait_ge(states_turned, 1)
            act.activation(states_t[:, :], bank[NORM_BANK][0:16, 0:P], ACT.Copy).then_inc(states_out, 1)

            mixed_hi(1, 0)
            mixed_hi(1, 1)
            mixed_hi(1, 2)
            for part in range(3):
                mixed_hi(2, part)
            split_hi(WEIGHT["w_out", 2])
            split_hi(WEIGHT["w_out", 3])
            split_hi(WEIGHT["gate", 0, 0])

            def ffn_evacuate(layer, b, g, i=None, js=range(HB)):
                def at_round(v, per):
                    return v if i is None else i * per + v

                for j in js:
                    k = PAIRS[layer] + 6 * b + 2 * g + j
                    act.wait_ge(gate_ready, at_round(k + 1, 12))
                    if k >= 2:
                        act.wait_ge(hid_split, at_round(k - 1, 12))
                    act.activation(hid[:, k % 2, :], bank[2 * (k % 2)][:, 0:GT], ACT.Silu).then_inc(silu_done, 1)
                    act.wait_ge(hid_ready, at_round(k + 1, 12))
                    if b:
                        act.wait_ge(out_ready, at_round(O_FFN[layer] + 24 * (b - 1) + KT * (g + 1), 48))
                    act.activation(hid_hi[:, j, g * GT:(g + 1) * GT], hid[:, k % 2, :], ACT.Copy
                                   ).then_inc(hid_hi_done, 1)

            def ffn_block(layer, b, i=None, last=False):
                w = WEIGHT["gate", layer, b]
                split_hi(w + 2, i)
                for g in range(NG):
                    ffn_evacuate(layer, b, g, i)
                if w + 3 in WEIGHTS:
                    split_hi(w + 3, i)
                    split_hi(w + 4, i)

            def ffn_first(layer, taken, free):
                w = WEIGHT["gate", layer, 0]

                def post_squares(g):
                    load_x(g, out_ready, free(g))
                    norm_squares(g, out_taken, lambda m: taken(g, m))

                if layer == 0:
                    act.wait_ge(mixed_ready, KT)
                    norm_squares(0, out_taken, lambda m: O_WOUT + (m if m < 4 else 8 + m) + 1, first=True)
                    load_x(0, out_ready, free(0))
                else:
                    post_squares(0)
                norm_root()
                new_squares(0)
                post_squares(1)
                norm_root()
                norm_hi_shifted(0, layer, 24)
                split_hi(w + 1)
                norm_root()
                post_squares(2)
                new_squares(1)
                norm_root()
                ffn_evacuate(layer, 0, 0)
                new_squares(2)
                norm_root()
                norm_hi_shifted(1, layer, 24)
                split_hi(w + 2)
                ffn_evacuate(layer, 0, 1, js=[0])
                norm_root()
                norm_hi_shifted(2, layer, 24)
                ffn_evacuate(layer, 0, 1, js=[1])
                ffn_evacuate(layer, 0, 2)
                split_hi(w + 3)
                split_hi(w + 4)

            def ffn_rest(layer):
                with act.Fori(0, LOOPS) as i:
                    ffn_block(layer, 1, i)
                    ffn_block(layer, 2, i)
                ffn_block(layer, NB - 2)
                ffn_block(layer, NB - 1)

            ffn_first(0, lambda g, m: O_WOUT + 12 + 4 * (g + 1), lambda g: O_WOUT + 12 + 4 * (g + 1))
            ffn_rest(0)
            for g in range(NG):
                load_x(g, pair_ready, PAIRS[0] + 6 * NB)

            def last_squares(layer, g):
                norm_squares(g, out_taken, lambda m: O_LAST[layer] + KT * g + m + 1)

            def scale_shift(g, used):
                for k in range(KT):
                    if k == KT - 1:
                        act.wait_ge(rstd_used, used)
                    else:
                        act.wait_ge(product_ready, (KT - 1) * g + k + 1)
                    for t0, t1, c in segments(g):
                        ins = act.activation(wide[:, k, t0:t1], wide[:, k, t0:t1], ACT.Identity,
                                             bias=modv[:, 1, k, c:c + 1], scale=coef[:, 1, 0, k, c:c + 1])
                ins.then_inc(h_affine, 1)

            last_squares(0, 0)
            norm_root()
            new_squares(0)
            last_squares(0, 1)
            norm_root()
            scale_shift(0, LAST_NORMS + 2)
            last_squares(0, 2)
            norm_root()
            norm_root()
            new_squares(1)
            norm_root()
            new_squares(2)

            scale_shift(1, LAST_NORMS + 5)
            norm_root()
            scale_shift(2, LAST_NORMS + 6)
            def pool_source(i, tiles, buf, src, begun):
                if i < len(tiles):
                    if i:
                        act.wait_ge(begun, i)
                    k = tiles[i]
                    scale = 1.0 / WINDOWS[k // 2]
                    act.activation(buf[:, 0, PAD:PAD + CTX], wide[:, k, 0:CTX], ACT.Copy, scale=scale)
                    act.activation(buf[:, 0, 2 * PAD + CTX:2 * PAD + T], wide[:, k, CTX:T], ACT.Copy, scale=scale
                                   ).then_inc(src, 1)

            of_d = (POOL_D, pool_d, pool_src_d, pool_begun_d)
            of_g = (POOL_G, pool_g, pool_src_g, pool_begun_g)
            act.wait_ge(h_affine, NG)
            act.wait_ge(pool_pads_d, 1)
            pool_source(0, *of_d)
            act.wait_ge(pool_pads_g, 1)
            pool_source(0, *of_g)
            for _, eng, i in sorted([(8 * i, "d", i) for i in range(len(POOL_D))] +
                                    [(12 * i, "g", i) for i in range(len(POOL_G))]):
                tiles, done, hi, of = ((POOL_D, pooled_d, pool_hi_d, of_d) if eng == "d" else
                                       (POOL_G, pooled_g, pool_hi_g, of_g))
                pool_source(i + 1, *of)
                act.wait_ge(done, i + 1)
                act.activation(mv_hi[:, tiles[i], :], y[:, tiles[i], :], ACT.Copy).then_inc(hi, 1)
            ffn_first(1, lambda g, m: O_POOL + KT * g + (m | 1) + 1, lambda g: O_POOL + KT * (g + 1))
            ffn_rest(1)
            for g in range(NG):
                load_x(g, pair_ready, PAIRS[1] + 6 * NB)
            act.wait_ge(w_ready, len(WEIGHTS))

            def take_turned(g):
                for half in range(2):
                    for t in range(3 * g, 3 * g + 3):
                        if t >= 4 and half == 0:
                            act.wait_ge(y_stored[t % 4], 16 * (t // 4))
                        n = 6 * g + 3 * half + t % 3
                        act.wait_ge(t_ready, n + 1)
                        act.activation(y_stage[:, t % 4, 4 * half * P:4 * (half + 1) * P], bank[T_BANKS[n % 3]][:, :],
                                       ACT.Copy).then_inc(t_freed, 1)

            for g in range(NG):
                last_squares(1, g)
                norm_root()
                if g:
                    take_turned(g - 1)
            take_turned(NG - 1)

        @block.vector
        def _(dve):
            steps = [0]

            def link(ins):
                steps[0] += 1
                ins.then_inc(dve_step, 1)
                dve.wait_ge(dve_step, steps[0])

            dve.memset(ones[:, :], 1.0).then_inc(ones_ready, 1)

            def mod_take(layer, t0, t1, used):
                dve.wait_ge(mod_done, used)
                c0 = P * layer
                b0 = V_MODB + 48 * layer
                link(dve.tensor_tensor(
                    modv[:, layer, t0:t1, :],
                    bank[MOD_BANK][:, c0 + 2 * t0:c0 + 2 * t1].rearrange("p (t c) -> p t c", c=2),
                    vec[:, b0 + t0:b0 + t1].unsqueeze(2).to_broadcast([P, t1 - t0, 2]), ALU.add))

            def mod_sum(m, i=None):
                item = next(x for x, n in MOD.items() if n == m)
                n = m - DIRECT
                if m < STAGED:
                    dve.wait_ge(mod_landed[m], 16)
                    src = mod_stage[:, m, :]
                else:
                    q = Q[item]
                    dve.wait_ge(raw_landed[q % 2], LANDED[q] if i is None else i * 96 + LANDED[q])
                    src = raw[:, q % 2, :]
                if n >= 2:
                    dve.wait_ge(mod_done, done_count(m - 2) if i is None else i * 6 + done_count(m - 2))
                for k in range(KT):
                    for c in range(2):
                        dst, src_k = mod_sums(m)[:, c, :], src[:, k * 2 * P:(k + 1) * 2 * P]
                        if k == 0:
                            ins = dve.tensor_scalar(dst, src_k, cond[:, k, c:c + 1], None, ALU.mult)
                        else:
                            v = 2 * (KT - 1) * n + 2 * (k - 1) + c + 1
                            dve.wait_ge(mod_step, v if i is None else i * (12 * (KT - 1)) + v)
                            ins = dve.scalar_tensor_tensor(out=dst, in0=src_k, scalar=cond[:, k, c:c + 1], in1=dst,
                                                           op0=ALU.mult, op1=ALU.add)
                        ins.then_inc(mod_summed if k == KT - 1 else mod_step, 1)

            def gain(layer, which):
                c0 = V_GAIN + 32 * layer + which
                return vec[:, c0:c0 + KT].unsqueeze(2).to_broadcast([P, KT, 2])

            def scale_coef(layer, n, tile, which):
                link(dve.scalar_tensor_tensor(out=coef[:, layer, n], in0=modv[:, layer, tile:tile + KT, :], scalar=1.0,
                                              in1=gain(layer, which), op0=ALU.add, op1=ALU.mult))

            def gate_coef(layer, n, tile, which):
                link(dve.tensor_tensor(coef[:, layer, n], modv[:, layer, tile:tile + KT, :], gain(layer, which),
                                       ALU.mult))

            stats = [0]

            begun, diags = [0], [0]

            def norm_begin():
                n = begun[0]
                dve.wait_ge(sum_ready, n + 1)
                link(dve.tensor_scalar(var[:, :], norm_bank(n)[:, 0:GT // P], 1.0 / D, EPS, ALU.mult, ALU.add))
                dve.reciprocal(var[:, :], var[:, :]).then_inc(var_ready, 1)
                begun[0] += 1

            def norm_diag():
                n = diags[0]
                dve.wait_ge(rstd_ready, n + 1)
                if n:
                    dve.wait_ge(spread_ready, n)
                dve.tensor_tensor(diag[:, :].rearrange("p (c t) -> p c t", t=P),
                                  ident.unsqueeze(1).to_broadcast([P, GT // P, P]),
                                  var[:, :].unsqueeze(2).to_broadcast([P, GT // P, P]), ALU.mult).then_inc(diag_ready, 1)
                diags[0] += 1

            def norm_stats(g):
                n = stats[0]
                if begun[0] == n:
                    norm_begin()
                if diags[0] == n:
                    norm_diag()
                dve.wait_ge(spread_ready, n + 1)
                stats[0] += 1

            def rstd():
                return norm_bank(stats[0] - 1)[:, P:P + GT]

            def next_norm(m):
                if m == 5:
                    norm_begin()
                elif m == 7:
                    norm_diag()

            def mark(ins):
                steps[0] += 1
                ins.then_inc(dve_step, 1)
                return steps[0]

            def times_rstd(out, g, then=lambda m: None, ahead=False):
                done = None
                for m in range(KT + 1):
                    if ahead:
                        next_norm(m)
                    if m < KT:
                        ins = dve.tensor_tensor(group(out, g)[:, m], group(y, g)[:, m], rstd(), ALU.mult)
                        if m == KT - 1:
                            ins.then_inc(rstd_used, 1)
                            after = None
                        else:
                            after = mark(ins)
                    if m:
                        if done is None:
                            dve.wait_ge(rstd_used, stats[0])
                        else:
                            dve.wait_ge(dve_step, done)
                        then(m - 1)
                    done = after

            loads = [0] * NG

            def post_norm(g, layer, n, ahead=False):
                norm_stats(g)
                loads[g] += 1
                dve.wait_ge(x_loaded[g], 16 * loads[g])

                def residual(k):
                    for t0, t1, c in segments(g):
                        ins = dve.scalar_tensor_tensor(out=y[:, k, t0:t1], in0=y[:, k, t0:t1],
                                                       scalar=coef[:, layer, n, k, c:c + 1], in1=x_old[:, k, t0:t1],
                                                       op0=ALU.mult, op1=ALU.add)
                    ins.then_inc(x_new, 1)

                times_rstd(y, g, residual, ahead)

            def affine(g, layer, n, shift, k):
                for t0, t1, c in segments(g):
                    ins = dve.tensor_scalar(wide[:, k, t0:t1], wide[:, k, t0:t1], coef[:, layer, n, k, c:c + 1],
                                            modv[:, layer, shift + k, c:c + 1], ALU.mult, ALU.add)
                if k % 2:
                    ins.then_inc(affine_ready, 1)

            def norm_product(g, ahead=False):
                norm_stats(g)
                for m in range(KT):
                    if ahead:
                        next_norm(m)
                    ins = dve.tensor_tensor(group(wide, g)[:, m], group(y, g)[:, m], rstd(), ALU.mult)
                    ins.then_inc(rstd_used if m == KT - 1 else product_ready, 1)

            pre_splits = [0]

            def pre_norm_split(g, layer, n, shift):
                norm_stats(g)

                def lo(k):
                    dve.wait_ge(mv_hi_done, HI_BEFORE_FFN + KT * pre_splits[0] + k + 1)
                    for t0, t1, c in segments(g):
                        ins = dve.scalar_tensor_tensor(out=mv_lo[:, k, t0:t1], in0=wide[:, k, t0:t1],
                                                       scalar=modv[:, layer, shift + k, c:c + 1],
                                                       in1=mv_hi[:, k, t0:t1].bitcast(F32),
                                                       op0=ALU.add, op1=ALU.subtract)
                    if k % 2:
                        ins.then_inc(mv_ready, 1)
                    elif k == KT - SPLIT_LAG:
                        ins.then_inc(rstd_used, 1)

                for k in range(KT):
                    for t0, t1, c in segments(g):
                        ins = dve.scalar_tensor_tensor(out=wide[:, k, t0:t1], in0=y[:, k, t0:t1],
                                                       scalar=coef[:, layer, n, k, c:c + 1],
                                                       in1=rstd()[:, t0 - g * GT:t1 - g * GT],
                                                       op0=ALU.mult, op1=ALU.mult)
                    ins.then_inc(affine_ready, 1)
                    if k >= SPLIT_LAG - 1:
                        lo(k - SPLIT_LAG + 1)
                for k in range(KT - SPLIT_LAG + 1, KT):
                    lo(k)
                pre_splits[0] += 1

            def take_x(t):
                for half in range(2):
                    n = 2 * t + half
                    dve.wait_ge(out_ready, n + 1)
                    src = bank[out_bank_of(n)][:, :].rearrange("p (k t) -> p k t", k=4)
                    dst = y[:, 4 * half:4 * half + 4, t * P:(t + 1) * P]
                    if t == 0:
                        ins = dve.tensor_copy(dst, src)
                    elif half == 0:
                        if t == 1:
                            dve.wait_ge(pos_landed, 16)
                        rows = pos[:, 0:4 * GRID_H].rearrange("p (k r) -> p k r", k=4)
                        r0 = (t - 1) * P // GRID_W
                        for r in range(P // GRID_W):
                            v = slice(r * GRID_W, (r + 1) * GRID_W)
                            ins = dve.tensor_tensor(dst[:, :, v], src[:, :, v],
                                                    rows[:, :, r0 + r:r0 + r + 1].to_broadcast([P, 4, GRID_W]),
                                                    ALU.add)
                    else:
                        cols = pos[:, 4 * GRID_H:NPOS].rearrange("p (k c) -> p k c", k=4)
                        for r in range(P // GRID_W):
                            v = slice(r * GRID_W, (r + 1) * GRID_W)
                            ins = dve.tensor_tensor(dst[:, :, v], src[:, :, v], cols, ALU.add)
                    ins.then_inc(out_taken, 1)

            for t in range(3):
                take_x(t)
            dve.wait_ge(vec_ready, 3)
            lv = vec[:, V_LAM:V_LAM + 16]
            link(dve.tensor_scalar(lam[:, 2, :], lv, -1.0, None, ALU.mult))
            dve.tensor_tensor(lam[:, 0, :], lam[:, 2, :], lv, ALU.max).then_inc(lam_abs, 1)
            for t in range(3, T // P):
                take_x(t)
            dve.wait_ge(out_taken, O_WOUT)
            dve.wait_ge(cond_ready, 1)
            for g in range(NG):
                norm_stats(g)
                times_rstd(wide, g)
                mod_sum(DIRECT + g)
            mod_take(0, 0, 16, FIRST_MODS)
            scale_coef(0, 0, 8, G_MIXPRE)
            for g in range(NG):
                for k in range(KT):
                    affine(g, 0, 0, 0, k)
            dve.wait_ge(lam_exp, 1)
            z, s, s2, t = lam[:, 1, :], lam[:, 3, :], lam[:, 4, :], lam[:, 5, :]
            link(dve.tensor_scalar(s, z, 2.0, None, ALU.add))
            link(dve.reciprocal(s, s))
            link(dve.tensor_tensor(s, s, z, ALU.mult))
            link(dve.tensor_tensor(s2, s, s, ALU.mult))
            link(dve.tensor_scalar(t, s2, 1.0 / 17, 1.0 / 15, ALU.mult, ALU.add))
            for odd in (13, 11, 9, 7, 5, 3, 1):
                link(dve.tensor_tensor(t, t, s2, ALU.mult))
                link(dve.tensor_scalar(t, t, 1.0 / odd, None, ALU.add))
            link(dve.tensor_tensor(t, t, s, ALU.mult))
            link(dve.tensor_scalar(lam[:, 2, :], lam[:, 2, :], 0.0, 0.5, ALU.max, ALU.mult))
            link(dve.tensor_tensor(s, t, lam[:, 2, :], ALU.add))
            link(dve.tensor_scalar(neg_rate, s, -16.0, None, ALU.mult))
            dve.tensor_scalar(half_rate, s, 8.0, None, ALU.mult).then_inc(rate_ready, 1)


            for g in range(NG):
                dve.wait_ge(x_stored[g], 16)
            dve.memset(rec[:, :, :], 0.0).then_inc(pads_ready, 1)

            def conv(n, j):
                k = 2 * n + j
                dve.wait_ge(p_freed, P_START["rec", n] + 5 + j)
                for seq, (t0, p0, size) in enumerate(((0, CP, CTX), (CTX, LP, LAT))):
                    dst = u[:, j, t0:t0 + size]

                    def tap(i):
                        return rec[:, j, p0 - 2 + i:p0 - 2 + i + size], vec[:, V_CONVW + 8 * i + k:V_CONVW + 8 * i + k + 1]

                    link(dve.tensor_scalar(dst, tap(0)[0], tap(0)[1], vec[:, V_CONVB + k:V_CONVB + k + 1],
                                           ALU.mult, ALU.add))
                    for i in range(1, 4):
                        ins = dve.scalar_tensor_tensor(out=dst, in0=tap(i)[0], scalar=tap(i)[1], in1=dst,
                                                       op0=ALU.mult, op1=ALU.add)
                        if (seq, i) == (1, 3):
                            ins.then_inc(conv_done, 1)
                        else:
                            link(ins)

            def lru_input(s):
                n, j, d = s // 4, s // 2 % 2, s % 2
                dve.wait_ge(p_freed, P_START["gates", n] + 6 * (s % 4 + 1))
                link(dve.tensor_tensor(lru_i[:, d, :], lru_i[:, d, :], u[:, j, :], ALU.mult))

            def lru_step(s):
                n, j, d = s // 4, s // 2 % 2, s % 2
                k = 2 * n + j
                dve.wait_ge(gates_ready, 2 * s + 2)
                av, iv, mv = lru_a[:, d, :], lru_i[:, d, :], lru_m[:, d, :]
                link(dve.scalar_tensor_tensor(out=mv, in0=av, scalar=1.0, in1=mv, op0=ALU.add, op1=ALU.mult))
                link(dve.tensor_tensor(mv, mv, iv, ALU.mult))
                dst = lru_f[:, :] if d == 0 else iv
                h0 = vec[:, V_STATE + 8 * d + k:V_STATE + 8 * d + k + 1]
                for (t0, t1), start in (((0, CTX), 0.0), ((CTX, T), h0)):
                    v = slice(t0, t1) if d == 0 else slice(t1 - 1, t0 - 1 if t0 else None, -1)
                    ins = dve.tensor_tensor_scan(dst[:, v], av[:, v], mv[:, v], start, ALU.mult, ALU.add)
                ins.then_inc(scanned, 1)
                dve.wait_ge(scanned, s + 1)
                col = 8 * d + k
                end = CTX - 1 if d == 0 else 0
                ins = dve.tensor_copy(states[:, col:col + 1], dst[:, end:end + 1])
                if s == 15:
                    ins.then_inc(states_ready, 1)
                    dve.wait_ge(states_ready, 1)
                else:
                    link(ins)
                if d == 1:
                    dve.tensor_tensor(iv, lru_f[:, :], iv, ALU.add).then_inc(h_ready, 1)
                    dve.wait_ge(h_ready, k + 1)

            conv(0, 0)
            conv(0, 1)
            for n in range(NLB):
                for j in range(2):
                    s = 4 * n + 2 * j
                    lru_input(s)
                    lru_step(s)
                    lru_input(s + 1)
                    if n < NLB - 1:
                        conv(n + 1, j)
                    lru_step(s + 1)

            mod_sum(8)
            mod_sum(9)
            for n in range(3):
                dve.wait_ge(h_loaded[n], 16)
                dve.wait_ge(p_freed, P_START["branch", n] + 6)
                for j in range(2):
                    k = MIXED_AT[2 * n + j]
                    dve.tensor_tensor(mixed[:, k, :], mixed[:, k, :], h_sum[:, 2 * n + j, :], ALU.mult
                                      ).then_inc(mixed_ready, 1)
                for m in ((), (10, 11), (12,))[n]:
                    mod_sum(m)
            dve.wait_ge(h_loaded[3], 16)
            for g in range(NG):
                dve.wait_ge(p_freed, P_START["branch", 3] + 2 * (g + 1))
                for j in range(2):
                    v = slice(g * GT, (g + 1) * GT)
                    k = MIXED_AT[6 + j]
                    dve.tensor_tensor(mixed[:, k, v], mixed[:, k, v], h_sum[:, j, v], ALU.mult
                                      ).then_inc(mixed_ready if g == NG - 1 else mixed_last, 1)
            mod_sum(13)
            dve.wait_ge(mixed_ready, KT)
            mod_sum(14)

            def take_y(n, m, g):
                dve.wait_ge(out_ready, n + 1)
                dve.tensor_copy(y[:, m, g * GT:(g + 1) * GT], bank[out_bank_of(n)][:, 0:GT]).then_inc(out_taken, 1)

            def wout(c, g, ms=range(4)):
                for m in ms:
                    take_y(O_WOUT + 12 * c + 4 * g + m, 4 * c + m, g)

            def ffn_hidden(layer, b, g, i=None, js=range(HB)):
                def at_round(v, per):
                    return v if i is None else i * per + v

                for j in js:
                    k = PAIRS[layer] + 6 * b + 2 * g + j
                    dve.wait_ge(silu_done, at_round(k + 1, 12))
                    dve.wait_ge(pair_ready, at_round(k + 1, 12))
                    h = hid[:, k % 2, :]
                    dve.tensor_tensor(h, h, bank[2 * (k % 2) + 1][:, 0:GT], ALU.mult).then_inc(hid_ready, 1)
                    dve.wait_ge(hid_hi_done, at_round(k + 1, 12))
                    v = slice(g * GT, (g + 1) * GT)
                    dve.tensor_tensor(hid_lo[:, j, v], h, hid_hi[:, j, v].bitcast(F32), ALU.subtract
                                      ).then_inc(hid_split, 1)

            def ffn_add(layer, b, g, i=None, ms=range(KT)):
                def at_round(v, per):
                    return v if i is None else i * per + v

                for m in ms:
                    n = O_FFN[layer] + 24 * b + KT * g + m
                    dve.wait_ge(out_ready, at_round(n + 1, 48))
                    dst, src = y[:, m, g * GT:(g + 1) * GT], bank[out_bank_of(n)][:, 0:GT]
                    if b == 0:
                        if m == 0:
                            dve.wait_ge(x_stored[g], 16 * (2 if layer == 0 else 4))
                        dve.tensor_copy(dst, src).then_inc(out_taken, 1)
                    else:
                        dve.wait_ge(out_taken, at_round(n - 23, 48))
                        dve.tensor_tensor(dst, dst, src, ALU.add).then_inc(out_taken, 1)

            def ffn_block(layer, b, i=None):
                m0, count = block_mods(layer, b)
                for g in range(NG):
                    for j in range(HB):
                        ffn_hidden(layer, b, g, i, js=[j])
                        nth = 2 * g + j - 1
                        if 0 <= nth < count:
                            mod_sum(m0 + nth, i)
                for g in range(NG):
                    ffn_add(layer, b, g, i)

            def ffn(layer, taking):
                taking("post 0")
                post_norm(0, layer, 1)
                taking("pre 0")
                pre_norm_split(0, layer, 2, 24)
                taking("post 1")
                post_norm(1, layer, 1)
                taking("post 2")
                post_norm(2, layer, 1)
                ffn_hidden(layer, 0, 0)
                pre_norm_split(1, layer, 2, 24)
                ffn_hidden(layer, 0, 1, js=[0])
                pre_norm_split(2, layer, 2, 24)
                ffn_hidden(layer, 0, 1, js=[1])
                if layer == 0:
                    mod_sum(20)
                ffn_hidden(layer, 0, 2, js=[0])
                if layer == 0:
                    mod_sum(21)
                ffn_hidden(layer, 0, 2, js=[1])
                for g in range(NG):
                    ffn_add(layer, 0, g)
                with dve.Fori(0, LOOPS) as i:
                    ffn_block(layer, 1, i)
                    ffn_block(layer, 2, i)
                ffn_block(layer, NB - 2)
                for g in range(NG):
                    ffn_hidden(layer, NB - 1, g)

            for g in range(NG):
                for half in range(2):
                    wout(0, g, [2 * half, 2 * half + 1])
                    m = 15 + 2 * g + half
                    if m < 20:
                        mod_sum(m)

            def taking_wout(norm):
                if norm == "post 0":
                    wout(1, 0)
                    mod_take(0, 16, 40, 20)
                    gate_coef(0, 1, 16, G_MIXPOST)
                    scale_coef(0, 2, 32, G_FFNPRE)
                elif norm == "pre 0":
                    wout(1, 1)
                elif norm == "post 2":
                    wout(1, 2)

            ffn(0, taking_wout)
            mod_take(0, 40, 48, 48)
            gate_coef(0, 3, 40, G_FFNPOST)
            mod_take(1, 0, 48, 48)
            scale_coef(1, 0, 8, G_MIXPRE)
            gate_coef(1, 1, 16, G_MIXPOST)
            scale_coef(1, 2, 32, G_FFNPRE)
            gate_coef(1, 3, 40, G_FFNPOST)
            ffn_add(0, NB - 1, 0)
            post_norm(0, 0, 3)
            ffn_add(0, NB - 1, 1)
            norm_product(0)
            ffn_add(0, NB - 1, 2)
            dve.memset(pool_d[:, 0, :], 0.0).then_inc(pool_pads_d, 1)
            post_norm(1, 0, 3, ahead=True)
            post_norm(2, 0, 3, ahead=True)
            norm_product(1)
            norm_product(2)
            for g in range(NG):
                dve.wait_ge(x_stored[g], 16 * 3)

            def pool_split(i):
                k = POOL_D[i]
                dve.wait_ge(pool_hi_d, i + 1)
                dve.tensor_tensor(mv_lo[:, k, :], y[:, k, :], mv_hi[:, k, :].bitcast(F32), ALU.subtract
                                  ).then_inc(pool_ready_d, 1)

            for i, k in enumerate(POOL_D):
                dve.wait_ge(pool_src_d, i + 1)
                pool_tile(dve, pool_d, wide, y, const, k, link, pool_begun_d, i + 1, pooled_d)
                if i:
                    pool_split(i - 1)
            pool_split(len(POOL_D) - 1)

            def take_pooled(g):
                for m in range(KT):
                    n = O_POOL + KT * g + m
                    dve.wait_ge(out_ready, n + 1)
                    dve.tensor_scalar(y[:, m, g * GT:(g + 1) * GT], bank[out_bank_of(n)][:, 0:GT],
                                      vec[:, V_POOLB + m:V_POOLB + m + 1], vec[:, V_PSCALE + m:V_PSCALE + m + 1],
                                      ALU.add, ALU.mult).then_inc(out_taken, 1)

            def taking_pooled(norm):
                if norm == "post 0":
                    take_pooled(0)
                elif norm == "pre 0":
                    take_pooled(1)
                elif norm == "post 1":
                    take_pooled(2)

            ffn(1, taking_pooled)
            ffn_add(1, NB - 1, 0)
            ffn_add(1, NB - 1, 1, ms=range(4))
            post_norm(0, 1, 3)
            ffn_add(1, NB - 1, 1, ms=range(4, KT))
            ffn_add(1, NB - 1, 2, ms=range(4))
            post_norm(1, 1, 3)
            ffn_add(1, NB - 1, 2, ms=range(4, KT))
            post_norm(2, 1, 3)

        @block.gpsimd
        def _(pool):
            steps = [0]

            def link(ins):
                steps[0] += 1
                ins.then_inc(pool_step, 1)
                pool.wait_ge(pool_step, steps[0])

            def split_lo(w, i=None):
                item = next(x for x, n in WEIGHT.items() if n == w)
                q = Q[item]
                pool.wait_ge(w_hi_ready, w + 1 if i is None else i * 6 + (w + 1))
                pool.tensor_tensor(w_lo[:, slot(w), :], raw[:, q % 2, :], w_hi[:, slot(w), :].bitcast(F32),
                                   ALU.subtract).then_inc(w_ready, 1)

            his = [0]

            sums = [0]

            def norm_acc(g, first=False):
                n = sums[0]
                tiles = norm_squares_of(g, first)
                for m in range(1, KT):
                    pool.wait_ge(squares, KT * n + m + 1)
                    if m == 1 and n:
                        pool.wait_ge(sum_ready, n)
                    ins = pool.tensor_tensor(acc[:, :], tiles[:, 0] if m == 1 else acc[:, :], tiles[:, m], ALU.add)
                    if m == KT - 1:
                        ins.then_inc(acc_ready, 1)
                    else:
                        link(ins)
                sums[0] += 1

            def norm_lo(g):
                for part in range(4):
                    his[0] += 1
                    pool.wait_ge(mv_hi_done, his[0])
                    v = slice(2 * part, 2 * part + 2)
                    pool.tensor_tensor(group(mv_lo, g)[:, v], group(wide, g)[:, v],
                                       group(mv_hi, g)[:, v].bitcast(F32), ALU.subtract).then_inc(mv_ready, 1)

            for g in range(NG):
                norm_acc(g)
            split_lo(0)
            for g in range(NG):
                norm_lo(g)

            def u_split_lo(n, j):
                pool.wait_ge(u_hi_done, 2 * n + j + 1)
                pool.tensor_tensor(u_lo[:, j, :], u[:, j, :], u_hi[:, j, :].bitcast(F32), ALU.subtract
                                   ).then_inc(u_ready, 1)

            def store_h(k):
                pool.wait_ge(h_ready, k + 1)
                pool.dma_start(scratch_h[:, k, :], lru_i[:, 1, :]).then_inc(h_stored, 16)

            def split_next(item):
                for w in NEXT_GRANULES[item]:
                    split_lo(w)

            split_next(("rec", 0))
            u_split_lo(0, 0)
            u_split_lo(0, 1)
            split_next(("rec", 1))
            for n in range(NLB):
                for j in range(2):
                    store_h(2 * n + j)
                    if n < NLB - 1:
                        u_split_lo(n + 1, j)
                if n < NLB - 1:
                    split_next(("rec", n + 2) if n < 2 else ("branch", 0))
            pool.wait_ge(h_stored, 16 * KT)
            pool.wait_ge(scanned, 16)
            for n in range(3):
                pool.dma_start(h_sum[:, 2 * n:2 * n + 2, :], scratch_h[:, 2 * n:2 * n + 2, :]).then_inc(h_loaded[n], 16)
            split_next(("branch", 1))
            split_next(("branch", 2))
            pool.wait_ge(mixed_ready, 2)
            pool.dma_start(h_sum[:, 0:2, :], scratch_h[:, 6:8, :]).then_inc(h_loaded[3], 16)
            split_next(("branch", 3))
            for g in range(NG):
                for t0, t1 in MIXED_PARTS:
                    his[0] += 1
                    pool.wait_ge(mv_hi_done, his[0])
                    s0 = MIXED_AT[t0]
                    pool.tensor_tensor(group(mv_lo, g)[:, t0:t1], group(mixed, g)[:, s0:s0 + t1 - t0],
                                       group(mv_hi, g)[:, t0:t1].bitcast(F32), ALU.subtract
                                       ).then_inc(mv_ready, (t1 - t0) // 2)
            split_lo(WEIGHT["w_out", 2])
            split_lo(WEIGHT["w_out", 3])
            split_lo(WEIGHT["gate", 0, 0])

            def ffn_first(layer):
                w = WEIGHT["gate", layer, 0]
                norm_acc(0, first=layer == 0)
                norm_acc(0)
                norm_acc(1)
                split_lo(w + 1)
                norm_acc(2)
                norm_acc(1)
                norm_acc(2)
                split_lo(w + 2)
                split_lo(w + 3)
                split_lo(w + 4)

            def ffn_block(layer, b, i=None):
                w = WEIGHT["gate", layer, b]
                split_lo(w + 2, i)
                if w + 3 in WEIGHTS:
                    split_lo(w + 3, i)
                    split_lo(w + 4, i)

            def ffn_rest(layer):
                with pool.Fori(0, LOOPS) as i:
                    ffn_block(layer, 1, i)
                    ffn_block(layer, 2, i)
                ffn_block(layer, NB - 2)
                ffn_block(layer, NB - 1)

            ffn_first(0)
            ffn_rest(0)
            for g in (0, 0, 1, 2, 1, 2):
                norm_acc(g)
            for g in range(NG):
                pool.wait_ge(x_stored[g], 16 * 3)
            pool.wait_ge(states_stored, 16)

            def pool_split(i):
                k = POOL_G[i]
                pool.wait_ge(pool_hi_g, i + 1)
                pool.tensor_tensor(mv_lo[:, k, :], y[:, k, :], mv_hi[:, k, :].bitcast(F32), ALU.subtract
                                   ).then_inc(pool_ready_g, 1)

            pool.memset(pool_g[:, 0, :], 0.0).then_inc(pool_pads_g, 1)
            for i, k in enumerate(POOL_G):
                pool.wait_ge(pool_src_g, i + 1)
                pool_tile(pool, pool_g, wide, y, const, k, link, pool_begun_g, i + 1, pooled_g)
                if i:
                    pool_split(i - 1)
            pool_split(len(POOL_G) - 1)
            ffn_first(1)
            ffn_rest(1)
            for g in range(NG):
                norm_acc(g)


NEXT_GRANULES = {("rec", 0): [1], ("rec", 1): [2, 3], ("rec", 2): [4, 5], ("rec", 3): [6, 7],
                 ("branch", 0): [8, 9], ("branch", 1): [10], ("branch", 2): [11, 12], ("branch", 3): [13]}
WEIGHTS = set(WEIGHT.values())
MIXED_AT = [6, 7, 0, 1, 2, 3, 4, 5]
MIXED_PARTS = ((0, 2), (2, 6), (6, 8))
HI_BEFORE_FFN = 4 * NG + len(MIXED_PARTS) * NG
SPLIT_LAG = 4
LAST_NORMS = NG + 2 * NG
POOL_D, POOL_G = (7, 6, 5, 3, 1), (4, 2, 0)


def pool_tile(eng, buf, h, out, const, k, link, begun, nth, done):
    w = WINDOWS[k // 2]
    c0, l0 = PAD, 2 * PAD + CTX
    src, dst, span, size = 0, 1, 1, PL
    if nth > 1:
        eng.wait_ge(done, nth - 1)
    while span < w:
        size -= span
        ins = eng.tensor_tensor(buf[:, dst, 0:size], buf[:, src, 0:size], buf[:, src, span:span + size], ALU.add)
        if src == 0:
            ins.then_inc(begun, 1)
            eng.wait_ge(begun, nth)
        else:
            link(ins)
        src, dst, span = dst, 3 - dst if src else 2, span * 2
    e0 = C_EDGE + sum(a + b for v, a, b in EDGES if v < w)
    left, right = w // 2, w // 2 - 1
    for start, size in ((c0, CTX), (l0, LAT)):
        first = start - w // 2
        ins = eng.tensor_tensor(buf[:, src, first:first + left], buf[:, src, first:first + left],
                                const[:, e0:e0 + left], ALU.mult)
        if right:
            ins = eng.tensor_tensor(buf[:, src, first + size - right:first + size],
                                    buf[:, src, first + size - right:first + size],
                                    const[:, e0 + left:e0 + left + right], ALU.mult)
    link(ins)
    for start, t0, size in ((c0, 0, CTX), (l0, CTX, LAT)):
        first = start - w // 2
        ins = eng.tensor_tensor(out[:, k, t0:t0 + size], buf[:, src, first:first + size], h[:, k, t0:t0 + size],
                                ALU.subtract)
    ins.then_inc(done, 1)


def block_mods(layer, b):
    if layer == 1 or b == NB - 1:
        return 0, 0
    if b == 0:
        return 20, 2
    return 22 + 3 * (b - 1), 2 if b == NB - 2 else 3


def STAGE_ROWS(a):
    rows = []
    for base, name in ((V_C, "c"), (V_CCTX, "c_ctx"), (V_CONVW, "l0_conv_w"), (V_CONVB, "l0_conv_b"),
                       (V_BA, "l0_gate_a_b"), (V_BX, "l0_gate_x_b"), (V_LAM, "l0_lambda"),
                       (V_STATE, "state_l0_rglru"), (V_POOLB, "l1_pool_b")):
        rows.append((0, base, name))
    for layer in range(2):
        for which, name in ((G_MIXPRE, "mix_pre_g"), (G_MIXPOST, "mix_post_g"), (G_FFNPRE, "ffn_pre_g"),
                            (G_FFNPOST, "ffn_post_g")):
            rows.append((1, V_GAIN - P + 32 * layer + which, f"l{layer}_{name}"))
    rows.append((1, V_PSCALE - P, "l1_pool_scale"))
    for layer in range(2):
        rows.append((2, 48 * layer, f"l{layer}_mod_b"))

    def flat(v):
        while len(v.shape) > 2:
            v = v.rearrange("a b c -> (a b) c")
        if len(v.shape) == 2:
            v = v.rearrange("a b -> (a b)")
        return v.rearrange("(r p) -> r p", p=P)

    return [(s, row, flat(a[name])) for s, row, name in rows]


STAGE_DMAS = (9, 9, 2)


def constants():
    quarter = D // 4
    omega = (1.0 / (10000.0 ** (np.arange(quarter, dtype=np.float32) / np.float32(quarter)))).astype(np.float32)

    def emb(n):
        ang = np.arange(n, dtype=np.float32)[:, None] * omega[None, :]
        e = np.concatenate([np.sin(ang), np.cos(ang)], axis=-1).astype(np.float32)
        return e.T.reshape(4, P, n).transpose(1, 0, 2).reshape(P, 4 * n)

    edge = []
    for w, left, right in EDGES:
        edge += [w / (w // 2 + t) for t in range(left)]
        edge += [w / (w - t) for t in range(1, right + 1)]
    out = np.concatenate([np.eye(P), np.tile(np.array(edge)[None], (P, 1)), emb(GRID_H), emb(GRID_W)], axis=1)
    return np.ascontiguousarray(out.astype(np.float32))


_INS = ['x_prompt', 'x_sample', 'state_l0_rglru', 'c', 'c_ctx', 'l0_mod_w', 'l0_mod_b', 'l0_mix_pre_g',
        'l0_mix_post_g', 'l0_w_in', 'l0_conv_w', 'l0_conv_b', 'l0_gate_a_w', 'l0_gate_a_b', 'l0_gate_x_w',
        'l0_gate_x_b', 'l0_lambda', 'l0_w_out', 'l0_ffn_pre_g', 'l0_ffn_post_g', 'l0_ffn_w_in', 'l0_ffn_w_out',
        'l1_mod_w', 'l1_mod_b', 'l1_mix_pre_g', 'l1_mix_post_g', 'l1_pool_w', 'l1_pool_b', 'l1_pool_scale',
        'l1_ffn_pre_g', 'l1_ffn_post_g', 'l1_ffn_w_in', 'l1_ffn_w_out']
_OUTS = [(1, CTX, D), (1, LAT, D), (1, 2, D)]


def kernel(**inputs):
    import concourse.bacc as _bacc
    from concourse.bass_utils import run_bass_kernel_spmd as _run

    nc = _bacc.Bacc("TRN2", target_bir_lowering=False, num_devices=1)
    arrays, aps = {}, {}
    for name in _INS:
        arrays[f"in_{name}"] = np.ascontiguousarray(inputs[name])
        aps[name] = nc.dram_tensor(f"in_{name}", arrays[f"in_{name}"].shape, F32, kind="ExternalInput").ap()
    arrays["in_constants"] = constants()
    consts = nc.dram_tensor("in_constants", arrays["in_constants"].shape, F32, kind="ExternalInput").ap()
    scratch_x = nc.dram_tensor("residual", [P, KT, T], F32).ap()
    scratch_h = nc.dram_tensor("recurrence", [P, KT, T], F32).ap()
    outs = [nc.dram_tensor(f"out_{i}", shape, F32, kind="ExternalOutput").ap() for i, shape in enumerate(_OUTS)]
    program(nc, aps, scratch_x, scratch_h, consts, outs)
    r = _run(nc, [arrays], core_ids=[0])
    return tuple(r.results[0][f"out_{i}"] for i in range(len(_OUTS)))
```
